# Optimizing a Trainium2 kernel written in Bass

```python
import math
import jax, jax.numpy as jnp
from jax import lax
import numpy as np

D_MODEL = 1024
BATCH = 1
SEQ = 256
DEPTH = 2

HEAD_DIM = 64
EPS = 1e-6

SWA_Q_HEADS = 8
SWA_KV_HEADS = 2
SWA_GROUP = SWA_Q_HEADS // SWA_KV_HEADS
WINDOW = 128
BLOCK = 128
SWA_WIDTH = SWA_Q_HEADS * HEAD_DIM
KV_WIDTH = SWA_KV_HEADS * HEAD_DIM

SSM_WIDTH = D_MODEL // 2
SSM_GROUP_CH = 16
SSM_GROUPS = SSM_WIDTH // SSM_GROUP_CH
SSM_STATE = 64
DT_MIN = 0.001
DT_MAX = 0.1

EVEN_IN = SWA_WIDTH + 2 * KV_WIDTH + SSM_WIDTH
EVEN_MIX = SWA_WIDTH + SSM_WIDTH

SB_HEADS = D_MODEL // HEAD_DIM
SB_WIDTH = SB_HEADS * HEAD_DIM
SB_BLOCK = 128

D_FF = -(-8 * D_MODEL // (3 * 256)) * 256

N_EVEN = (DEPTH + 1) // 2
N_ODD = DEPTH // 2


def rmsnorm(x, g):
    xf = x.astype(jnp.float32)
    y = xf * lax.rsqrt(jnp.mean(xf * xf, axis=-1, keepdims=True) + EPS)
    return (y * g.astype(jnp.float32)).astype(x.dtype)

def swa_sink_attention(q, k, v, sinks):
    b, l, _, d = q.shape
    nb = l // BLOCK
    qb = q.reshape(b, nb, BLOCK, SWA_KV_HEADS, SWA_GROUP, d)

    def with_prev(t):
        t = t.reshape(b, nb, BLOCK, SWA_KV_HEADS, d)
        prev = jnp.concatenate([jnp.zeros_like(t[:, :1]), t[:, :-1]], axis=1)
        return jnp.concatenate([prev, t], axis=2)

    kb, vb = with_prev(k), with_prev(v)
    scores = jnp.einsum('bnqhgd,bnkhd->bnhgqk', qb, kb).astype(jnp.float32) * (d ** -0.5)
    qpos = jnp.arange(BLOCK) + BLOCK
    kpos = jnp.arange(2 * BLOCK)
    diff = qpos[:, None] - kpos[None, :]
    band = (diff >= 0) & (diff < WINDOW)
    has_prev = (jnp.arange(nb)[:, None] > 0) | (kpos[None, :] >= BLOCK)
    mask = (band[None, :, :] & has_prev[:, None, :])[None, :, None, None]
    scores = jnp.where(mask, scores, -jnp.inf)
    sink = sinks.astype(jnp.float32).reshape(SWA_KV_HEADS, SWA_GROUP)[None, None, :, :, None, None]
    m = jnp.maximum(scores.max(axis=-1, keepdims=True), sink)
    p = jnp.exp(scores - m)
    probs = p / (p.sum(axis=-1, keepdims=True) + jnp.exp(sink - m))
    o = jnp.einsum('bnhgqk,bnkhd->bnqhgd', probs.astype(v.dtype), vb)
    return o.reshape(b, l, SWA_WIDTH)

def _complex_affine_combine(left, right):
    ar1, ai1, br1, bi1 = left
    ar2, ai2, br2, bi2 = right
    return (ar2 * ar1 - ai2 * ai1,
            ar2 * ai1 + ai2 * ar1,
            ar2 * br1 - ai2 * bi1 + br2,
            ar2 * bi1 + ai2 * br1 + bi2)

def s5_mixer(u, a_re, a_im, b_re, b_im, c_re, c_im, d_skip, log_dt, w_glu, b_glu):
    f32 = jnp.float32
    b, l, _ = u.shape
    uf = u.astype(f32)
    ug = uf.reshape(b, l, SSM_GROUPS, SSM_GROUP_CH)
    a_re, a_im = a_re.astype(f32), a_im.astype(f32)
    b_re, b_im = b_re.astype(f32), b_im.astype(f32)
    c_re, c_im = c_re.astype(f32), c_im.astype(f32)
    dt = jnp.exp(log_dt.astype(f32))[:, None]
    mag = jnp.exp(a_re * dt)
    lam_re = mag * jnp.cos(a_im * dt)
    lam_im = mag * jnp.sin(a_im * dt)
    den = a_re * a_re + a_im * a_im
    w_re = ((lam_re - 1.0) * a_re + lam_im * a_im) / den
    w_im = (lam_im * a_re - (lam_re - 1.0) * a_im) / den
    bb_re = w_re[..., None] * b_re - w_im[..., None] * b_im
    bb_im = w_re[..., None] * b_im + w_im[..., None] * b_re
    bu_re = jnp.einsum('blgp,gnp->blgn', ug, bb_re)
    bu_im = jnp.einsum('blgp,gnp->blgn', ug, bb_im)
    shape = (1, l, SSM_GROUPS, SSM_STATE)
    lr = jnp.broadcast_to(lam_re, shape)
    li = jnp.broadcast_to(lam_im, shape)
    _, _, h_re, h_im = lax.associative_scan(_complex_affine_combine, (lr, li, bu_re, bu_im), axis=1)
    y = jnp.einsum('blgn,gpn->blgp', h_re, c_re) - jnp.einsum('blgn,gpn->blgp', h_im, c_im)
    y = y.reshape(b, l, SSM_WIDTH) + d_skip.astype(f32) * uf
    y = jax.nn.gelu(y)
    out = y * jax.nn.sigmoid(y @ w_glu.astype(f32) + b_glu.astype(f32))
    return out.astype(u.dtype)

def stick_breaking_attention(q, k, v):
    b, l, h, d = q.shape
    nb = l // SB_BLOCK
    qb = q.reshape(b, nb, SB_BLOCK, h, d).transpose(1, 0, 3, 2, 4)
    kt = k.transpose(0, 2, 1, 3)
    vt = v.transpose(0, 2, 1, 3)
    kpos = jnp.arange(l)
    scale = d ** -0.5

    def block(args):
        q_blk, start = args
        z = jnp.einsum('bhqd,bhkd->bhqk', q_blk, kt).astype(jnp.float32) * scale
        qpos = start + jnp.arange(SB_BLOCK)
        mask = kpos[None, :] < qpos[:, None]
        log_keep = jnp.where(mask, jax.nn.log_sigmoid(-z), 0.0)
        log_survive = lax.cumsum(log_keep, axis=3, reverse=True) - log_keep
        weights = jnp.where(mask, jnp.exp(jax.nn.log_sigmoid(z) + log_survive), 0.0)
        return jnp.einsum('bhqk,bhkd->bhqd', weights.astype(vt.dtype), vt)

    starts = jnp.arange(nb, dtype=jnp.int32) * SB_BLOCK
    o = lax.map(block, (qb, starts))
    return o.transpose(1, 0, 3, 2, 4).reshape(b, l, h * d)

def _normal(key, shape, scale):
    return jax.random.normal(key, shape, jnp.float32) * scale

def _gain(key, shape):
    return 1.0 + 0.02 * jax.random.normal(key, shape, jnp.float32)

def first_inputs(seed: int = 0) -> dict:
    key = jax.random.key(seed)
    ks = jax.random.split(key, 26)
    E, O, L = N_EVEN, N_ODD, DEPTH
    G, N, P = SSM_GROUPS, SSM_STATE, SSM_GROUP_CH
    n = jnp.arange(N, dtype=jnp.float32)
    log_dt = jax.random.uniform(ks[13], (E, G), jnp.float32,
                                math.log(DT_MIN), math.log(DT_MAX))
    return {
        "x": _normal(ks[0], (BATCH, SEQ, D_MODEL), 1.0),
        "even_norm": _gain(ks[1], (E, D_MODEL)),
        "even_w_in": _normal(ks[2], (E, D_MODEL, EVEN_IN), D_MODEL ** -0.5),
        "q_norm": _gain(ks[3], (E, HEAD_DIM)),
        "k_norm": _gain(ks[4], (E, HEAD_DIM)),
        "sinks": _normal(ks[5], (E, SWA_Q_HEADS), 0.5),
        "ssm_a_re": -0.5 * jnp.exp(0.02 * jax.random.normal(ks[6], (E, G, N), jnp.float32)),
        "ssm_a_im": jnp.pi * n + 0.01 * jax.random.normal(ks[7], (E, G, N), jnp.float32),
        "ssm_b_re": _normal(ks[8], (E, G, N, P), (2 * P) ** -0.5),
        "ssm_b_im": _normal(ks[9], (E, G, N, P), (2 * P) ** -0.5),
        "ssm_c_re": _normal(ks[10], (E, G, P, N), N ** -0.5),
        "ssm_c_im": _normal(ks[11], (E, G, P, N), N ** -0.5),
        "ssm_d": _normal(ks[12], (E, SSM_WIDTH), 0.5),
        "ssm_log_dt": log_dt,
        "ssm_w_glu": _normal(ks[14], (E, SSM_WIDTH, SSM_WIDTH), SSM_WIDTH ** -0.5),
        "ssm_b_glu": _normal(ks[15], (E, SSM_WIDTH), 0.02),
        "even_w_out": _normal(ks[16], (E, EVEN_MIX, D_MODEL), EVEN_MIX ** -0.5),
        "odd_norm": _gain(ks[17], (O, D_MODEL)),
        "odd_w_in": _normal(ks[18], (O, D_MODEL, 3 * SB_WIDTH), D_MODEL ** -0.5),
        "odd_w_out": _normal(ks[19], (O, SB_WIDTH, D_MODEL), SB_WIDTH ** -0.5),
        "ffn_norm": _gain(ks[20], (L, D_MODEL)),
        "ffn_w_gate": _normal(ks[21], (L, D_MODEL, D_FF), D_MODEL ** -0.5),
        "ffn_w_up": _normal(ks[22], (L, D_MODEL, D_FF), D_MODEL ** -0.5),
        "ffn_w_down": _normal(ks[23], (L, D_FF, D_MODEL), D_FF ** -0.5),
    }

def first_block(x, even_norm, even_w_in, q_norm, k_norm, sinks,
              ssm_a_re, ssm_a_im, ssm_b_re, ssm_b_im, ssm_c_re, ssm_c_im,
              ssm_d, ssm_log_dt, ssm_w_glu, ssm_b_glu, even_w_out,
              odd_norm, odd_w_in, odd_w_out,
              ffn_norm, ffn_w_gate, ffn_w_up, ffn_w_down):
    b, l, _ = x.shape
    for layer in range(DEPTH):
        i = layer // 2
        if layer % 2 == 0:
            hn = rmsnorm(x, even_norm[i])
            proj = hn @ even_w_in[i]
            q, k, v, u = jnp.split(
                proj, [SWA_WIDTH, SWA_WIDTH + KV_WIDTH, SWA_WIDTH + 2 * KV_WIDTH], axis=-1)
            q = rmsnorm(q.reshape(b, l, SWA_Q_HEADS, HEAD_DIM), q_norm[i])
            k = rmsnorm(k.reshape(b, l, SWA_KV_HEADS, HEAD_DIM), k_norm[i])
            v = v.reshape(b, l, SWA_KV_HEADS, HEAD_DIM)
            o_attn = swa_sink_attention(q, k, v, sinks[i])
            o_ssm = s5_mixer(u, ssm_a_re[i], ssm_a_im[i], ssm_b_re[i], ssm_b_im[i],
                             ssm_c_re[i], ssm_c_im[i], ssm_d[i], ssm_log_dt[i],
                             ssm_w_glu[i], ssm_b_glu[i])
            mixed = jnp.concatenate([o_attn, o_ssm], axis=-1) @ even_w_out[i]
        else:
            hn = rmsnorm(x, odd_norm[i])
            q, k, v = jnp.split(hn @ odd_w_in[i], 3, axis=-1)
            q = q.reshape(b, l, SB_HEADS, HEAD_DIM)
            k = k.reshape(b, l, SB_HEADS, HEAD_DIM)
            v = v.reshape(b, l, SB_HEADS, HEAD_DIM)
            mixed = stick_breaking_attention(q, k, v) @ odd_w_out[i]
        x = x + mixed
        hn = rmsnorm(x, ffn_norm[layer])
        x = x + (jax.nn.silu(hn @ ffn_w_gate[layer]) * (hn @ ffn_w_up[layer])) @ ffn_w_down[layer]
    return x


DEPTH_2 = 1

M_HEADS = 4
M_HEAD_DIM = 128
M_WIDTH = M_HEADS * M_HEAD_DIM
CONV_W = 4
CHUNK = 128
A_HEADS = 8
A_HEAD_DIM = 64
A_WIDTH = A_HEADS * A_HEAD_DIM
DIL_PATTERNS = ((128, 1), (512, 4), (2048, 16))
N_BUCKETS = 32
MAX_DISTANCE = 2048
MIX_WIDTH = M_WIDTH + A_WIDTH
IN_SIZES = (M_WIDTH, M_WIDTH, M_WIDTH, M_HEADS, M_HEADS, A_WIDTH, A_WIDTH, A_WIDTH)
IN_COLS = 3 * M_WIDTH + 2 * M_HEADS + 3 * A_WIDTH
PEER_HEADS = 8
N_KEYS = 128
N_EXPERTS = N_KEYS * N_KEYS
PEER_QDIM = 256
PEER_TOPK = 16
PEER_BLOCK = 128


def rms_norm(x, g):
    xf = x.astype(jnp.float32)
    y = xf * lax.rsqrt(jnp.mean(xf * xf, axis=-1, keepdims=True) + EPS)
    return (y * g).astype(x.dtype)

def t5_bucket(dist):
    max_exact = N_BUCKETS // 2
    nf = jnp.maximum(dist, 1).astype(jnp.float32)
    large = max_exact + (jnp.log(nf / max_exact) / np.log(MAX_DISTANCE / max_exact)
                         * (N_BUCKETS - max_exact)).astype(jnp.int32)
    large = jnp.minimum(large, N_BUCKETS - 1)
    return jnp.where(dist < max_exact, dist, large)

def causal_short_conv(u, w, b):
    y = lax.conv_general_dilated(u, w[:, None, :], window_strides=(1,),
                                 padding=[(CONV_W - 1, 0)],
                                 dimension_numbers=('NWC', 'WIO', 'NWC'),
                                 feature_group_count=u.shape[-1])
    return y + b

def mlstm_chunkwise(q, k, v, ipre, fpre):
    B, H, S, Dh = q.shape
    nc = S // CHUNK
    q = q.reshape(B, H, nc, CHUNK, Dh)
    k = k.reshape(B, H, nc, CHUNK, Dh)
    v = v.reshape(B, H, nc, CHUNK, Dh)
    logi = ipre.reshape(B, H, nc, CHUNK)
    b = jnp.cumsum(jax.nn.log_sigmoid(fpre).reshape(B, H, nc, CHUNK), axis=-1)
    b_last = b[..., -1]
    g = b_last[..., None] - b + logi
    m_loc = jnp.max(g, axis=-1)
    wts = jnp.exp(g - m_loc[..., None])
    c_chunk = jnp.einsum('bhnl,bhnlk,bhnlv->bhnkv', wts, k, v)
    n_chunk = jnp.einsum('bhnl,bhnlk->bhnk', wts, k)

    def step(carry, inp):
        C, n, m = carry
        bl, ml, cc, nn = inp
        m_new = jnp.maximum(bl + m, ml)
        a = jnp.exp(bl + m - m_new)
        bb = jnp.exp(ml - m_new)
        C_new = a[..., None, None] * C + bb[..., None, None] * cc
        n_new = a[..., None] * n + bb[..., None] * nn
        return (C_new, n_new, m_new), (C, n, m)

    init = (jnp.zeros((B, H, Dh, Dh), jnp.float32), jnp.zeros((B, H, Dh), jnp.float32),
            jnp.zeros((B, H), jnp.float32))
    xs = (jnp.moveaxis(b_last, 2, 0), jnp.moveaxis(m_loc, 2, 0),
          jnp.moveaxis(c_chunk, 2, 0), jnp.moveaxis(n_chunk, 2, 0))
    _, (C_prev, n_prev, m_prev) = lax.scan(step, init, xs)
    C_prev = jnp.moveaxis(C_prev, 0, 2)
    n_prev = jnp.moveaxis(n_prev, 0, 2)
    m_prev = jnp.moveaxis(m_prev, 0, 2)

    causal = jnp.tril(jnp.ones((CHUNK, CHUNK), bool))
    log_d = jnp.where(causal, b[..., :, None] - b[..., None, :] + logi[..., None, :], -jnp.inf)
    inter = b + m_prev[..., None]
    m_t = jnp.maximum(inter, jnp.max(log_d, axis=-1))
    d_mat = jnp.exp(log_d - m_t[..., None])
    inter_w = jnp.exp(inter - m_t)
    s = jnp.einsum('bhnqd,bhnkd->bhnqk', q, k) * d_mat
    num = (jnp.einsum('bhnqk,bhnkd->bhnqd', s, v)
           + inter_w[..., None] * jnp.einsum('bhnqd,bhnde->bhnqe', q, C_prev))
    den = jnp.sum(s, axis=-1) + inter_w * jnp.einsum('bhnqd,bhnd->bhnq', q, n_prev)
    h = num / jnp.maximum(jnp.abs(den), jnp.exp(-m_t))[..., None]
    return h.reshape(B, H, S, Dh)

def dilated_branch(q, k, v, rel_bias, window, dilation):
    B, S, H, Dh = q.shape
    blk = window // dilation
    span = dilation * blk
    s_pad = -(-S // span) * span
    nb = s_pad // span

    def to_blocks(t):
        t = jnp.pad(t, ((0, 0), (0, s_pad - S), (0, 0), (0, 0)))
        return t.reshape(B, nb, blk, dilation, H, Dh).transpose(0, 3, 4, 1, 2, 5)

    qb, kb, vb = to_blocks(q), to_blocks(k), to_blocks(v)
    shift = lambda t: jnp.pad(t, ((0, 0), (0, 0), (0, 0), (1, 0), (0, 0), (0, 0)))[:, :, :, :-1]
    kk = jnp.concatenate([shift(kb), kb], axis=4)
    vv = jnp.concatenate([shift(vb), vb], axis=4)
    i = jnp.arange(blk)[:, None]
    j = jnp.arange(2 * blk)[None, :]
    steps = i + blk - j
    band = (steps >= 0) & (steps <= blk)
    valid = band[None] & ((jnp.arange(nb)[:, None, None] > 0) | (j >= blk)[None])
    bias = rel_bias[t5_bucket(jnp.maximum(steps, 0) * dilation)].transpose(2, 0, 1)
    s = (jnp.einsum('brhnqc,brhnkc->brhnqk', qb, kk).astype(jnp.float32) * (A_HEAD_DIM ** -0.5)
         + bias[None, None, :, None])
    s = jnp.where(valid[None, None, None], s, -jnp.inf)
    m = jnp.max(s, axis=-1, keepdims=True)
    p = jnp.exp(s - m)
    den = jnp.sum(p, axis=-1)
    o = jnp.einsum('brhnqk,brhnkc->brhnqc', p, vv) / den[..., None]
    lse = m[..., 0] + jnp.log(den)
    o = o.transpose(0, 3, 4, 1, 2, 5).reshape(B, s_pad, H, Dh)[:, :S]
    lse = lse.transpose(0, 3, 4, 1, 2).reshape(B, s_pad, H)[:, :S]
    return o, lse

def peer(h, w_query, sub_keys1, sub_keys2, expert_u, expert_v):
    B, S, D = h.shape
    T = B * S
    hf = h.reshape(T, D)
    q = (hf @ w_query).reshape(T, PEER_HEADS, 2, PEER_QDIM // 2)
    s1 = jnp.einsum('thc,hkc->thk', q[:, :, 0], sub_keys1).astype(jnp.float32)
    s2 = jnp.einsum('thc,hkc->thk', q[:, :, 1], sub_keys2).astype(jnp.float32)
    v1, i1 = lax.top_k(s1, PEER_TOPK)
    v2, i2 = lax.top_k(s2, PEER_TOPK)
    cand = (v1[..., :, None] + v2[..., None, :]).reshape(T, PEER_HEADS, PEER_TOPK * PEER_TOPK)
    vc, ic = lax.top_k(cand, PEER_TOPK)
    e1 = jnp.take_along_axis(i1, ic // PEER_TOPK, axis=-1)
    e2 = jnp.take_along_axis(i2, ic % PEER_TOPK, axis=-1)
    idx = (e1 * N_KEYS + e2).reshape(T, PEER_HEADS * PEER_TOPK)
    gate = jax.nn.softmax(vc, axis=-1).reshape(T, PEER_HEADS * PEER_TOPK)

    def block(args):
        xb, ib, gb = args
        u = expert_u[ib]
        pre = jnp.einsum('td,tkd->tk', xb, u).astype(jnp.float32)
        a = jax.nn.gelu(pre, approximate=False) * gb
        return jnp.einsum('tk,tkd->td', a, expert_v[ib])

    nblk = T // PEER_BLOCK
    out = lax.map(block, (hf.reshape(nblk, PEER_BLOCK, D),
                          idx.reshape(nblk, PEER_BLOCK, -1),
                          gate.reshape(nblk, PEER_BLOCK, -1)))
    return out.reshape(B, S, D).astype(h.dtype)

def second_inputs(seed: int = 0) -> dict:
    key = jax.random.key(seed)
    ks = jax.random.split(key, 24)
    n = lambda i, shape: jax.random.normal(ks[i], shape, jnp.float32)
    return {
        'x': n(0, (BATCH, SEQ, D_MODEL)),
        'norm1_g': 1.0 + 0.02 * n(1, (DEPTH_2, D_MODEL)),
        'w_in': n(2, (DEPTH_2, D_MODEL, IN_COLS)) * D_MODEL ** -0.5,
        'conv_w': n(3, (DEPTH_2, CONV_W, M_WIDTH)) * CONV_W ** -0.5,
        'conv_b': 0.02 * n(4, (DEPTH_2, M_WIDTH)),
        'wq_m': n(5, (DEPTH_2, M_HEADS, M_HEAD_DIM, M_HEAD_DIM)) * M_HEAD_DIM ** -0.5,
        'wk_m': n(6, (DEPTH_2, M_HEADS, M_HEAD_DIM, M_HEAD_DIM)) * M_HEAD_DIM ** -0.5,
        'ig_b': 0.1 * n(7, (DEPTH_2, M_HEADS)),
        'fg_b': jnp.linspace(3.0, 6.0, M_HEADS, dtype=jnp.float32)[None] + 0.1 * n(8, (DEPTH_2, M_HEADS)),
        'mh_norm_g': 1.0 + 0.02 * n(9, (DEPTH_2, M_HEADS, M_HEAD_DIM)),
        'skip_m': 1.0 + 0.02 * n(10, (DEPTH_2, M_HEADS, M_HEAD_DIM)),
        'qn_g': 1.0 + 0.02 * n(11, (DEPTH_2, A_HEADS, A_HEAD_DIM)),
        'kn_g': 1.0 + 0.02 * n(12, (DEPTH_2, A_HEADS, A_HEAD_DIM)),
        'rel_bias': 0.5 * n(13, (N_BUCKETS, A_HEADS)),
        'w_out': n(14, (DEPTH_2, MIX_WIDTH, D_MODEL)) * MIX_WIDTH ** -0.5,
        'norm2_g': 1.0 + 0.02 * n(15, (DEPTH_2, D_MODEL)),
        'w_query': n(16, (DEPTH_2, D_MODEL, PEER_HEADS * PEER_QDIM)) * D_MODEL ** -0.5,
        'sub_keys1': n(17, (DEPTH_2, PEER_HEADS, N_KEYS, PEER_QDIM // 2)) * (PEER_QDIM // 2) ** -0.5,
        'sub_keys2': n(18, (DEPTH_2, PEER_HEADS, N_KEYS, PEER_QDIM // 2)) * (PEER_QDIM // 2) ** -0.5,
        'expert_u': n(19, (DEPTH_2, N_EXPERTS, D_MODEL)) * D_MODEL ** -0.5,
        'expert_v': n(20, (DEPTH_2, N_EXPERTS, D_MODEL)) * D_MODEL ** -0.5,
    }

def second_block(x, norm1_g, w_in, conv_w, conv_b, wq_m, wk_m, ig_b, fg_b, mh_norm_g, skip_m,
              qn_g, kn_g, rel_bias, w_out, norm2_g, w_query, sub_keys1, sub_keys2,
              expert_u, expert_v):
    B, S, D = x.shape
    offsets = []
    acc = 0
    for sz in IN_SIZES[:-1]:
        acc += sz
        offsets.append(acc)
    for l in range(DEPTH_2):
        h = rms_norm(x, norm1_g[l])
        proj = h @ w_in[l]
        u, vm, z, ipre, fpre, qa, ka, va = jnp.split(proj, offsets, axis=-1)
        c = jax.nn.silu(causal_short_conv(u, conv_w[l], conv_b[l]))
        ch = c.reshape(B, S, M_HEADS, M_HEAD_DIM)
        qm = jnp.einsum('bshc,hcd->bhsd', ch, wq_m[l]).astype(jnp.float32)
        km = jnp.einsum('bshc,hcd->bhsd', ch, wk_m[l]).astype(jnp.float32) * (M_HEAD_DIM ** -0.5)
        vmh = vm.reshape(B, S, M_HEADS, M_HEAD_DIM).transpose(0, 2, 1, 3).astype(jnp.float32)
        ig = (ipre + ig_b[l]).astype(jnp.float32).transpose(0, 2, 1)
        fg = (fpre + fg_b[l]).astype(jnp.float32).transpose(0, 2, 1)
        hm = mlstm_chunkwise(qm, km, vmh, ig, fg).transpose(0, 2, 1, 3).astype(x.dtype)
        hm = rms_norm(hm, mh_norm_g[l]) + skip_m[l] * ch
        ym = jax.nn.sigmoid(z) * hm.reshape(B, S, M_WIDTH)
        qh = rms_norm(qa.reshape(B, S, A_HEADS, A_HEAD_DIM), qn_g[l])
        kh = rms_norm(ka.reshape(B, S, A_HEADS, A_HEAD_DIM), kn_g[l])
        vh = va.reshape(B, S, A_HEADS, A_HEAD_DIM)
        outs, lses = [], []
        for window, dilation in DIL_PATTERNS:
            o, lse = dilated_branch(qh, kh, vh, rel_bias, window, dilation)
            outs.append(o)
            lses.append(lse)
        wts = jax.nn.softmax(jnp.stack(lses, axis=0), axis=0)
        ya = jnp.sum(wts[..., None] * jnp.stack(outs, axis=0), axis=0)
        ya = ya.reshape(B, S, A_WIDTH).astype(x.dtype)
        x = x + jnp.concatenate([ym, ya], axis=-1) @ w_out[l]
        h2 = rms_norm(x, norm2_g[l])
        x = x + peer(h2, w_query[l], sub_keys1[l], sub_keys2[l], expert_u[l], expert_v[l])
    return x


def setup_inputs(seed=0):
    out = dict(first_inputs(seed))
    for name, value in second_inputs(seed + 1).items():
        if name != "x":
            out[name + "_2"] = value
    return out


def reference(
    x, even_norm, even_w_in, q_norm, k_norm, sinks, ssm_a_re, ssm_a_im, ssm_b_re, ssm_b_im,
    ssm_c_re, ssm_c_im, ssm_d, ssm_log_dt, ssm_w_glu, ssm_b_glu, even_w_out, odd_norm, odd_w_in,
    odd_w_out, ffn_norm, ffn_w_gate, ffn_w_up, ffn_w_down, norm1_g_2, w_in_2, conv_w_2,
    conv_b_2, wq_m_2, wk_m_2, ig_b_2, fg_b_2, mh_norm_g_2, skip_m_2, qn_g_2, kn_g_2, rel_bias_2,
    w_out_2, norm2_g_2, w_query_2, sub_keys1_2, sub_keys2_2, expert_u_2, expert_v_2,
):
    x = first_block(
        x, even_norm, even_w_in, q_norm, k_norm, sinks, ssm_a_re, ssm_a_im, ssm_b_re, ssm_b_im,
        ssm_c_re, ssm_c_im, ssm_d, ssm_log_dt, ssm_w_glu, ssm_b_glu, even_w_out, odd_norm,
        odd_w_in, odd_w_out, ffn_norm, ffn_w_gate, ffn_w_up, ffn_w_down,
    )
    return second_block(
        x, norm1_g_2, w_in_2, conv_w_2, conv_b_2, wq_m_2, wk_m_2, ig_b_2, fg_b_2, mh_norm_g_2,
        skip_m_2, qn_g_2, kn_g_2, rel_bias_2, w_out_2, norm2_g_2, w_query_2, sub_keys1_2,
        sub_keys2_2, expert_u_2, expert_v_2,
    )


_drawn_inputs = setup_inputs


def setup_inputs(seed=0):
    import zlib

    import numpy as np

    out = dict(_drawn_inputs(seed))
    spreads = {}
    factors = {'even_norm': 7.186,
     'q_norm': 8.0,
     'k_norm': 8.0,
     'sinks': 4.777,
     'ssm_a_re': 8.0,
     'ssm_b_re': 3.072,
     'ssm_b_im': 3.118,
     'ssm_c_re': 3.052,
     'ssm_c_im': 3.043,
     'ssm_b_glu': 8.0,
     'odd_norm': 4.078,
     'norm1_g_2': 4.67,
     'conv_b_2': 6.433,
     'ig_b_2': 200.0,
     'mh_norm_g_2': 8.0,
     'skip_m_2': 8.0,
     'qn_g_2': 8.0,
     'kn_g_2': 8.0,
     'norm2_g_2': 8.0,
     'w_query_2': 5.814,
     'sub_keys1_2': 5.986,
     'sub_keys2_2': 5.9,
     'expert_u_2': 6.449,
     'expert_v_2': 5.792}
    for name, (base, spread) in spreads.items():
        noise = np.random.default_rng([zlib.crc32(name.encode()), seed]).standard_normal(out[name].shape)
        drawn = base * np.exp(spread * noise) if base else spread * noise
        out[name] = __import__('jax').numpy.asarray(drawn.astype(out[name].dtype))
    for name, factor in factors.items():
        out[name] = (out[name] * factor).astype(out[name].dtype)
    return out
```

```python
from contextlib import ExitStack

import numpy as np

import concourse.bass as bass
from concourse import mybir

P = 128
D = 1024
T = 256
NT = T // P
KC = D // P
RING = 6
FC = 2816 // P
HD = 64
SG = 16
NH = 8
MH = 4
PH = 8
TOPK = 16
NE1 = 128
EPS = 1e-6
BIG = 1e30

F32 = mybir.dt.float32
U32 = mybir.dt.uint32
ALU = mybir.AluOpType
ACT = mybir.ActivationFunctionType
AX = mybir.AxisListType.X

TWO_PI = 6.283185307179586
INV_2PI = 0.15915494309189535
C1 = 6.28125
C2 = TWO_PI - C1
ROUND = 12582912.0
PI_LO = 3.1415925
STAGES = 6

NORMS = ["even_norm", "mlp0_norm", "odd_norm", "mlp1_norm", "mix_norm", "peer_norm"]
LASTS = [("even", "out", 7), ("mlp0", "down", FC - 1), ("odd", "out", 7), ("mlp1", "down", FC - 1),
         ("mix", "out", 7), ("peer", "v", NE1 - 1)]
STAGE_OF = {"mlp0": 1, "mlp1": 3}
EVEN_HEADS = [(n // 2, n % 2, 4, HD * (n % 2)) for n in range(NH)]
MIX_HEADS = [(n // 2, n % 2, 4 + n // 2, HD * n) for n in range(NH)]
GATE_EVAC = 10 + 24
SMALL = ["x", "const", "param", "ssm", "keys", "mix"]
SMALL_N = {"x": 1, "const": 1, "param": 1, "ssm": 2, "keys": 1, "mix": 2}


def strip_names():
    names = []

    def mlp(n):
        names.extend([(n, "gate", 0), (n, "up", 0)])
        for c in range(1, FC):
            names.extend([(n, "gate", c), (n, "up", c), (n, "down", c - 1)])
        names.append((n, "down", FC - 1))

    names += [("even", "u", j) for j in range(4)] + [("even", "k", 0)]
    names += [("even", "q", j) for j in range(4)] + [("even", "v", 0)]
    names += [("even", "glu", j) for j in range(2)] + [("even", "out", j) for j in range(8)]
    mlp("mlp0")
    names += [("odd", "v", j) for j in range(8)]
    for j in range(8):
        names += [("odd", "q", j), ("odd", "k", j)]
    names += [("odd", "out", j) for j in range(8)]
    mlp("mlp1")
    names += [("mix", "if", 0)] + [("mix", "u", j) for j in range(4)]
    names += [("mix", "vm", j) for j in range(4)]
    names += [("mix", n, j) for n in ("qa", "ka", "va", "z") for j in range(4)]
    names += [("mix", "out", j) for j in range(8)]
    names += [("peer", "q", j) for j in range(2 * PH)]
    names += [("peer", "u", e) for e in range(NE1)] + [("peer", "v", e) for e in range(NE1)]
    return names


STRIPS = strip_names()
AT = {name: n for n, name in enumerate(STRIPS)}
NS = len(STRIPS)

CONST = {}
PARAM = {}


def _columns(table, widths):
    at = 0
    for name, width in widths:
        table[name] = (at, at + width)
        at += width
    return at


N_CONST = _columns(CONST, [
    ("ident", P), ("ones", P), ("head_ones", P), ("neg_tri", P), ("neg_ones", P), ("iota", P),
    ("window_mask", 3 * P), ("strict_mask", 3 * P), ("causal_mask", 3 * P), ("dilated_mask", 3 * P),
    ("dilated_count", 3 * P), ("head_row", MH * P), ("eps", 1), ("tokens", 0)])
N_PARAM = _columns(PARAM, [
    ("even_norm", KC), ("mlp0_norm", KC), ("odd_norm", KC), ("mlp1_norm", KC), ("mix_norm", KC),
    ("peer_norm", KC), ("q_norm", 1), ("k_norm", 1), ("sinks", NH), ("a_re", SG), ("a_im", SG),
    ("log_dt", SG), ("ssm_d", 4), ("b_glu", 4), ("conv_w", 16), ("conv_b", 4), ("ig_b", 1),
    ("fg_b", 1), ("mh_norm", MH), ("skip", MH), ("qn", 4), ("kn", 4)])


def build(nc, A, out):
    with ExitStack() as ctx:
        def sb(name, shape, dt=F32):
            return ctx.enter_context(nc.sbuf_tensor(name, shape, dt))

        def sem(name):
            return ctx.enter_context(nc.semaphore(name))

        ring = sb("ring", [P, RING, D])
        x_s = sb("x_s", [P, NT, D])
        xn = sb("xn", [P, NT, D])
        hT = sb("hT", [P, KC, T])
        const = sb("const", [P, N_CONST])
        param = sb("param", [P, N_PARAM])
        stat = sb("stat", [P, 8])
        keys_s = sb("keys_s", [P, 2, D])
        eT = sb("eT", [P, 3, T])
        ARENA = NE1 * T
        arena = sb("arena", [P, ARENA])
        ps = ctx.enter_context(nc.psum_tensor("ps", [P, 8, 512], F32))

        def k(name, a=0, b=None):
            lo, hi = CONST[name]
            return const[:, lo + a:(hi if b is None else lo + b)]

        def prm(name, a=0, b=None):
            lo, hi = PARAM[name]
            return param[:, lo + a:(hi if b is None else lo + b)]

        class Lay:

            def __init__(self, at=0):
                self.at = at

            def __call__(self, *shape):
                n = int(np.prod(shape))
                assert self.at + n <= ARENA, (self.at, n)
                v = arena[:, self.at:self.at + n]
                self.at += n
                if len(shape) == 2:
                    v = v.rearrange("p (a b) -> p a b", a=shape[0])
                if len(shape) == 3:
                    v = v.rearrange("p (a b c) -> p a b c", a=shape[0], b=shape[1])
                return v

        ident = k("ident")
        ones = k("ones")

        L = Lay()
        e_uT = L(4, T)
        e_qk = L(5, T)
        e_v = L(NT, P)
        e_B = L(2, 4, P)
        e_C = L(2, SG, 32)
        e_CW = L(2, SG, 32)
        e_ctmp = L(SG, 32)
        e_cos = L(SG, T)
        e_sin = L(SG, T)
        e_sq = L(5, T)
        e_rt = L(5, T)
        e_p = L(24, SG)
        e_z = L(4, 2, T)
        e_zt = L(2, 2 * T)
        e_ht = L(2, 2 * T)
        e_mark = L.at
        e_tmp = L(2, SG * P)
        L.at = e_mark
        e_h = L(4, 2, T)
        e_S = L(NH, 3 * P)
        e_PT = L(NH, 3 * P)
        e_sm = L(6, 2 * NH)
        e_y = L(4, T)
        e_mixT = L(KC, T)

        L = Lay()
        f_silu = L(2, T)
        f_act = L(2, T)

        L = Lay(2048)
        o_v = L(NT, D)
        o_qT = L(8, T)
        o_kT = L(8, T)
        o_t = L(2, 3 * P)
        o_sp = L(4, 3 * P)
        o_w0 = L(4, 3 * P)
        o_w = L(4, 3 * P)
        o_mixT = L(KC, T)

        L = Lay(1024)
        m_up = L(4, T + 3)
        m_x_at = L.at
        m_cv = L(4, T)
        m_cs = L(4, T)
        m_x = Lay(m_x_at)(MH, 3 * P)
        m_cT = L(4, T)
        m_sz = L(4, T)
        m_vm = L(NT, 512)
        m_va = L(NT, 512)
        m_qk = L(8, T)
        m_pT_at = L.at
        m_sq = L(8, T)
        m_rt = L(8, T)
        m_PT = Lay(m_pT_at)(NH, 3 * P)
        m_S = L(NH, 3 * P)
        m_bias = L(NH, T)
        m_wqk = L(2, MH, P)
        m_qm = L(MH, T)
        m_km = L(MH, T)
        m_row = L(10, T)
        m_rc = L(3, MH)
        m_d_at = L.at
        m_d = L(MH, 3 * P)
        m_hm = Lay(m_d_at)(MH, T)
        m_s = L(MH, 3 * P)
        m_em = L(MH, T)
        m_dn = L(MH, T)
        m_sm = L(6, 2 * NH)
        m_mixT = L(KC, T)

        act = arena[:, 0:NE1 * T].rearrange("p (e t) -> p e t", t=T)
        L = Lay(96 * T)
        r_q = L(2, T)
        r_sc = L(4, NT, P)
        r_v = L(NT, 2 * PH, TOPK)
        r_i = L(NT, 2 * PH, TOPK)
        r_if = L(NT, 2 * PH, TOPK)
        r_c = L(2, 256)
        r_vc = L(NT, PH, TOPK)
        r_ic = L(NT, PH, TOPK)
        r_hl = L(2, NT * PH * TOPK)
        r_hlf = L(2, NT * PH * TOPK)
        r_e = L(3, NT * PH * TOPK)
        r_sum = L(1, NT * PH)
        oh = hT[:, :, :].rearrange("p a (b c) -> p (a b) c", c=P).rearrange(
            "p (s t) c -> p s t c", s=2)

        strip_landed = [sem(f"strip_landed{i}") for i in range(RING)]
        strip_done = sem("strip_done")
        small_in = [sem(f"small_in{i}") for i in range(8)]
        squares = sem("squares")
        roots = sem("roots")
        xn_ready = sem("xn_ready")
        x_ready = sem("x_ready")
        turned = sem("turned")
        hT_act = sem("hT_act")
        hT_dve = sem("hT_dve")
        evac = sem("evac")
        silu_ready = sem("silu_ready")
        ff_ready = sem("ff_ready")
        prm_act = sem("prm_act")
        prm_dve = sem("prm_dve")
        cw_ready = sem("cw_ready")
        sq_ready = sem("sq_ready")
        sq_summed = sem("sq_summed")
        rt_ready = sem("rt_ready")
        qk_ready = sem("qk_ready")
        score_done = sem("score_done")
        score_out = sem("score_out")
        shifted = sem("shifted")
        exp_done = sem("exp_done")
        probs = sem("probs")
        pT_done = sem("pT_done")
        pT_out = sem("pT_out")
        pv_done = sem("pv_done")
        pv_out = sem("pv_out")
        bu_done = sem("bu_done")
        bu_used = sem("bu_used")
        scanned = sem("scanned")
        back = sem("back")
        y_done = sem("y_done")
        y_sum = sem("y_sum")
        y_gelu = sem("y_gelu")
        glu_sig = sem("glu_sig")
        glu_out = sem("glu_out")
        z_done = sem("z_done")
        z_log = sem("z_log")
        sp_ready = sem("sp_ready")
        sp_masked = sem("sp_masked")
        cum_done = sem("cum_done")
        w_masked = sem("w_masked")
        w_ready = sem("w_ready")
        ov_done = sem("ov_done")
        ov_out = sem("ov_out")
        gate_act = sem("gate_act")
        rows_ready = sem("rows_ready")
        cols_done = sem("cols_done")
        cols_out = sem("cols_out")
        conv_done = sem("conv_done")
        conv_silu = sem("conv_silu")
        qkm_done = sem("qkm_done")
        qkm_out = sem("qkm_out")
        bcast_done = sem("bcast_done")
        expo_in = sem("expo_in")
        expo_out = sem("expo_out")
        em_out = sem("em_out")
        st_done = sem("st_done")
        s_ready = sem("s_ready")
        num_done = sem("num_done")
        den_abs = sem("den_abs")
        hm_sq = sem("hm_sq")
        hm_summed = sem("hm_summed")
        hm_rt = sem("hm_rt")
        ym_ready = sem("ym_ready")
        key_done = sem("key_done")
        key_out = sem("key_out")
        key_used = sem("key_used")
        route_dve = sem("route_dve")
        route_act = sem("route_act")
        route_ready = sem("route_ready")
        eT_done = sem("eT_done")
        gelu_done = sem("gelu_done")
        onehot_ready = sem("onehot_ready")
        spread = sem("spread")
        gate_free = sem("gate_free")
        yT_out = sem("yT_out")
        out_turned = sem("out_turned")
        act_chain = sem("act_chain")
        dve_chain = sem("dve_chain")
        pool_chain = sem("pool_chain")
        out_done = sem("out_done")

        block = ctx.enter_context(nc.Block())

        class Chain:

            def __init__(self, eng, s):
                self.eng, self.s, self.n = eng, s, 0

            def add(self, ins):
                self.n += 1
                ins.then_inc(self.s, 1)

            def wait(self):
                self.eng.wait_ge(self.s, self.n)

            def link(self, ins):
                self.add(ins)
                self.wait()

        n_strips = AT[LASTS[STAGES - 1]] + 1

        def small_load(eng, name, dst, src):
            eng.dma_start(dst, src).then_inc(small_in[SMALL.index(name)], 16)

        def small_wait(eng, name):
            eng.wait_ge(small_in[SMALL.index(name)], 16 * SMALL_N[name])

        @block.sync
        def _(sp):
            for n in range(RING):
                sp.dma_start(ring[:, n, :], A["strips"][n]).then_inc(strip_landed[n], 16)
            rounds = n_strips // RING
            with sp.Fori(1, rounds) as i:
                for j in range(RING):
                    sp.wait_ge(strip_done, RING * i + (j + 1 - RING))
                    sp.dma_start(ring[:, j, :], A["strips"][RING * i + j]).then_inc(strip_landed[j], 16)
            for n in range(rounds * RING, n_strips):
                sp.wait_ge(strip_done, n + 1 - RING)
                sp.dma_start(ring[:, n % RING, :], A["strips"][n]).then_inc(strip_landed[n % RING], 16)
            sp.wait_ge(x_ready, NT * STAGES)
            sp.dma_start(out.rearrange("b (a p) d -> p (b a) d", p=P), x_s[:, :, :]).then_inc(out_done, 16)
            sp.wait_ge(out_done, 16)

        @block.tensor
        def _(pe):
            def landed(n, i=None):
                v = 16 * (n // RING + 1)
                pe.wait_ge(strip_landed[n % RING], v if i is None else 16 * i + v)
                return ring[:, n % RING, :]

            nproj = [0]

            def proj_bank():
                m = nproj[0]
                nproj[0] += 1
                if m >= 2:
                    pe.wait_ge(evac, m - 1)
                return 4 + m % 2

            def proj_fm(name):
                w = landed(AT[name])
                b = proj_bank()
                for c in range(KC):
                    mm = pe.matmul(ps[:, b, 0:T], w[:, c * P:(c + 1) * P], hT[:, c, :],
                                   start=(c == 0), stop=(c == KC - 1))
                mm.then_inc(strip_done, 1)

            def proj_tm(name):
                w = landed(AT[name])
                b = proj_bank()
                for a in range(NT):
                    for c in range(KC):
                        mm = pe.matmul(ps[:, b, a * P:(a + 1) * P], hT[:, c, a * P:(a + 1) * P],
                                       w[:, c * P:(c + 1) * P], start=(c == 0), stop=(c == KC - 1))
                mm.then_inc(strip_done, 1)

            def norm(i):
                pe.wait_ge(xn_ready, i + 1)
                for c in range(KC // 2):
                    if c >= 2:
                        pe.wait_ge(hT_dve if c % 2 else hT_act, 4 * i + 2)
                    for cc in range(2):
                        for a in range(NT):
                            mm = pe.transpose(ps[:, 6 + c % 2, cc * T + a * P:cc * T + (a + 1) * P],
                                              xn[:, a, (2 * c + cc) * P:(2 * c + cc + 1) * P], ident)
                    mm.then_inc(turned, 1)
                pe.wait_ge(hT_act, 4 * i + 4)
                pe.wait_ge(hT_dve, 4 * i + 4)

            def seed(i):
                if i:
                    pe.wait_ge(x_ready, NT * i)
                for a in range(NT):
                    for b in range(2):
                        pe.matmul(ps[:, 2 * a + b, :], ident, x_s[:, a, b * 512:(b + 1) * 512],
                                  start=True, stop=False, skip_group_check=True)

            def rows(w, lhs, last):
                for a in range(NT):
                    for b in range(2):
                        mm = pe.matmul(ps[:, 2 * a + b, :], lhs[:, a * P:(a + 1) * P],
                                       w[:, b * 512:(b + 1) * 512], start=False, stop=last,
                                       skip_group_check=True)
                mm.then_inc(strip_done, 1)

            def attention(t, qk, heads, v, probs_s, pT):
                pe.wait_ge(qk_ready, t + 1)
                for n, (jq, half, jk, vc) in enumerate(heads):
                    if n >= 4:
                        pe.wait_ge(score_out, NH * t + n - 3)
                    lo, hi = HD * half, HD * half + HD
                    pe.matmul(ps[:, n % 4, 0:P], qk[lo:hi, jq, 0:P], qk[lo:hi, jk, 0:P],
                              start=True, stop=True)
                    pe.matmul(ps[:, n % 4, P:3 * P], qk[lo:hi, jq, P:T], qk[lo:hi, jk, :],
                              start=True, stop=True).then_inc(score_done, 1)

            def attention_out(t, heads, v, probs_s, pT):
                pe.wait_ge(probs, t + 1)
                for n in range(NH):
                    if n >= 4:
                        pe.wait_ge(pT_out, NH * t + n - 3)
                    for b in range(3):
                        mm = pe.transpose(ps[:, n % 4, b * P:(b + 1) * P],
                                          probs_s[:, n, b * P:(b + 1) * P], ident)
                    mm.then_inc(pT_done, 1)
                for n, (jq, half, jk, vc) in enumerate(heads):
                    pe.wait_ge(pT_out, NH * t + n + 1)
                    if n % 2 == 0 and n >= 4:
                        pe.wait_ge(pv_out, 4 * t + n // 2 - 1)
                    b = 6 + (n // 2) % 2
                    o = ps[HD * half:HD * half + HD, b, 0:T]
                    pe.matmul(o, v[:, 0, vc:vc + HD], pT[:, n, 0:T], start=True, stop=False,
                              skip_group_check=True)
                    mm = pe.matmul(o[:, P:T], v[:, 1, vc:vc + HD], pT[:, n, T:3 * P], start=False,
                                   stop=True, skip_group_check=True)
                    if n % 2:
                        mm.then_inc(pv_done, 1)

            def even():
                for j in range(4):
                    proj_fm(("even", "u", j))
                proj_fm(("even", "k", 0))
                for j in range(4):
                    proj_fm(("even", "q", j))
                proj_tm(("even", "v", 0))
                pe.wait_ge(sq_ready, 1)
                for b, n in ((0, 512), (1, 512), (2, 256)):
                    mm = pe.matmul(ps[:, b, 0:n], k("head_ones"),
                                   e_sq.rearrange("p a b -> p (a b)")[:, b * 512:b * 512 + n],
                                   start=True, stop=True)
                mm.then_inc(sq_summed, 1)

                def bu(c):
                    if c >= 2:
                        pe.wait_ge(bu_used, c - 1)
                    lo = 32 * (c % 4)
                    for part in range(2):
                        mm = pe.matmul(ps[:, 6 + c % 2, part * T:(part + 1) * T],
                                       e_B[lo:lo + 32, part, c // 4, :], e_uT[lo:lo + 32, c // 4, :],
                                       start=True, stop=True)
                    mm.then_inc(bu_done, 1)

                def y(c):
                    pe.wait_ge(back, c + 1)
                    if c == 0:
                        pe.wait_ge(cw_ready, 1)
                    lo = 32 * (c % 4)
                    for part in range(2):
                        mm = pe.matmul(ps[lo:lo + 32, 4 + (c // 4) % 2, 0:T], e_CW[:, part, c, :],
                                       e_h[:, c % 4, part, :], start=(part == 0),
                                       stop=(part == 1), skip_group_check=True)
                    mm.then_inc(y_done, 1)

                small_wait(pe, "ssm")
                bu(0)
                bu(1)
                attention(0, e_qk, EVEN_HEADS, e_v, e_S, e_PT)
                for c in range(SG):
                    if c >= 4 and c % 4 == 0 and c >= 8:
                        pe.wait_ge(y_sum, c // 4 - 1)
                    if c == 0:
                        pe.wait_ge(evac, nproj[0])
                    y(c)
                    if c + 2 < SG:
                        bu(c + 2)
                attention_out(0, EVEN_HEADS, e_v, e_S, e_PT)
                pe.wait_ge(y_gelu, 4)
                for s in range(2):
                    w = landed(AT[("even", "glu", s)])
                    for j in range(2):
                        for c in range(4):
                            mm = pe.matmul(ps[:, 4 + s, j * T:(j + 1) * T],
                                           w[:, c * T + j * P:c * T + (j + 1) * P], e_y[:, c, :],
                                           start=(c == 0), stop=(c == 3))
                    mm.then_inc(strip_done, 1)
                seed(0)
                pe.wait_ge(pv_out, 4)
                for j in range(8):
                    if j == 4:
                        pe.wait_ge(glu_out, 1)
                    rows(landed(AT[("even", "out", j)]), e_mixT[:, j, :], j == 7)

            def mlp(n, name):
                base = AT[(name, "gate", 0)]

                def gate_up(slot, bank, i=None):
                    for part in range(2):
                        w = landed(slot + part, i)
                        for c in range(KC):
                            mm = pe.matmul(ps[:, bank + 2 * part, 0:T],
                                           w[:, c * P:(c + 1) * P], hT[:, c, :],
                                           start=(c == 0), stop=(c == KC - 1))
                        mm.then_inc(strip_done, 1)

                seed(STAGE_OF[name])
                gate_up(base, 4)
                with pe.Fori(0, (FC - 2) // 2) as i:
                    for u in range(2):
                        pe.wait_ge(ff_ready, 2 * i + (FC * n + u))
                        gate_up(base + 2 + 3 * u, 4 + (1 + u) % 2, i)
                        w = landed(base + 4 + 3 * u, i)
                        pe.wait_ge(ff_ready, 2 * i + (FC * n + 1 + u))
                        rows(w, f_act[:, u, :], False)
                last = base + 2 + 3 * (FC - 2)
                pe.wait_ge(ff_ready, FC * n + FC - 2)
                gate_up(last, 4 + (FC - 1) % 2)
                pe.wait_ge(ff_ready, FC * n + FC - 1)
                rows(landed(last + 2), f_act[:, FC % 2, :], False)
                w = landed(last + 3)
                pe.wait_ge(ff_ready, FC * n + FC)
                rows(w, f_act[:, (FC - 1) % 2, :], True)

            def odd():
                for j in range(8):
                    proj_tm(("odd", "v", j))

                def z(h):
                    j, lo = h // 2, HD * (h % 2)
                    if h % 2 == 0:
                        pe.wait_ge(evac, nproj[0])
                    if h >= 4:
                        pe.wait_ge(w_masked, h - 3)
                    pe.matmul(ps[:, h % 4, 0:T], o_kT[lo:lo + HD, j, 0:P], o_qT[lo:lo + HD, j, :],
                              start=True, stop=True, skip_group_check=True)
                    pe.matmul(ps[:, h % 4, T:3 * P], o_kT[lo:lo + HD, j, P:T], o_qT[lo:lo + HD, j, P:T],
                              start=False, stop=True, skip_group_check=True).then_inc(z_done, 1)

                def cum(h):
                    pe.wait_ge(sp_masked, h + 1)
                    pe.matmul(ps[:, h % 4, 0:3 * P], k("neg_tri"), o_sp[:, h % 4, :], start=False,
                              stop=False, skip_group_check=True)
                    pe.matmul(ps[:, h % 4, P:T], k("neg_ones"), o_sp[:, h % 4, T:3 * P], start=False,
                              stop=True, skip_group_check=True).then_inc(cum_done, 1)

                def ov(h):
                    pe.wait_ge(w_ready, h + 1)
                    if h % 2 == 0 and h >= 4:
                        pe.wait_ge(ov_out, h // 2 - 1)
                    o = ps[HD * (h % 2):HD * (h % 2) + HD, 6 + (h // 2) % 2, 0:T]
                    pe.matmul(o, o_v[:, 0, h * HD:(h + 1) * HD], o_w[:, h % 4, 0:T], start=True,
                              stop=False, skip_group_check=True)
                    mm = pe.matmul(o[:, P:T], o_v[:, 1, h * HD:(h + 1) * HD], o_w[:, h % 4, T:3 * P],
                                   start=False, stop=True, skip_group_check=True)
                    if h % 2:
                        mm.then_inc(ov_done, 1)

                for j in range(10):
                    if j < 8:
                        proj_fm(("odd", "q", j))
                    if 1 <= j <= 8:
                        cum(2 * j - 2)
                        cum(2 * j - 1)
                    if j < 8:
                        proj_fm(("odd", "k", j))
                    if j >= 2:
                        ov(2 * j - 4)
                        ov(2 * j - 3)
                    if j < 8:
                        z(2 * j)
                        z(2 * j + 1)
                pe.wait_ge(w_masked, 16)
                seed(2)
                pe.wait_ge(ov_out, 8)
                for j in range(8):
                    rows(landed(AT[("odd", "out", j)]), o_mixT[:, j, :], j == 7)

            def mix():
                w = landed(AT[("mix", "if", 0)])
                b = proj_bank()
                for part in range(2):
                    for c in range(KC):
                        mm = pe.matmul(ps[0:MH, b, part * T:(part + 1) * T],
                                       w[:, c * P + part * MH:c * P + (part + 1) * MH], hT[:, c, :],
                                       start=(c == 0), stop=(c == KC - 1))
                mm.then_inc(strip_done, 1)
                for j in range(4):
                    proj_fm(("mix", "u", j))
                for j in range(4):
                    proj_tm(("mix", "vm", j))
                pe.wait_ge(rows_ready, 1)
                for n in range(3):
                    mm = pe.transpose(ps[:, 7, n * MH:(n + 1) * MH],
                                      m_row[0:MH, 7 if n == 2 else 3, (n % 2) * P:(n % 2 + 1) * P],
                                      ident[0:MH, 0:MH])
                mm.then_inc(cols_done, 1)
                small_wait(pe, "mix")
                for h in range(MH):
                    pe.wait_ge(conv_silu, h + 1)
                    for part in range(2):
                        mm = pe.matmul(ps[:, h, part * T:(part + 1) * T], m_wqk[:, part, h, :],
                                       m_cT[:, h, :], start=True, stop=True)
                    mm.then_inc(qkm_done, 1)
                for n in ("qa", "ka"):
                    for j in range(4):
                        proj_fm(("mix", n, j))
                for j in range(4):
                    proj_tm(("mix", "va", j))
                for h in range(MH):
                    pe.wait_ge(qkm_out, h + 1)
                    pe.matmul(ps[:, h, :], k("head_row", h * P, (h + 1) * P)[0:MH],
                              m_row[0:MH, 4:6, :].rearrange("p a b -> p (a b)"), start=True,
                              stop=True).then_inc(bcast_done, 1)
                for j in range(4):
                    proj_fm(("mix", "z", j))
                for h in range(MH):
                    b = 6 + h % 2
                    if h == 1:
                        pe.wait_ge(cols_out, 1)
                    if h >= 2:
                        pe.wait_ge(s_ready, h - 1)
                    pe.matmul(ps[:, b, 0:T], m_km[:, h, 0:P], m_qm[:, h, :], start=True, stop=True)
                    pe.matmul(ps[:, b, T:3 * P], m_km[:, h, P:T], m_qm[:, h, P:T], start=True,
                              stop=True).then_inc(st_done, 1)
                for h in range(MH):
                    pe.wait_ge(s_ready, h + 1)
                    if h == 0:
                        pe.wait_ge(em_out, MH)
                    vh = m_vm[:, :, h * P:(h + 1) * P]
                    for at, l0, l1 in ((0, vh[:, 0, :], vh[:, 1, :]), (T, ones, ones)):
                        pe.matmul(ps[:, h, at:at + T], l0, m_s[:, h, 0:T], start=(at == 0), stop=False,
                                  skip_group_check=True)
                        mm = pe.matmul(ps[:, h, at + P:at + T], l1, m_s[:, h, T:3 * P], start=False,
                                       stop=True, skip_group_check=True)
                    mm.then_inc(num_done, 1)
                pe.wait_ge(sq_ready, 2)
                pe.wait_ge(evac, nproj[0])
                pe.wait_ge(s_ready, MH)
                for b in range(4):
                    mm = pe.matmul(ps[:, 4 + b, :], k("head_ones"),
                                   m_sq.rearrange("p a b -> p (a b)")[:, b * 512:(b + 1) * 512],
                                   start=True, stop=True)
                mm.then_inc(sq_summed, 1)
                pe.wait_ge(hm_sq, 1)
                for b in range(2):
                    mm = pe.matmul(ps[:, b, :], ones,
                                   m_dn.rearrange("p a b -> p (a b)")[:, b * 512:(b + 1) * 512],
                                   start=True, stop=True)
                mm.then_inc(hm_summed, 1)
                pe.wait_ge(hm_rt, 1)
                attention(1, m_qk, MIX_HEADS, m_va, m_S, m_PT)
                attention_out(1, MIX_HEADS, m_va, m_S, m_PT)
                seed(4)
                pe.wait_ge(ym_ready, 1)
                pe.wait_ge(pv_out, 8)
                for j in range(8):
                    rows(landed(AT[("mix", "out", j)]), m_mixT[:, j, :], j == 7)

            def peer():
                first = nproj[0]
                small_wait(pe, "keys")

                def key_scores(s):
                    pe.wait_ge(evac, first + s + 1)
                    if s >= 2:
                        pe.wait_ge(key_out, s - 1)
                    for a in range(NT):
                        mm = pe.matmul(ps[:, 6 + s % 2, a * P:(a + 1) * P],
                                       r_q[:, s % 2, a * P:(a + 1) * P],
                                       keys_s[:, s % 2, (s // 2) * P:(s // 2 + 1) * P],
                                       start=True, stop=True)
                    mm.then_inc(key_done, 1)

                for s in range(2 * PH):
                    proj_fm(("peer", "q", s))
                    if s:
                        key_scores(s - 1)
                key_scores(2 * PH - 1)
                pe.wait_ge(evac, nproj[0])
                base = AT[("peer", "u", 0)]

                def up(e, i=None):
                    w = landed(base + e, i)
                    if i is not None:
                        pe.wait_ge(gelu_done, RING * i + (e - 1))
                    elif e >= 2:
                        pe.wait_ge(gelu_done, e - 1)
                    for c in range(KC):
                        mm = pe.matmul(ps[:, 4 + e % 2, 0:T], w[:, c * P:(c + 1) * P], hT[:, c, :],
                                       start=(c == 0), stop=(c == KC - 1))
                    mm.then_inc(strip_done, 1)

                for e in range(RING):
                    up(e)
                with pe.Fori(1, NE1 // RING) as i:
                    for e in range(RING):
                        up(e, i)
                for e in range(NE1 // RING * RING, NE1):
                    up(e)
                pe.wait_ge(route_ready, 1)
                for n in range(3):
                    for a in range(NT):
                        mm = pe.transpose(ps[:, 6 + n // 2, (n % 2) * T + a * P:(n % 2) * T + (a + 1) * P],
                                          xn[:, 0, n * T + a * P:n * T + (a + 1) * P], ident)
                mm.then_inc(eT_done, 1)
                with pe.Fori(0, T // 8) as i:
                    for g in range(2):
                        pe.wait_ge(onehot_ready, 2 * i + (g + 1))
                        pe.wait_ge(gate_free, 2 * i + (g + 1))
                        for q in range(4):
                            mm = pe.matmul(ps[:, 4 + 2 * g, q * P:(q + 1) * P], oh[:, 1, 4 * g + q, :],
                                           oh[:, 0, 4 * g + q, :], start=True, stop=True)
                        mm.then_inc(spread, 1)
                for c in range(KC):
                    for a in range(NT):
                        pe.matmul(ps[:, c // 2, (c % 2) * T + a * P:(c % 2) * T + (a + 1) * P],
                                  x_s[:, a, c * P:(c + 1) * P], ident, start=(c % 2 == 0 and a == 0),
                                  stop=False, skip_group_check=True)
                pe.wait_ge(gate_free, T // 4 + 2)
                base = AT[("peer", "v", 0)]

                def down(e, i=None, last=False):
                    w = landed(base + e, i)
                    at = act[:, e, :] if i is None else act[:, bass.ds(RING * i + e, 1), :].rearrange(
                        "p a t -> p (a t)")
                    for c in range(KC):
                        mm = pe.matmul(ps[:, c // 2, (c % 2) * T:(c % 2 + 1) * T],
                                       w[:, c * P:(c + 1) * P], at, start=False, stop=last,
                                       skip_group_check=True)
                    mm.then_inc(strip_done, 1)

                with pe.Fori(0, NE1 // RING) as i:
                    for e in range(RING):
                        down(e, i)
                for e in range(NE1 // RING * RING, NE1):
                    down(e, None, e == NE1 - 1)
                pe.wait_ge(yT_out, 2)
                for c in range(KC):
                    for a in range(NT):
                        mm = pe.transpose(ps[:, 4 + 2 * a + c // 4, (c % 4) * P:(c % 4 + 1) * P],
                                          xn[:, c // 4, (c % 4) * T + a * P:(c % 4) * T + (a + 1) * P], ident)
                mm.then_inc(out_turned, 1)

            small_wait(pe, "const")
            for n, (name, body) in enumerate([("even", even), ("mlp0", lambda: mlp(0, "mlp0")),
                                              ("odd", odd), ("mlp1", lambda: mlp(1, "mlp1")),
                                              ("mix", mix), ("peer", peer)][:STAGES]):
                norm(n)
                body()

        @block.scalar
        def _(sc):
            small_load(sc, "x", x_s[:, :, :], A["x"].rearrange("b (a p) d -> p (b a) d", p=P))
            small_load(sc, "param", param[:, :], A["param"])
            small_load(sc, "const", const[:, :], A["const"])
            ch = Chain(sc, act_chain)
            nproj = [0]

            def norm(i):
                if i == 0:
                    small_wait(sc, "x")
                    small_wait(sc, "const")
                    small_wait(sc, "param")
                for a in range(NT):
                    if i:
                        sc.wait_ge(x_ready, NT * (i - 1) + a + 1)
                    ch.add(sc.activation(hT[:, 0:4, :].rearrange("p a b -> p (a b)"), x_s[:, a, :], ACT.Square, accum_out=stat[:, a:a + 1]))
                    ch.wait()
                sc.activation(stat[:, 2:4], stat[:, 0:2], ACT.Sqrt, bias=k("eps"),
                              scale=1.0 / D).then_inc(roots, 1)
                for c in range(0, KC // 2, 2):
                    sc.wait_ge(turned, 4 * i + c + 1)
                    for cc in range(2):
                        sc.activation(hT[:, 2 * c + cc, :], ps[:, 6, cc * T:(cc + 1) * T], ACT.Copy,
                                      scale=prm(NORMS[i], 2 * c + cc, 2 * c + cc + 1)).then_inc(hT_act, 1)

            def out_of(name, dst, src=None, func=ACT.Copy, width=T, **kw):
                sc.wait_ge(strip_done, AT[name] + 1)
                b = 4 + nproj[0] % 2
                nproj[0] += 1
                sc.activation(dst, ps[:, b, 0:width] if src is None else src(b), func, **kw).then_inc(evac, 1)

            def softmax(t, S, sm, sink):
                sc.wait_ge(shifted, t + 1)
                f = S.rearrange("p a b -> p (a b)")
                if sink:
                    ch.add(sc.activation(sm[:, 2, :], sm[:, 2, :], ACT.Exp))
                sc.activation(f, f, ACT.Exp).then_inc(exp_done, 1)

            def attention_out(t, pT, mixT, at):
                for n in range(NH):
                    sc.wait_ge(pT_done, NH * t + n + 1)
                    sc.activation(pT[:, n, :], ps[:, n % 4, 0:3 * P], ACT.Copy).then_inc(pT_out, 1)
                for j in range(4):
                    sc.wait_ge(pv_done, 4 * t + j + 1)
                    sc.activation(mixT[:, at + j, :], ps[:, 6 + j % 2, 0:T], ACT.Copy).then_inc(pv_out, 1)

            def even():
                sc.activation(e_p[:, 0, :], prm("log_dt"), ACT.Exp).then_inc(prm_act, 1)
                sc.wait_ge(prm_dve, 1)
                sc.activation(e_p[:, 3, :], e_p[:, 1, :], ACT.Exp).then_inc(prm_act, 1)
                sc.wait_ge(prm_dve, 2)
                sc.activation(e_p[:, 9, :], e_p[:, 6, :], ACT.Sin).then_inc(prm_act, 1)
                sc.activation(e_p[:, 10, :], e_p[:, 7, :], ACT.Sin).then_inc(prm_act, 1)
                for j in range(4):
                    out_of(("even", "u", j), e_uT[:, j, :])
                out_of(("even", "k", 0), e_qk[:, 4, :])
                for j in range(4):
                    out_of(("even", "q", j), e_qk[:, j, :])
                out_of(("even", "v", 0), e_v.rearrange("p a b -> p (a b)"))
                sc.wait_ge(sq_summed, 1)
                sc.activation(e_rt.rearrange("p a b -> p (a b)"),
                              ps[:, 0:3, :].rearrange("p a b -> p (a b)")[:, 0:5 * T], ACT.Sqrt,
                              bias=k("eps"), scale=1.0 / HD).then_inc(rt_ready, 1)
                softmax(0, e_S, e_sm, True)
                attention_out(0, e_PT, e_mixT, 0)
                for j in range(4):
                    sc.wait_ge(y_sum, j + 1)
                    sc.activation(e_y[:, j, :], e_y[:, j, :], ACT.Gelu_apprx_tanh).then_inc(y_gelu, 1)
                for s in range(2):
                    sc.wait_ge(strip_done, AT[("even", "glu", s)] + 1)
                    for j in range(2):
                        sc.activation(e_sq[:, 2 * s + j, :], ps[:, 4 + s, j * T:(j + 1) * T], ACT.Sigmoid,
                                      bias=prm("b_glu", 2 * s + j, 2 * s + j + 1)).then_inc(glu_sig, 1)

            def mlp(n, name):
                base = AT[(name, "gate", 0)]

                def silu(strip, c, i=None):
                    sc.wait_ge(strip_done, strip + 1 if i is None else 6 * i + (strip + 1))
                    if i is not None:
                        sc.wait_ge(ff_ready, 2 * i + (FC * n + c - 1))
                    elif c >= 2:
                        sc.wait_ge(ff_ready, FC * n + c - 1)
                    sc.activation(f_silu[:, c % 2, :], ps[:, 4 + c % 2, 0:T], ACT.Silu).then_inc(silu_ready, 1)

                silu(base, 0)
                with sc.Fori(0, (FC - 2) // 2) as i:
                    silu(base + 2, 1, i)
                    silu(base + 5, 2, i)
                silu(base + 2 + 3 * (FC - 2), FC - 1)

            def odd():
                for j in range(8):
                    out_of(("odd", "v", j), o_v[:, :, j * P:(j + 1) * P],
                           lambda b: ps[:, b, 0:T].rearrange("p (a c) -> p a c", a=NT))

                def softplus(h):
                    sc.wait_ge(z_done, h + 1)
                    if h >= 2:
                        sc.wait_ge(sp_ready, h - 1)
                    t = o_t[:, h % 2, :]
                    ch.link(sc.activation(t, ps[:, h % 4, 0:3 * P], ACT.Abs))
                    ch.link(sc.activation(t, t, ACT.Exp, scale=-1.0))
                    sc.activation(t, t, ACT.Ln, bias=1.0).then_inc(z_log, 1)

                def weights(h):
                    sc.wait_ge(w_masked, h + 1)
                    if h >= 4:
                        sc.wait_ge(ov_done, (h - 4) // 2 + 1)
                    sc.activation(o_w[:, h % 4, :], o_w0[:, h % 4, :], ACT.Exp).then_inc(w_ready, 1)

                def ov_copy(j):
                    sc.wait_ge(ov_done, j + 1)
                    sc.activation(o_mixT[:, j, :], ps[:, 6 + j % 2, 0:T], ACT.Copy).then_inc(ov_out, 1)

                for j in range(10):
                    if j < 8:
                        out_of(("odd", "q", j), o_qT[:, j, :], scale=HD ** -0.5)
                    if 1 <= j <= 8:
                        weights(2 * j - 2)
                        weights(2 * j - 1)
                    if j < 8:
                        out_of(("odd", "k", j), o_kT[:, j, :])
                    if j >= 2:
                        ov_copy(j - 2)
                    if j < 8:
                        softplus(2 * j)
                        softplus(2 * j + 1)

            def mix():
                r = m_row[0:MH]
                sc.wait_ge(strip_done, AT[("mix", "if", 0)] + 1)
                b = 4 + nproj[0] % 2
                nproj[0] += 1
                ch.add(sc.activation(r[:, 0, :], ps[0:MH, b, 0:T], ACT.Identity, bias=prm("ig_b")[0:MH]))
                sc.activation(r[:, 1, :], ps[0:MH, b, T:2 * T], ACT.Identity,
                              bias=prm("fg_b")[0:MH]).then_inc(evac, 1)
                sc.wait_ge(evac, nproj[0])
                ch.link(sc.activation(r[:, 2, :], r[:, 1, :], ACT.Abs))
                ch.link(sc.activation(r[:, 2, :], r[:, 2, :], ACT.Exp, scale=-1.0))
                sc.activation(r[:, 2, :], r[:, 2, :], ACT.Ln, bias=1.0).then_inc(gate_act, 1)
                for j in range(4):
                    out_of(("mix", "u", j), m_up[:, j, 3:T + 3])
                for j in range(4):
                    out_of(("mix", "vm", j), m_vm[:, :, j * P:(j + 1) * P],
                           lambda b: ps[:, b, 0:T].rearrange("p (a c) -> p a c", a=NT))
                sc.wait_ge(cols_done, 1)
                sc.activation(m_rc.rearrange("p a b -> p (a b)"), ps[:, 7, 0:3 * MH],
                              ACT.Copy).then_inc(cols_out, 1)
                for j in range(4):
                    sc.wait_ge(conv_done, j + 1)
                    sc.activation(m_cT[:, j, :], m_cv[:, j, :], ACT.Silu).then_inc(conv_silu, 1)
                for h in range(MH):
                    sc.wait_ge(qkm_done, h + 1)
                    ch.add(sc.activation(m_qm[:, h, :], ps[:, h, 0:T], ACT.Copy))
                    sc.activation(m_km[:, h, :], ps[:, h, T:2 * T], ACT.Copy,
                                  scale=P ** -0.5).then_inc(qkm_out, 1)
                for n, at in (("qa", 0), ("ka", 4)):
                    for j in range(4):
                        out_of(("mix", n, j), m_qk[:, at + j, :])
                for j in range(4):
                    out_of(("mix", "va", j), m_va[:, :, j * P:(j + 1) * P],
                           lambda b: ps[:, b, 0:T].rearrange("p (a c) -> p a c", a=NT))
                sc.wait_ge(cols_out, 1)
                for h in range(MH):
                    sc.wait_ge(expo_in, h + 1)
                    for n, col in ((0, 0), (1, 2), (2, 1)):
                        ins = sc.activation(m_d[:, h, n * P:(n + 1) * P], m_x[:, h, n * P:(n + 1) * P],
                                            ACT.Exp, bias=m_rc[:, col, h:h + 1])
                        if n < 2:
                            ch.add(ins)
                    ins.then_inc(expo_out, 1)
                    sc.activation(m_em[:, h, :], ps[:, h, T:2 * T], ACT.Exp, scale=-1.0).then_inc(em_out, 1)
                for j in range(4):
                    out_of(("mix", "z", j), m_sz[:, j, :], func=ACT.Sigmoid)
                for h in range(MH):
                    sc.wait_ge(num_done, h + 1)
                    sc.activation(m_dn[:, h, :], ps[:, h, T:2 * T], ACT.Abs).then_inc(den_abs, 1)
                sc.wait_ge(sq_summed, 2)
                sc.activation(m_rt.rearrange("p a b -> p (a b)"),
                              ps[:, 4:8, :].rearrange("p a b -> p (a b)"), ACT.Sqrt,
                              bias=k("eps"), scale=1.0 / HD).then_inc(rt_ready, 1)
                sc.wait_ge(hm_summed, 1)
                sc.activation(m_dn.rearrange("p a b -> p (a b)"),
                              ps[:, 0:2, :].rearrange("p a b -> p (a b)"), ACT.Sqrt,
                              bias=k("eps"), scale=1.0 / P).then_inc(hm_rt, 1)
                softmax(1, m_S, m_sm, False)
                attention_out(1, m_PT, m_mixT, 4)

            def peer():
                def key_copy(s):
                    sc.wait_ge(key_done, s + 1)
                    if s >= 4:
                        sc.wait_ge(key_used, s - 3)
                    sc.activation(r_sc[:, s % 4].rearrange("p a b -> p (a b)"), ps[:, 6 + s % 2, 0:T],
                                  ACT.Copy).then_inc(key_out, 1)

                for s in range(2 * PH):
                    if s >= 2:
                        sc.wait_ge(key_done, s - 1)
                    out_of(("peer", "q", s), r_q[:, s % 2, :])
                    if s:
                        key_copy(s - 1)
                key_copy(2 * PH - 1)
                base = AT[("peer", "u", 0)]

                def gelu(e, i=None):
                    sc.wait_ge(strip_done, base + e + 1 if i is None else RING * i + (base + e + 1))
                    dst = act[:, e, :] if i is None else act[:, bass.ds(RING * i + e, 1), :].rearrange(
                        "p a t -> p (a t)")
                    sc.activation(dst, ps[:, 4 + e % 2, 0:T], ACT.Gelu).then_inc(gelu_done, 1)

                with sc.Fori(0, 10) as i:
                    for e in range(RING):
                        gelu(e, i)
                sc.wait_ge(route_dve, 1)
                f = r_e[:, 2, :]
                sc.activation(f, f, ACT.Exp).then_inc(route_act, 1)
                with sc.Fori(10, 15) as i:
                    for e in range(RING):
                        gelu(e, i)
                sc.wait_ge(route_ready, 1)
                with sc.Fori(15, NE1 // RING) as i:
                    for e in range(RING):
                        gelu(e, i)
                for e in range(NE1 // RING * RING, NE1):
                    gelu(e)
                sc.wait_ge(strip_done, AT[LASTS[5]] + 1)
                sc.activation(xn[:, 1, :], ps[:, 2:4, :].rearrange("p a b -> p (a b)"),
                              ACT.Copy).then_inc(yT_out, 1)

            for n, body in enumerate([even, lambda: mlp(0, "mlp0"), odd, lambda: mlp(1, "mlp1"), mix,
                                      peer][:STAGES]):
                norm(n)
                body()

        @block.vector
        def _(ve):
            ch = Chain(ve, dve_chain)

            def tt(o, a, b, op):
                return ve.tensor_tensor(o, a, b, op)

            def norm(i):
                if i:
                    ve.wait_ge(strip_done, AT[LASTS[i - 1]] + 1)
                    for a in range(NT):
                        ve.tensor_copy(x_s[:, a, :], ps[:, 2 * a:2 * a + 2, :].rearrange(
                            "p a b -> p (a b)")).then_inc(x_ready, 1)
                    ve.wait_ge(x_ready, NT * i)
                else:
                    small_wait(ve, "x")
                    small_wait(ve, "const")
                    small_wait(ve, "param")
                ve.wait_ge(roots, i + 1)
                ch.link(ve.reciprocal(stat[:, 4:6], stat[:, 2:4]))
                ch.link(ve.tensor_scalar(xn[:, 0, :], x_s[:, 0, :], stat[:, 4:5], None, ALU.mult))
                ve.tensor_scalar(xn[:, 1, :], x_s[:, 1, :], stat[:, 5:6], None, ALU.mult).then_inc(xn_ready, 1)
                for c in range(1, KC // 2, 2):
                    ve.wait_ge(turned, 4 * i + c + 1)
                    for cc in range(2):
                        ve.tensor_scalar(hT[:, 2 * c + cc, :], ps[:, 7, cc * T:(cc + 1) * T],
                                         prm(NORMS[i], 2 * c + cc, 2 * c + cc + 1), None,
                                         ALU.mult).then_inc(hT_dve, 1)

            def bc(a, axis, shape):
                return a.unsqueeze(axis).broadcast_to(shape)

            def head_norm(t, qk, sq, rt, gains):
                tt(sq, qk, qk, ALU.mult).then_inc(sq_ready, 1)
                ve.wait_ge(rt_ready, t + 1)
                f = rt.rearrange("p a b -> p (a b)")
                ch.link(ve.reciprocal(f, f))
                for lo, hi, g in gains:
                    ins = ve.scalar_tensor_tensor(out=qk[:, lo:hi, :], in0=qk[:, lo:hi, :], scalar=g,
                                                  in1=rt[:, lo:hi, :], op0=ALU.mult, op1=ALU.mult)
                    if hi < qk.shape[1]:
                        ch.add(ins)
                ins.then_inc(qk_ready, 1)

            def softmax_in(t, S, sm, masks, sink):
                for n in range(NH):
                    ve.wait_ge(score_done, NH * t + n + 1)
                    lo, hi = masks(n)
                    ch.add(ve.scalar_tensor_tensor(out=S[:, n, 0:P], in0=ps[:, n % 4, 0:P],
                                                   scalar=HD ** -0.5, in1=lo, op0=ALU.mult, op1=ALU.add))
                    ve.scalar_tensor_tensor(out=S[:, n, P:3 * P], in0=ps[:, n % 4, P:3 * P],
                                            scalar=HD ** -0.5, in1=hi, op0=ALU.mult,
                                            op1=ALU.add).then_inc(score_out, 1)
                ve.wait_ge(score_out, NH * (t + 1))
                parts = ((S[:, :, 0:P], 0, P), (S[:, :, P:3 * P], NH, 2 * P))
                for s, at, w in parts:
                    ch.add(ve.tensor_reduce(sm[:, 0, at:at + NH], s, AX, ALU.max))
                ch.wait()
                if sink is not None:
                    m = sm[:, 0, :].rearrange("p (a h) -> p a h", a=2)
                    ch.link(tt(m, m, bc(sink, 1, [P, 2, NH]), ALU.max))
                    ch.add(tt(sm[:, 2, :].rearrange("p (a h) -> p a h", a=2),
                              bc(sink, 1, [P, 2, NH]), m, ALU.subtract))
                s, at, w = parts[0]
                ch.add(tt(s, s, bc(sm[:, 0, at:at + NH], 2, [P, NH, w]), ALU.subtract))
                s, at, w = parts[1]
                tt(s, s, bc(sm[:, 0, at:at + NH], 2, [P, NH, w]), ALU.subtract).then_inc(shifted, 1)

            def softmax_out(t, S, sm, count, sink):
                ve.wait_ge(exp_done, t + 1)
                if count is not None:
                    ch.link(tt(S, S, bc(count, 1, [P, NH, 3 * P]), ALU.mult))
                parts = ((S[:, :, 0:P], 0, P), (S[:, :, P:3 * P], NH, 2 * P))
                for s, at, w in parts:
                    ch.add(ve.tensor_reduce(sm[:, 1, at:at + NH], s, AX, ALU.add))
                ch.wait()
                if sink:
                    ch.link(tt(sm[:, 1, :], sm[:, 1, :], sm[:, 2, :], ALU.add))
                ch.link(ve.reciprocal(sm[:, 3, :], sm[:, 1, :]))
                for s, at, w in parts:
                    ins = tt(s, s, bc(sm[:, 3, at:at + NH], 2, [P, NH, w]), ALU.mult)
                    if at == 0:
                        ch.add(ins)
                ins.then_inc(probs, 1)

            def even():
                small_wait(ve, "ssm")
                p = lambda n: e_p[:, n, :]
                ve.wait_ge(prm_act, 1)
                ch.add(tt(p(2), prm("a_im"), p(0), ALU.mult))
                tt(p(1), prm("a_re"), p(0), ALU.mult).then_inc(prm_dve, 1)
                ve.wait_ge(prm_dve, 1)
                ch.link(ve.tensor_scalar(p(4), p(2), INV_2PI, None, ALU.mult))
                ch.link(ve.tensor_scalar(p(4), p(4), ROUND, None, ALU.add))
                ch.link(ve.tensor_scalar(p(4), p(4), -ROUND, None, ALU.add))
                ch.link(ve.scalar_tensor_tensor(out=p(5), in0=p(4), scalar=-C1, in1=p(2), op0=ALU.mult, op1=ALU.add))
                ch.link(ve.scalar_tensor_tensor(out=p(5), in0=p(4), scalar=-C2, in1=p(5), op0=ALU.mult, op1=ALU.add))
                ch.add(ve.tensor_scalar(p(6), p(5), PI_LO, -PI_LO, ALU.min, ALU.max))
                ch.link(ve.tensor_scalar(p(7), p(5), TWO_PI / 4, None, ALU.add))
                ch.link(ve.tensor_scalar(p(8), p(7), TWO_PI / 2, -TWO_PI, ALU.is_gt, ALU.mult))
                ch.link(tt(p(7), p(7), p(8), ALU.add))
                ve.tensor_scalar(p(7), p(7), PI_LO, -PI_LO, ALU.min, ALU.max).then_inc(prm_dve, 1)
                ve.wait_ge(prm_act, 4)
                ch.add(tt(p(11), p(3), p(10), ALU.mult))
                ch.add(tt(p(12), p(3), p(9), ALU.mult))
                ch.add(tt(p(15), prm("a_re"), prm("a_re"), ALU.mult))
                ch.link(tt(p(16), prm("a_im"), prm("a_im"), ALU.mult))
                ch.link(tt(p(15), p(15), p(16), ALU.add))
                ch.link(ve.reciprocal(p(15), p(15)))
                ch.link(ve.tensor_scalar(p(17), p(11), -1.0, None, ALU.add))
                ch.add(tt(p(13), p(17), prm("a_re"), ALU.mult))
                ch.add(tt(p(16), p(12), prm("a_im"), ALU.mult))
                ch.add(tt(p(14), p(12), prm("a_re"), ALU.mult))
                ch.link(tt(p(18), p(17), prm("a_im"), ALU.mult))
                ch.add(tt(p(13), p(13), p(16), ALU.add))
                ch.link(tt(p(14), p(14), p(18), ALU.subtract))
                ch.add(tt(p(13), p(13), p(15), ALU.mult))
                ch.link(tt(p(14), p(14), p(15), ALU.mult))
                wr, wi = (bc(p(n), 2, [P, SG, 32]) for n in (13, 14))
                cr, ci = e_C[:, 0], e_C[:, 1]
                ch.add(tt(e_CW[:, 0], cr, wr, ALU.mult))
                ch.link(tt(e_ctmp, ci, wi, ALU.mult))
                ch.link(tt(e_CW[:, 0], e_CW[:, 0], e_ctmp, ALU.subtract))
                ch.add(tt(e_CW[:, 1], cr, wi, ALU.mult))
                ch.link(tt(e_ctmp, ci, wr, ALU.mult))
                ve.scalar_tensor_tensor(out=e_CW[:, 1], in0=e_CW[:, 1], scalar=-1.0, in1=e_ctmp,
                                        op0=ALU.mult, op1=ALU.subtract).then_inc(cw_ready, 1)
                ch.add(ve.memset(e_cos[:, :, 0:1], 1.0))
                ch.add(ve.memset(e_sin[:, :, 0:1], 0.0))
                ch.add(ve.tensor_copy(p(19), p(10)))
                ch.link(ve.tensor_copy(p(20), p(9)))
                n = 1
                while n < T:
                    bcos, bsin = bc(p(19), 2, [P, SG, n]), bc(p(20), 2, [P, SG, n])
                    t0 = e_tmp[:, 0, 0:SG * n].rearrange("p (a b) -> p a b", a=SG)
                    t1 = e_tmp[:, 1, 0:SG * n].rearrange("p (a b) -> p a b", a=SG)
                    old_c, old_s = e_cos[:, :, 0:n], e_sin[:, :, 0:n]
                    new_c, new_s = e_cos[:, :, n:2 * n], e_sin[:, :, n:2 * n]
                    ch.add(tt(t0, old_s, bsin, ALU.mult))
                    ch.add(tt(t1, old_s, bcos, ALU.mult))
                    ch.add(tt(new_c, old_c, bcos, ALU.mult))
                    ch.add(tt(new_s, old_c, bsin, ALU.mult))
                    ch.add(tt(p(21), p(19), p(19), ALU.mult))
                    ch.add(tt(p(22), p(20), p(20), ALU.mult))
                    ch.link(tt(p(23), p(19), p(20), ALU.mult))
                    ch.add(tt(new_c, new_c, t0, ALU.subtract))
                    ch.add(tt(new_s, new_s, t1, ALU.add))
                    ch.add(tt(p(19), p(21), p(22), ALU.subtract))
                    ch.link(ve.tensor_scalar(p(20), p(23), 2.0, None, ALU.mult))
                    n *= 2
                ve.wait_ge(evac, 9)
                head_norm(0, e_qk, e_sq, e_rt, [(0, 4, prm("q_norm")), (4, 5, prm("k_norm"))])

                def ssm(c):
                    ve.wait_ge(bu_done, c + 1)
                    if c >= 4:
                        ve.wait_ge(back, c - 3)
                    src = ps[:, 6 + c % 2, :].rearrange("p (a b) -> p a b", a=2)
                    zt0 = e_zt[:, 0, :].rearrange("p (a b) -> p a b", a=2)
                    zt1 = e_zt[:, 1, :].rearrange("p (a b) -> p a b", a=2)
                    ch.add(tt(zt0, src, bc(e_cos[:, c, :], 1, [P, 2, T]), ALU.mult))
                    tt(zt1, src, bc(e_sin[:, c, :], 1, [P, 2, T]), ALU.mult).then_inc(bu_used, 1)
                    ve.wait_ge(bu_used, c + 1)
                    z = e_z[:, c % 4]
                    ch.add(tt(z[:, 0, :], zt0[:, 0, :], zt1[:, 1, :], ALU.add))
                    ch.link(tt(z[:, 1, :], zt0[:, 1, :], zt1[:, 0, :], ALU.subtract))
                    m = e_p[:, 3, c:c + 1].broadcast_to([P, T])
                    ch.add(ve.tensor_tensor_scan(z[:, 0, :], m, z[:, 0, :], 0.0, ALU.mult, ALU.add))
                    ve.tensor_tensor_scan(z[:, 1, :], m, z[:, 1, :], 0.0, ALU.mult, ALU.add).then_inc(scanned, 1)

                def y(j):
                    ve.wait_ge(y_done, 4 * j + 4)
                    ve.scalar_tensor_tensor(out=e_y[:, j, :], in0=e_uT[:, j, :], scalar=prm("ssm_d", j, j + 1),
                                            in1=ps[:, 4 + j % 2, 0:T], op0=ALU.mult,
                                            op1=ALU.add).then_inc(y_sum, 1)

                ssm(0)
                ssm(1)
                mask = k("window_mask")
                softmax_in(0, e_S, e_sm, lambda n: (mask[:, 0:P], mask[:, P:3 * P]), prm("sinks"))
                for c in range(2, 6):
                    ssm(c)
                softmax_out(0, e_S, e_sm, None, True)
                for c in range(6, SG):
                    ssm(c)
                    if c % 4 == 0 and c >= 8:
                        y(c // 4 - 2)
                y(2)
                y(3)
                ve.wait_ge(glu_sig, 4)
                tt(e_mixT[:, 4:8, :], e_y, e_sq[:, 0:4, :], ALU.mult).then_inc(glu_out, 1)

            def mlp(n, name):
                base = AT[(name, "gate", 0)]

                def combine(strip, c, i=None):
                    ve.wait_ge(strip_done, strip + 1 if i is None else 6 * i + (strip + 1))
                    ve.wait_ge(silu_ready, (FC * n + c + 1) if i is None else 2 * i + (FC * n + c + 1))
                    tt(f_act[:, c % 2, :], f_silu[:, c % 2, :], ps[:, 6 + c % 2, 0:T],
                       ALU.mult).then_inc(ff_ready, 1)

                combine(base + 1, 0)
                with ve.Fori(0, (FC - 2) // 2) as i:
                    combine(base + 3, 1, i)
                    combine(base + 6, 2, i)
                combine(base + 3 + 3 * (FC - 2), FC - 1)

            def odd():
                def softplus(h):
                    ve.wait_ge(z_log, h + 1)
                    if h >= 4:
                        ve.wait_ge(cum_done, h - 3)
                    ve.scalar_tensor_tensor(out=o_sp[:, h % 4, :], in0=ps[:, h % 4, 0:3 * P], scalar=0.0,
                                            in1=o_t[:, h % 2, :], op0=ALU.max,
                                            op1=ALU.add).then_inc(sp_ready, 1)

                def weights(h):
                    ve.wait_ge(cum_done, h + 1)
                    if h >= 4:
                        ve.wait_ge(w_ready, h - 3)
                    tt(o_w0[:, h % 4, :], ps[:, h % 4, 0:3 * P], k("strict_mask"),
                       ALU.add).then_inc(w_masked, 1)

                for j in range(9):
                    if j >= 1:
                        weights(2 * j - 2)
                        weights(2 * j - 1)
                    if j < 8:
                        softplus(2 * j)
                        softplus(2 * j + 1)

            def mix():
                r = m_row[0:MH]
                ch.add(ve.memset(r[:, 9, :], 1.0))
                ch.link(ve.memset(m_up[:, :, 0:3], 0.0))
                ve.wait_ge(gate_act, 1)
                ch.link(ve.scalar_tensor_tensor(out=r[:, 1, :], in0=r[:, 1, :], scalar=0.0, in1=r[:, 2, :],
                                                op0=ALU.min, op1=ALU.subtract))
                for a in range(NT):
                    ch.add(ve.tensor_tensor_scan(r[:, 6, a * P:(a + 1) * P], r[:, 9, a * P:(a + 1) * P],
                                                 r[:, 1, a * P:(a + 1) * P], 0.0, ALU.mult, ALU.add))
                ch.wait()
                ch.link(tt(r[:, 3, :], r[:, 0, :], r[:, 6, :], ALU.subtract))
                ch.link(ve.tensor_tensor_scan(r[:, 8, 0:P], r[:, 3, 0:P], r[:, 3, 0:P], 0.0, ALU.max, ALU.max))
                ch.link(tt(r[:, 2, 0:1], r[:, 6, P - 1:P], r[:, 8, P - 1:P], ALU.add))
                ch.link(ve.tensor_tensor_scan(r[:, 8, P:T], r[:, 3, P:T], r[:, 3, P:T], r[:, 2, 0:1],
                                              ALU.max, ALU.max))
                ch.add(ve.tensor_scalar(r[:, 4, :], r[:, 8, :], -1.0, None, ALU.mult))
                ch.add(tt(r[:, 5, :], r[:, 6, :], r[:, 8, :], ALU.add))
                ve.tensor_scalar(r[:, 7, 0:P], r[:, 3, 0:P], r[:, 6, P - 1:P], None,
                                 ALU.add).then_inc(rows_ready, 1)
                for j in range(4):
                    ve.wait_ge(evac, GATE_EVAC + 1 + j + 1)
                    cw = lambda i: prm("conv_w", 4 * j + i, 4 * j + i + 1)
                    o = m_cv[:, j, :]
                    ch.link(ve.tensor_scalar(o, m_up[:, j, 0:T], cw(0), prm("conv_b", j, j + 1),
                                             ALU.mult, ALU.add))
                    for i in range(1, 4):
                        ins = ve.scalar_tensor_tensor(out=o, in0=m_up[:, j, i:T + i], scalar=cw(i), in1=o,
                                                      op0=ALU.mult, op1=ALU.add)
                        if i < 3:
                            ch.link(ins)
                    ins.then_inc(conv_done, 1)
                for h in range(MH):
                    ve.wait_ge(bcast_done, h + 1)
                    x = m_x[:, h, :]
                    ch.add(tt(x[:, 0:T], ps[:, h, 0:T], k("causal_mask", 0, T), ALU.add))
                    tt(x[:, T:3 * P], ps[:, h, P:T], k("causal_mask", T, 3 * P), ALU.add).then_inc(expo_in, 1)
                for h in range(MH):
                    decay(h)
                small_wait(ve, "mix")
                ch.add(tt(m_bias, m_bias, bc(k("dilated_mask", P, 3 * P), 1, [P, NH, T]), ALU.add))
                head_norm(1, m_qk, m_sq, m_rt,
                          [(j, j + 1, prm("qn" if j < 4 else "kn", j % 4, j % 4 + 1)) for j in range(8)])
                f = lambda a: a.rearrange("p a b -> p (a b)")
                ve.wait_ge(den_abs, MH)
                ve.wait_ge(em_out, MH)
                ch.link(tt(f(m_dn), f(m_dn), f(m_em), ALU.max))
                ch.link(ve.reciprocal(f(m_dn), f(m_dn)))
                ch.link(tt(m_hm, ps[:, 0:MH, 0:T], m_dn, ALU.mult))
                tt(f(m_dn), f(m_hm), f(m_hm), ALU.mult).then_inc(hm_sq, 1)
                for h in range(MH):
                    ch.add(ve.tensor_scalar(m_cs[:, h, :], m_cT[:, h, :], prm("skip", h, h + 1), None, ALU.mult))
                ve.wait_ge(hm_rt, 1)
                ch.link(ve.reciprocal(f(m_dn), f(m_dn)))
                ch.link(tt(f(m_hm), f(m_hm), f(m_dn), ALU.mult))
                for h in range(MH):
                    ch.add(ve.scalar_tensor_tensor(out=m_hm[:, h, :], in0=m_hm[:, h, :],
                                                   scalar=prm("mh_norm", h, h + 1), in1=m_cs[:, h, :],
                                                   op0=ALU.mult, op1=ALU.add))
                ch.wait()
                ve.wait_ge(evac, GATE_EVAC + 1 + 24)
                tt(m_mixT[:, 0:4, :], m_hm, m_sz, ALU.mult).then_inc(ym_ready, 1)
                softmax_in(1, m_S, m_sm, lambda n: (m_bias[:, n, P:T], m_bias[:, n, :]), None)
                softmax_out(1, m_S, m_sm, k("dilated_count"), False)

            def decay(h):
                ve.wait_ge(st_done, h + 1)
                ve.wait_ge(expo_out, h + 1)
                tt(m_s[:, h, :], ps[:, 6 + h % 2, 0:3 * P], m_d[:, h, :], ALU.mult).then_inc(s_ready, 1)

            def peer():
                def top16(v, i, row, used=None):
                    ch.link(ve.max(v[:, 0:8], row))
                    ch.link(ve.max_index(i[:, 0:8], v[:, 0:8], row))
                    ch.link(ve.match_replace(out=row, in_to_replace=v[:, 0:8], in_values=row, imm_value=-3e38))
                    ch.link(ve.max(v[:, 8:16], row))
                    ins = ve.max_index(i[:, 8:16], v[:, 8:16], row)
                    if used is None:
                        ch.link(ins)
                    else:
                        ins.then_inc(used, 1)

                iu, icu = r_i.bitcast(U32), r_ic.bitcast(U32)
                for s in range(2 * PH):
                    ve.wait_ge(key_out, s + 1)
                    for a in range(NT):
                        top16(r_v[:, a, s, :], iu[:, a, s, :], r_sc[:, s % 4, a, :],
                              key_used if a == NT - 1 else None)
                    if s % 2:
                        h = s // 2
                        for a in range(NT):
                            ch.link(tt(r_c[:, a, :].rearrange("p (a b) -> p a b", a=TOPK),
                                       bc(r_v[:, a, s - 1, :], 2, [P, TOPK, TOPK]),
                                       bc(r_v[:, a, s, :], 1, [P, TOPK, TOPK]), ALU.add))
                            top16(r_vc[:, a, h, :], icu[:, a, h, :], r_c[:, a, :])
                n = NT * PH
                g = r_e[:, 2, :].rearrange("p (a b) -> p a b", b=TOPK)
                vc = r_vc.rearrange("p a h b -> p (a h) b")
                tt(g, vc, vc[:, :, 0:1].broadcast_to([P, n, TOPK]), ALU.subtract).then_inc(route_dve, 1)
                ic = icu.rearrange("p a h b -> p (a h b)")
                hl = r_hl.bitcast(U32)
                ch.add(ve.tensor_scalar(hl[:, 0, :], ic, 4, None, ALU.logical_shift_right))
                ch.add(ve.tensor_scalar(hl[:, 1, :], ic, 15, None, ALU.bitwise_and))
                ch.link(ve.tensor_copy(r_if.rearrange("p a s b -> p (a s b)"),
                                       iu.rearrange("p a s b -> p (a s b)")))
                ch.link(ve.tensor_copy(r_hlf.rearrange("p a b -> p (a b)"), hl.rearrange("p a b -> p (a b)")))
                big = [P, PH, TOPK, TOPK]
                tmp = xn[:, :, :].rearrange("p a b -> p (a b)").rearrange(
                    "p (h k i) -> p h k i", h=PH, k=TOPK)
                iota16 = k("iota", 0, TOPK).unsqueeze(1).unsqueeze(1).broadcast_to(big)
                for a in range(NT):
                    for part in range(2):
                        at = r_hlf[:, part, a * P:(a + 1) * P].rearrange("p (h k) -> p h k", h=PH)
                        keys = r_if[:, a, part:2 * PH:2, :]
                        ch.link(tt(tmp, at.unsqueeze(3).broadcast_to(big), iota16, ALU.is_equal))
                        ch.link(tt(tmp, tmp, keys.unsqueeze(2).broadcast_to(big), ALU.mult))
                        ch.link(ve.tensor_reduce(
                            r_e[:, part, a * P:(a + 1) * P].rearrange("p (h k) -> p h k", h=PH), tmp, AX,
                            ALU.add))
                ve.wait_ge(route_act, 1)
                s = r_sum[:, 0, :]
                ch.link(ve.tensor_reduce(s, g, AX, ALU.add))
                ch.link(ve.reciprocal(s, s))
                ch.link(tt(g, g, bc(s, 2, [P, n, TOPK]), ALU.mult))
                ve.tensor_copy(xn[:, 0, 0:3 * T], r_e.rearrange("p a b -> p (a b)")).then_inc(route_ready, 1)
                ve.wait_ge(eT_done, 1)
                ve.tensor_copy(eT[:, 0:2, :], ps[:, 6, :].rearrange("p (a b) -> p a b", a=2)).then_inc(gate_free, 1)
                ve.tensor_copy(eT[:, 2, :], ps[:, 7, 0:T]).then_inc(gate_free, 1)
                ve.wait_ge(gate_free, 2)
                ve.wait_ge(gelu_done, NE1)

                def one_hot(g, i):
                    for q in range(4):
                        col = bass.ds(8 * i + (4 * g + q), 1)
                        ve.tensor_scalar(oh[:, 0, 4 * g + q, :], k("iota"), eT[:, 0, col], None,
                                         ALU.is_equal)
                        ins = ve.tensor_scalar(oh[:, 1, 4 * g + q, :], k("iota"), eT[:, 1, col], eT[:, 2, col],
                                               ALU.is_equal, ALU.mult)
                    ins.then_inc(onehot_ready, 1)

                with ve.Fori(0, T // 8) as i:
                    for g in range(2):
                        one_hot(g, i)
                    for g in range(2):
                        ve.wait_ge(spread, 2 * i + (g + 1))
                        part = act[:, :, bass.ds(8 * i + 4 * g, 4)]
                        tt(part, part, ps[:, 4 + 2 * g, :].rearrange("p (q e) -> p e q", q=4),
                           ALU.mult).then_inc(gate_free, 1)
                ve.wait_ge(strip_done, AT[LASTS[5]] + 1)
                ve.tensor_copy(xn[:, 0, :], ps[:, 0:2, :].rearrange("p a b -> p (a b)")).then_inc(yT_out, 1)
                ve.wait_ge(out_turned, 1)
                for a in range(NT):
                    ve.tensor_copy(x_s[:, a, :], ps[:, 4 + 2 * a:6 + 2 * a, :].rearrange(
                        "p a b -> p (a b)")).then_inc(x_ready, 1)

            for n, body in enumerate([even, lambda: mlp(0, "mlp0"), odd, lambda: mlp(1, "mlp1"), mix,
                                      peer][:STAGES]):
                norm(n)
                body()
            if STAGES < 6:
                ve.wait_ge(strip_done, n_strips)
                for a in range(2):
                    ve.tensor_copy(x_s[:, a, :],
                               ps[:, 2*a:2*a+2, :].rearrange("p a b -> p (a b)")).then_inc(x_ready, 1)

        @block.gpsimd
        def _(po):
            ch = Chain(po, pool_chain)
            small_load(po, "ssm", e_B.rearrange("p a b c -> p (a b c)"), A["ssm_b"])
            small_load(po, "ssm", e_C.rearrange("p a b c -> p (a b c)"), A["ssm_c"])
            small_load(po, "keys", keys_s.rearrange("p a b -> p (a b)"), A["keys"])
            for c in range(SG):
                po.wait_ge(scanned, c + 1)
                z = e_z[:, c % 4]
                h0 = e_ht[:, 0, :].rearrange("p (a b) -> p a b", a=2)
                h1 = e_ht[:, 1, :].rearrange("p (a b) -> p a b", a=2)
                ch.add(po.tensor_tensor(h0, z, e_cos[:, c, :].unsqueeze(1).broadcast_to([P, 2, T]), ALU.mult))
                ch.link(po.tensor_tensor(h1, z, e_sin[:, c, :].unsqueeze(1).broadcast_to([P, 2, T]), ALU.mult))
                if c >= 4:
                    po.wait_ge(y_done, c - 3)
                h = e_h[:, c % 4]
                ch.add(po.tensor_tensor(h[:, 0, :], h0[:, 0, :], h1[:, 1, :], ALU.subtract))
                po.tensor_tensor(h[:, 1, :], h0[:, 1, :], h1[:, 0, :], ALU.add).then_inc(back, 1)
                po.wait_ge(back, c + 1)
            if STAGES >= 3:
                for h in range(2 * NH):
                    po.wait_ge(sp_ready, h + 1)
                    v = o_sp[:, h % 4, :].rearrange("p (b c) -> p b c", c=P)[:, 0:3:2, :]
                    po.affine_select(out=v, in_=v, compare_op=ALU.is_gt, fill=0.0, base=0,
                                     pattern=[[0, 2], [1, P]], channel_multiplier=-1).then_inc(sp_masked, 1)
            if STAGES >= 5:
                po.wait_ge(x_ready, NT * 3)
                small_load(po, "mix", m_bias.rearrange("p a b -> p (a b)"), A["rel"])
                small_load(po, "mix", m_wqk.rearrange("p a b c -> p (a b c)"), A["wqk"])


def _constants():
    c = np.zeros((P, N_CONST), np.float32)

    def put(name, v):
        c[:v.shape[0], CONST[name][0]:CONST[name][1]] = v

    i, j = np.arange(P)[:, None], np.arange(P)[None, :]
    put("ident", np.eye(P))
    put("ones", np.ones((P, P)))
    put("head_ones", (i // HD == j // HD) * 1.0)
    put("neg_tri", (i >= j) * -1.0)
    put("neg_ones", -np.ones((P, P)))
    put("iota", np.broadcast_to(j, (P, P)))
    free = np.zeros((P, P))
    strict, causal = np.where(i < j, 0.0, -BIG), np.where(i <= j, 0.0, -BIG)
    put("strict_mask", np.concatenate([strict, free, strict], 1))
    put("causal_mask", np.concatenate([causal, free, causal], 1))
    dist = np.concatenate([i - j, i - j + P, i - j], 1)
    put("window_mask", np.where((dist >= 0) & (dist < 128), 0.0, -BIG))
    count = sum(((dist >= 0) & (dist % dil == 0) & (dist // dil <= win // dil)).astype(np.float32)
                for win, dil in ((128, 1), (512, 4), (2048, 16)))
    put("dilated_count", count)
    put("dilated_mask", np.where(count > 0, 0.0, -BIG))
    put("head_row", np.repeat(np.eye(MH), P, axis=1))
    put("eps", np.full((P, 1), EPS))
    return c


def _buckets():
    d = np.arange(T)
    large = 16 + (np.log(np.maximum(d, 1).astype(np.float32) / np.float32(16))
                  / np.float32(np.log(2048 / 16)) * 16).astype(np.int32)
    return np.where(d < 16, d, np.minimum(large, 31))


def _layout(v):
    f = {n: np.asarray(a) for n, a in v.items()}
    strips = np.empty((NS, P, D), np.float32)

    def cols(w, at, rows=D):
        w = w[:, at]
        return w.reshape(rows // P, P, w.shape[1]).transpose(1, 0, 2).reshape(P, -1)

    def put(name, w):
        strips[AT[name]] = w

    ar = np.arange
    w = f["even_w_in"][0]
    for j in range(4):
        put(("even", "u", j), cols(w, 768 + P * j + ar(P)))
        put(("even", "q", j), cols(w, np.concatenate([HD * j + ar(HD), HD * (j + 4) + ar(HD)])))
    put(("even", "k", 0), cols(w, 512 + ar(P)))
    put(("even", "v", 0), cols(w, 640 + ar(P)))
    for j in range(2):
        put(("even", "glu", j), cols(f["ssm_w_glu"][0], 256 * j + ar(256), 512))
    w = f["even_w_out"][0]
    for j in range(8):
        rows = np.concatenate([HD * j + ar(HD), HD * (j + 4) + ar(HD)]) if j < 4 else P * j + ar(P)
        put(("even", "out", j), w[rows])
        put(("odd", "out", j), f["odd_w_out"][0][P * j:P * j + P])
        put(("mix", "out", j), f["w_out_2"][0][P * j:P * j + P])
    for n in range(2):
        for c in range(FC):
            put((f"mlp{n}", "gate", c), cols(f["ffn_w_gate"][n], P * c + ar(P)))
            put((f"mlp{n}", "up", c), cols(f["ffn_w_up"][n], P * c + ar(P)))
            put((f"mlp{n}", "down", c), f["ffn_w_down"][n][P * c:P * c + P])
    for j in range(8):
        for n, part in enumerate("qkv"):
            put(("odd", part, j), cols(f["odd_w_in"][0], D * n + P * j + ar(P)))
    w = f["w_in_2"][0]
    at = {"u": 0, "vm": 512, "z": 1024, "qa": 1544, "ka": 2056, "va": 2568}
    for part, first in at.items():
        for j in range(4):
            put(("mix", part, j), cols(w, first + P * j + ar(P)))
    gates = np.zeros((P, KC, P), np.float32)
    gates[:, :, 0:2 * MH] = cols(w, 1536 + ar(2 * MH)).reshape(P, KC, 2 * MH)
    put(("mix", "if", 0), gates.reshape(P, D))
    for s in range(2 * PH):
        put(("peer", "q", s), cols(f["w_query_2"][0], P * s + ar(P)))
    u = f["expert_u_2"][0].reshape(NE1, P, KC, P)
    first = AT[("peer", "u", 0)]
    strips[first:first + NE1] = u.transpose(0, 3, 2, 1).reshape(NE1, P, D)
    first = AT[("peer", "v", 0)]
    strips[first:first + NE1] = f["expert_v_2"][0].reshape(NE1, P, D)

    param = np.zeros((P, N_PARAM), np.float32)

    def prm(name, w):
        param[:w.shape[0], PARAM[name][0]:PARAM[name][1]] = w

    chunks = lambda a: a.reshape(-1, P).T
    for name, a in (("even_norm", f["even_norm"][0]), ("mlp0_norm", f["ffn_norm"][0]),
                    ("odd_norm", f["odd_norm"][0]), ("mlp1_norm", f["ffn_norm"][1]),
                    ("mix_norm", f["norm1_g_2"][0]), ("peer_norm", f["norm2_g_2"][0]),
                    ("ssm_d", f["ssm_d"][0]), ("b_glu", f["ssm_b_glu"][0]),
                    ("conv_b", f["conv_b_2"][0]), ("mh_norm", f["mh_norm_g_2"][0].reshape(-1)),
                    ("skip", f["skip_m_2"][0].reshape(-1)), ("qn", f["qn_g_2"][0].reshape(-1)),
                    ("kn", f["kn_g_2"][0].reshape(-1)), ("a_re", f["ssm_a_re"][0].reshape(-1)),
                    ("a_im", f["ssm_a_im"][0].reshape(-1)),
                    ("log_dt", np.repeat(f["ssm_log_dt"][0], HD))):
        prm(name, chunks(a))
    prm("q_norm", np.tile(f["q_norm"][0], 2)[:, None])
    prm("k_norm", np.tile(f["k_norm"][0], 2)[:, None])
    order = [n // 2 + 4 * (n % 2) for n in range(NH)]
    prm("sinks", np.broadcast_to(f["sinks"][0][order], (P, NH)))
    prm("conv_w", f["conv_w_2"][0].reshape(4, 4, P).transpose(2, 1, 0).reshape(P, 16))
    prm("ig_b", f["ig_b_2"][0][:, None])
    prm("fg_b", f["fg_b_2"][0][:, None])

    ssm_b = np.zeros((4, 2, 16, 2, 4, 2, HD), np.float32)
    ssm_c = np.zeros((2, HD, 2, SG, 2, 16), np.float32)
    for part, (b, c) in enumerate((("ssm_b_re", "ssm_c_re"), ("ssm_b_im", "ssm_c_im"))):
        bb = f[b][0].reshape(4, 4, 2, HD, 16)
        cc = f[c][0].reshape(SG, 2, 16, HD)
        for g in range(2):
            ssm_b[:, g, :, part, :, g, :] = bb[:, :, g].transpose(1, 3, 0, 2)
            ssm_c[g, :, part, :, g, :] = cc[:, g].transpose(2, 0, 1)
    keys = np.stack([f[f"sub_keys{n}_2"][0].transpose(2, 0, 1).reshape(P, D) for n in (1, 2)], 1)
    wqk = np.stack([f[n][0].transpose(1, 0, 2) for n in ("wq_m_2", "wk_m_2")], 1)
    dist = np.arange(P)[:, None] + P - np.arange(T)[None, :]
    rel = f["rel_bias_2"][_buckets()[np.abs(dist) % T]].transpose(0, 2, 1)
    return {"strips": strips, "const": _constants(), "param": param, "ssm_b": ssm_b.reshape(P, D),
            "ssm_c": ssm_c.reshape(P, D), "keys": keys.reshape(P, 2 * D), "wqk": wqk.reshape(P, D),
            "rel": np.ascontiguousarray(rel).reshape(P, NH * T), "x": f["x"]}


def kernel(**inputs):
    import concourse.bacc as bacc
    from concourse.bass_utils import run_bass_kernel_spmd

    arrays = {f"in_{n}": np.ascontiguousarray(a) for n, a in _layout(inputs).items()}
    nc = bacc.Bacc("TRN2", target_bir_lowering=False, num_devices=1)
    A = {n[3:]: nc.dram_tensor(n, a.shape, F32, kind="ExternalInput").ap() for n, a in arrays.items()}
    out = nc.dram_tensor("out", (1, T, D), F32, kind="ExternalOutput").ap()
    build(nc, A, out)
    return run_bass_kernel_spmd(nc, [arrays], core_ids=[0]).results[0]["out"]
```

```python
from contextlib import ExitStack

import numpy as np

import concourse.bass as bass
from concourse import mybir

P = 128
D = 1024
T = 256
NT = T // P
KC = D // P
RING = 3
UNROLL = 2 * RING
FC = 2816 // P
HD = 64
SG = 16
NH = 8
MH = 4
PH = 8
TOPK = 16
FREE_TILES = 78
NE1 = 128
HALF = NE1 // 2
EPS = 1e-6
BIG = 1e30

F32 = mybir.dt.float32
F32R = mybir.dt.float32r
BF16 = mybir.dt.bfloat16
U32 = mybir.dt.uint32
ALU = mybir.AluOpType
ACT = mybir.ActivationFunctionType
AX = mybir.AxisListType.X

TWO_PI = 6.283185307179586
INV_2PI = 0.15915494309189535
C1 = 6.28125
C2 = TWO_PI - C1
ROUND = 12582912.0
PI_LO = 3.1415925
STAGES = 6

NORMS = ["even_norm", "mlp0_norm", "odd_norm", "mlp1_norm", "mix_norm", "peer_norm"]
LASTS = [("even", "out", 7), ("mlp0", "down", FC - 1), ("odd", "out", 7), ("mlp1", "down", FC - 1),
         ("mix", "out", 7), ("peer", "v", NE1 - 1)]
STAGE_OF = {"mlp0": 1, "mlp1": 3}
EVEN_HEADS = [(n // 2, n % 2, 4, HD * (n % 2)) for n in range(NH)]
MIX_HEADS = [(n // 2, n % 2, 4 + n // 2, HD * n) for n in range(NH)]
EXP_AT = 6
FG_AT = 32
GATE_EVAC = 10 + 20
SMALL = ["x", "const", "param", "ssm", "keys", "mix"]
SMALL_N = {"x": 1, "const": 1, "param": 1, "ssm": 2, "keys": 1, "mix": 2}


def strip_names():
    names = []

    def mlp(n):
        names.extend([(n, "gate", 0), (n, "up", 0)])
        for c in range(1, FC):
            names.extend([(n, "gate", c), (n, "up", c), (n, "down", c - 1)])
        names.append((n, "down", FC - 1))

    names += [("even", "u", j) for j in range(4)] + [("even", "k", 0)]
    names += [("even", "q", j) for j in range(4)] + [("even", "v", 0)]
    names += [("even", "glu", j) for j in range(2)] + [("even", "out", j) for j in range(8)]
    mlp("mlp0")
    names += [("odd", "v", j) for j in range(8)]
    for j in range(8):
        names += [("odd", "q", j), ("odd", "k", j)]
    names += [("odd", "out", j) for j in range(8)]
    mlp("mlp1")
    names += [("mix", "if", 0)] + [("mix", "u", j) for j in range(4)]
    names += [("mix", "vm", j) for j in range(4)]
    names += [("mix", n, j) for n in ("qa", "ka", "va", "z") for j in range(4)]
    names += [("mix", "out", j) for j in range(8)]
    names += [("peer", "q", j) for j in range(2 * PH)]
    names += [("peer", "u", e) for e in range(NE1)] + [("peer", "v", e) for e in range(NE1)]
    return names


STRIPS = strip_names()
AT = {name: n for n, name in enumerate(STRIPS)}
NS = len(STRIPS)

CONST = {}
PARAM = {}


def _columns(table, widths):
    at = 0
    for name, width in widths:
        table[name] = (at, at + width)
        at += width
    return at


N_CONST = _columns(CONST, [
    ("ident", P), ("ones", P), ("head_ones", P), ("neg_tri", P), ("neg_ones", P), ("iota", P),
    ("window_mask", 3 * P), ("strict_mask", 3 * P), ("causal_mask", 3 * P), ("dilated_mask", 3 * P),
    ("dilated_count", 3 * P), ("head_row", MH * P), ("eps", 1), ("tokens", 0)])
N_PARAM = _columns(PARAM, [
    ("even_norm", KC), ("mlp0_norm", KC), ("odd_norm", KC), ("mlp1_norm", KC), ("mix_norm", KC),
    ("peer_norm", KC), ("q_norm", 1), ("k_norm", 1), ("sinks", NH), ("a_re", SG), ("a_im", SG),
    ("log_dt", SG), ("ssm_d", 4), ("b_glu", 4), ("conv_w", 16), ("conv_b", 4), ("ig_b", 1),
    ("fg_b", 1), ("mh_norm", MH), ("skip", MH), ("qn", 4), ("kn", 4)])


def build(nc, A, out):
    with ExitStack() as ctx:
        def sb(name, shape, dt=F32):
            return ctx.enter_context(nc.sbuf_tensor(name, shape, dt))

        def sem(name):
            return ctx.enter_context(nc.semaphore(name))

        ring = sb("ring", [P, RING, D])
        w_hi = sb("w_hi", [P, RING, D], F32R)
        w_lo = sb("w_lo", [P, RING, D], F32R)
        x_s = sb("x_s", [P, NT, D])
        xn = sb("xn", [P, NT, D])
        hT_hi = sb("hT_hi", [P, KC, T], F32R)
        hT_lo = sb("hT_lo", [P, KC, T], F32R)
        a_hi = sb("a_hi", [P, 2, T], F32R)
        a_lo = sb("a_lo", [P, 2, T], F32R)
        const = sb("const", [P, N_CONST])
        param = sb("param", [P, N_PARAM])
        stat = sb("stat", [P, 8])
        key_at = sb("key_at", [P, 2, T], BF16)
        gate3 = sb("gate3", [P, T, 3], BF16)
        gate_rest = sb("gate_rest", [P, 2, T])
        iota_b = sb("iota_b", [P, P], BF16)
        ARENA = NE1 * T
        arena = sb("arena", [P, ARENA])
        ps = ctx.enter_context(nc.psum_tensor("ps", [P, 8, 512], F32))

        def k(name, a=0, b=None):
            lo, hi = CONST[name]
            return const[:, lo + a:(hi if b is None else lo + b)]

        def prm(name, a=0, b=None):
            lo, hi = PARAM[name]
            return param[:, lo + a:(hi if b is None else lo + b)]

        class Lay:

            def __init__(self, at=0):
                self.at = at

            def __call__(self, *shape):
                n = int(np.prod(shape))
                assert self.at + n <= ARENA, (self.at, n)
                v = arena[:, self.at:self.at + n]
                self.at += n
                if len(shape) == 2:
                    v = v.rearrange("p (a b) -> p a b", a=shape[0])
                if len(shape) == 3:
                    v = v.rearrange("p (a b c) -> p a b c", a=shape[0], b=shape[1])
                return v

        ident = k("ident")
        ones = k("ones")

        L = Lay()
        e_uT = L(4, T)
        e_qk = L(5, T)
        e_v = L(NT, P)
        e_B = L(2, 4, P)
        e_C = L(2, SG, 32)
        e_CW = L(2, SG, 32)
        e_ctmp = L(SG, 32)
        e_cos = L(SG, T)
        e_sin = L(SG, T)
        e_sq = L(5, T)
        e_rt = L(5, T)
        e_p = L(24, SG)
        e_z = L(4, 2, T)
        e_zt = L(2, 2 * T)
        e_ht = L(2, 2 * T)
        e_mark = L.at
        e_tmp = L(2, SG * P)
        L.at = e_mark
        e_h = L(4, 2, T)
        e_S = L(NH, 3 * P)
        e_PT = L(NH, 3 * P)
        e_sm = L(6, 2 * NH)
        e_y = L(4, T)
        e_mixT = L(KC, T)

        L = Lay()
        f_silu = L(2, T)
        f_act = L(2, T)

        L = Lay(2048)
        o_v = L(NT, D)
        o_qT = L(8, T)
        o_kT = L(8, T)
        o_t = L(2, 3 * P)
        o_sp = L(4, 3 * P)
        o_w0 = L(4, 3 * P)
        o_w = L(4, 3 * P)
        o_mixT = L(KC, T)

        L = Lay(1024)
        m_up = L(4, T + 3)
        m_x_at = L.at
        m_cv = L(4, T)
        m_cs = L(4, T)
        m_x = Lay(m_x_at)(MH, 3 * P)
        m_cT = L(4, T)
        m_sz = L(4, T)
        m_vm = L(NT, 512)
        m_va = L(NT, 512)
        m_qk = L(8, T)
        m_pT_at = L.at
        m_sq = L(8, T)
        m_rt = L(8, T)
        m_PT = Lay(m_pT_at)(NH, 3 * P)
        m_S = L(NH, 3 * P)
        m_bias = L(NH, T)
        m_wqk = L(2, MH, P)
        m_qm = L(MH, T)
        m_km = L(MH, T)
        m_row = L(10, T)
        m_rc = L(3, MH)
        m_d_at = L.at
        m_d = L(MH, 3 * P)
        m_hm = Lay(m_d_at)(MH, T)
        m_s = L(MH, 3 * P)
        m_em = L(MH, T)
        m_dn = L(MH, T)
        m_sm = L(6, 2 * NH)
        m_mixT = L(KC, T)

        act = arena[:, 0:NE1 * T].rearrange("p (e t) -> p e t", t=T)
        L = Lay(FREE_TILES * T)
        keys_s = L(2, D)
        r_q = L(2, T)
        r_sc = L(2 * PH, NT, P)
        r_v = L(NT, 2 * PH, TOPK)
        r_i = L(NT, 2 * PH, TOPK)
        r_if = L(NT, 2 * PH, TOPK)
        r_c = L(2, 256)
        r_vc = L(NT, PH, TOPK)
        r_ic = L(NT, PH, TOPK)
        r_hl = L(2, NT * PH * TOPK)
        r_hlf = L(2, NT * PH * TOPK)
        r_e = L(3, NT * PH * TOPK)
        r_sum = L(1, NT * PH)
        spare = xn[:, :, :].bitcast(BF16)
        oh_second = spare[:, :, 0:4 * P].rearrange("p g (t c) -> p g t c", c=P)
        oh_first = spare[:, :, 4 * P:4 * P + 4 * HALF].rearrange("p g (t c) -> p g t c", c=HALF)
        oh_gate = spare[:, :, 4 * P + 4 * HALF:4 * P + 16 * HALF].rearrange(
            "p g (t s c) -> p g t s c", s=3, c=HALF)

        strip_landed = [sem(f"strip_landed{i}") for i in range(RING)]
        strip_done = sem("strip_done")
        high_ready = sem("high_ready")
        low_ready = sem("low_ready")
        small_in = [sem(f"small_in{i}") for i in range(8)]
        squares = sem("squares")
        roots = sem("roots")
        xn_ready = sem("xn_ready")
        x_ready = sem("x_ready")
        turned = sem("turned")
        hT_high = sem("hT_high")
        hT_low = sem("hT_low")
        mix_high = sem("mix_high")
        mix_low = sem("mix_low")
        a_ready = sem("a_ready")
        a_high = sem("a_high")
        evac = sem("evac")
        silu_ready = sem("silu_ready")
        ff_ready = sem("ff_ready")
        prm_act = sem("prm_act")
        prm_dve = sem("prm_dve")
        cw_ready = sem("cw_ready")
        sq_ready = sem("sq_ready")
        sq_summed = sem("sq_summed")
        rt_ready = sem("rt_ready")
        qk_ready = sem("qk_ready")
        score_done = sem("score_done")
        score_out = sem("score_out")
        shifted = sem("shifted")
        exp_done = sem("exp_done")
        probs = sem("probs")
        pT_done = sem("pT_done")
        pT_out = sem("pT_out")
        pv_done = sem("pv_done")
        pv_out = sem("pv_out")
        bu_done = sem("bu_done")
        bu_used = sem("bu_used")
        scanned = sem("scanned")
        back = sem("back")
        y_done = sem("y_done")
        y_sum = sem("y_sum")
        y_gelu = sem("y_gelu")
        y_high = sem("y_high")
        y_low = sem("y_low")
        glu_sig = sem("glu_sig")
        glu_out = sem("glu_out")
        z_done = sem("z_done")
        z_log = sem("z_log")
        sp_ready = sem("sp_ready")
        sp_masked = sem("sp_masked")
        cum_done = sem("cum_done")
        w_masked = sem("w_masked")
        w_ready = sem("w_ready")
        ov_done = sem("ov_done")
        ov_out = sem("ov_out")
        gate_act = sem("gate_act")
        rows_ready = sem("rows_ready")
        cols_done = sem("cols_done")
        cols_out = sem("cols_out")
        conv_done = sem("conv_done")
        conv_silu = sem("conv_silu")
        qkm_done = sem("qkm_done")
        qkm_out = sem("qkm_out")
        bcast_done = sem("bcast_done")
        expo_in = sem("expo_in")
        expo_out = sem("expo_out")
        em_out = sem("em_out")
        st_done = sem("st_done")
        s_ready = sem("s_ready")
        num_done = sem("num_done")
        den_abs = sem("den_abs")
        hm_sq = sem("hm_sq")
        hm_summed = sem("hm_summed")
        hm_rt = sem("hm_rt")
        ym_ready = sem("ym_ready")
        key_done = sem("key_done")
        key_out = sem("key_out")
        route_dve = sem("route_dve")
        route_act = sem("route_act")
        route_ready = sem("route_ready")
        eT_done = sem("eT_done")
        gelu_done = sem("gelu_done")
        first_ready = sem("first_ready")
        onehot_ready = sem("onehot_ready")
        spread = sem("spread")
        gate_free = sem("gate_free")
        yT_out = sem("yT_out")
        out_turned = sem("out_turned")
        act_chain = sem("act_chain")
        dve_chain = sem("dve_chain")
        pool_chain = sem("pool_chain")
        out_done = sem("out_done")

        block = ctx.enter_context(nc.Block())

        class Chain:

            def __init__(self, eng, s):
                self.eng, self.s, self.n = eng, s, 0

            def add(self, ins):
                self.n += 1
                ins.then_inc(self.s, 1)

            def wait(self):
                self.eng.wait_ge(self.s, self.n)

            def link(self, ins):
                self.add(ins)
                self.wait()

        def half_tiles(eng, first, step, more=None):
            with eng.Fori(0, HALF // UNROLL) as i:
                for u in range(UNROLL):
                    step(first + u, i)
            for e in range(HALF // UNROLL * UNROLL, HALF if more is None else HALF + more):
                step(first + e, None)

        n_strips = AT[LASTS[STAGES - 1]] + 1

        def small_load(eng, name, dst, src):
            eng.dma_start(dst, src).then_inc(small_in[SMALL.index(name)], 16)

        def small_wait(eng, name):
            eng.wait_ge(small_in[SMALL.index(name)], 16 * SMALL_N[name])

        @block.sync
        def _(sp):
            for n in range(RING):
                sp.dma_start(ring[:, n, :], A["strips"][n]).then_inc(strip_landed[n], 16)
            rounds = n_strips // RING
            with sp.Fori(1, rounds) as i:
                for j in range(RING):
                    sp.wait_ge(low_ready, RING * i + (j + 1 - RING))
                    sp.dma_start(ring[:, j, :], A["strips"][RING * i + j]).then_inc(strip_landed[j], 16)
            for n in range(rounds * RING, n_strips):
                sp.wait_ge(low_ready, n + 1 - RING)
                sp.dma_start(ring[:, n % RING, :], A["strips"][n]).then_inc(strip_landed[n % RING], 16)
            sp.wait_ge(x_ready, NT * STAGES)
            sp.dma_start(out.rearrange("b (a p) d -> p (b a) d", p=P), x_s[:, :, :]).then_inc(out_done, 16)
            sp.wait_ge(out_done, 16)

        @block.tensor
        def _(pe):
            def split(n, i=None):
                pe.wait_ge(low_ready, n + 1 if i is None else UNROLL * i + (n + 1))
                return w_hi[:, n % RING, :], w_lo[:, n % RING, :]

            def mm3(out, l_hi, l_lo, r_hi, r_lo, start, stop, **kw):
                pe.matmul(out, l_hi, r_hi, start=start, stop=False, **kw)
                pe.matmul(out, l_lo, r_hi, start=False, stop=False, **kw)
                return pe.matmul(out, l_hi, r_lo, start=False, stop=stop, **kw)

            def strip_fm(out, w):
                for c in range(KC):
                    cols = slice(c * P, (c + 1) * P)
                    mm = mm3(out, w[0][:, cols], w[1][:, cols], hT_hi[:, c, :], hT_lo[:, c, :],
                             c == 0, c == KC - 1)
                mm.then_inc(strip_done, 1)

            nproj = [0]

            def proj_bank():
                m = nproj[0]
                nproj[0] += 1
                if m >= 2:
                    pe.wait_ge(evac, m - 1)
                return 4 + m % 2

            def proj_fm(name):
                w = split(AT[name])
                strip_fm(ps[:, proj_bank(), 0:T], w)

            def proj_tm(name):
                w = split(AT[name])
                b = proj_bank()
                for a in range(NT):
                    for c in range(KC):
                        cols, tok = slice(c * P, (c + 1) * P), slice(a * P, (a + 1) * P)
                        mm = mm3(ps[:, b, tok], hT_hi[:, c, tok], hT_lo[:, c, tok], w[0][:, cols],
                                 w[1][:, cols], c == 0, c == KC - 1)
                mm.then_inc(strip_done, 1)

            def proj_tm_pair(name, g):
                b = proj_bank()
                for half in range(2):
                    w = split(AT[name + (2 * g + half,)])
                    for a in range(NT):
                        for c in range(4):
                            cols, tok = slice(c * T, (c + 1) * T), slice(a * P, (a + 1) * P)
                            mm = mm3(ps[:, b, a * T:(a + 1) * T], hT_hi[:, 4 * half + c, tok],
                                     hT_lo[:, 4 * half + c, tok], w[0][:, cols], w[1][:, cols],
                                     half == 0 and a == 0 and c == 0, half == 1 and c == 3,
                                     skip_group_check=True)
                    mm.then_inc(strip_done, 1)

            def norm(i):
                pe.wait_ge(xn_ready, i + 1)
                for c in range(KC // 2):
                    for cc in range(2):
                        for a in range(NT):
                            mm = pe.transpose(ps[:, 4 + c, cc * T + a * P:cc * T + (a + 1) * P],
                                              xn[:, a, (2 * c + cc) * P:(2 * c + cc + 1) * P], ident)
                    mm.then_inc(turned, 1)
                pe.wait_ge(hT_low, 4 * i + 4)

            def seed(i):
                if i:
                    pe.wait_ge(x_ready, NT * i)
                for a in range(NT):
                    for b in range(2):
                        pe.matmul(ps[:, 2 * a + b, :], ident, x_s[:, a, b * 512:(b + 1) * 512],
                                  start=True, stop=False, skip_group_check=True)

            def rows(w, hi, lo, last):
                for a in range(NT):
                    for b in range(2):
                        tok, cols = slice(a * P, (a + 1) * P), slice(b * 512, (b + 1) * 512)
                        mm = mm3(ps[:, 2 * a + b, :], hi[:, tok], lo[:, tok], w[0][:, cols],
                                 w[1][:, cols], False, last, skip_group_check=True)
                mm.then_inc(strip_done, 1)

            def out_rows(i, name):
                for j in range(KC):
                    pe.wait_ge(mix_low, KC * i + j + 1)
                    rows(split(AT[(name, "out", j)]), hT_hi[:, j, :], hT_lo[:, j, :], j == KC - 1)

            def attention(t, qk, heads, v, probs_s, pT):
                pe.wait_ge(qk_ready, t + 1)
                for n, (jq, half, jk, vc) in enumerate(heads):
                    if n >= 4:
                        pe.wait_ge(score_out, NH * t + n - 3)
                    lo, hi = HD * half, HD * half + HD
                    pe.matmul(ps[:, n % 4, 0:P], qk[lo:hi, jq, 0:P], qk[lo:hi, jk, 0:P],
                              start=True, stop=True)
                    pe.matmul(ps[:, n % 4, P:3 * P], qk[lo:hi, jq, P:T], qk[lo:hi, jk, :],
                              start=True, stop=True).then_inc(score_done, 1)

            def attention_out(t, heads, v, probs_s, pT):
                pe.wait_ge(probs, t + 1)
                for n in range(NH):
                    if n >= 4:
                        pe.wait_ge(pT_out, NH * t + n - 3)
                    for b in range(3):
                        mm = pe.transpose(ps[:, n % 4, b * P:(b + 1) * P],
                                          probs_s[:, n, b * P:(b + 1) * P], ident)
                    mm.then_inc(pT_done, 1)
                for n, (jq, half, jk, vc) in enumerate(heads):
                    pe.wait_ge(pT_out, NH * t + n + 1)
                    if n % 2 == 0 and n >= 4:
                        pe.wait_ge(pv_out, 4 * t + n // 2 - 1)
                    b = 6 + (n // 2) % 2
                    o = ps[HD * half:HD * half + HD, b, 0:T]
                    pe.matmul(o, v[:, 0, vc:vc + HD], pT[:, n, 0:T], start=True, stop=False,
                              skip_group_check=True)
                    mm = pe.matmul(o[:, P:T], v[:, 1, vc:vc + HD], pT[:, n, T:3 * P], start=False,
                                   stop=True, skip_group_check=True)
                    if n % 2:
                        mm.then_inc(pv_done, 1)

            def even():
                for j in range(4):
                    proj_fm(("even", "u", j))
                proj_fm(("even", "k", 0))
                for j in range(4):
                    proj_fm(("even", "q", j))
                proj_tm(("even", "v", 0))
                pe.wait_ge(sq_ready, 1)
                for b, n in ((0, 512), (1, 512), (2, 256)):
                    mm = pe.matmul(ps[:, b, 0:n], k("head_ones"),
                                   e_sq.rearrange("p a b -> p (a b)")[:, b * 512:b * 512 + n],
                                   start=True, stop=True)
                mm.then_inc(sq_summed, 1)

                def bu(c):
                    if c >= 2:
                        pe.wait_ge(bu_used, c - 1)
                    lo = 32 * (c % 4)
                    for part in range(2):
                        mm = pe.matmul(ps[:, 6 + c % 2, part * T:(part + 1) * T],
                                       e_B[lo:lo + 32, part, c // 4, :], e_uT[lo:lo + 32, c // 4, :],
                                       start=True, stop=True)
                    mm.then_inc(bu_done, 1)

                def y(c):
                    pe.wait_ge(back, c + 1)
                    if c == 0:
                        pe.wait_ge(cw_ready, 1)
                    lo = 32 * (c % 4)
                    for part in range(2):
                        mm = pe.matmul(ps[lo:lo + 32, 4 + (c // 4) % 2, 0:T], e_CW[:, part, c, :],
                                       e_h[:, c % 4, part, :], start=(part == 0),
                                       stop=(part == 1), skip_group_check=True)
                    mm.then_inc(y_done, 1)

                small_wait(pe, "ssm")
                bu(0)
                bu(1)
                attention(0, e_qk, EVEN_HEADS, e_v, e_S, e_PT)
                for c in range(SG):
                    if c >= 4 and c % 4 == 0 and c >= 8:
                        pe.wait_ge(y_sum, c // 4 - 1)
                    if c == 0:
                        pe.wait_ge(evac, nproj[0])
                    y(c)
                    if c + 2 < SG:
                        bu(c + 2)
                attention_out(0, EVEN_HEADS, e_v, e_S, e_PT)
                pe.wait_ge(y_low, 4)
                for s in range(2):
                    w = split(AT[("even", "glu", s)])
                    for j in range(2):
                        for c in range(4):
                            cols = slice(c * T + j * P, c * T + (j + 1) * P)
                            mm = mm3(ps[:, 4 + s, j * T:(j + 1) * T], w[0][:, cols], w[1][:, cols],
                                     hT_hi[:, 4 + c, :], hT_lo[:, 4 + c, :], c == 0, c == 3)
                    mm.then_inc(strip_done, 1)
                seed(0)
                out_rows(0, "even")

            def mlp(n, name):
                base = AT[(name, "gate", 0)]

                def gate_up(strip, bank, i=None):
                    for part in range(2):
                        strip_fm(ps[:, bank + 2 * part, 0:T], split(strip + part, i))

                def down(strip, c, last=False, i=None):
                    w = split(strip, i)
                    pe.wait_ge(ff_ready, FC * n + c + 1 if i is None else 2 * i + (FC * n + c + 1))
                    rows(w, a_hi[:, c % 2, :], a_lo[:, c % 2, :], last)

                seed(STAGE_OF[name])
                gate_up(base, 4)
                with pe.Fori(0, (FC - 2) // 2) as i:
                    for u in range(2):
                        gate_up(base + 2 + 3 * u, 4 + (1 + u) % 2, i)
                        down(base + 4 + 3 * u, u, False, i)
                last = base + 2 + 3 * (FC - 2)
                gate_up(last, 4 + (FC - 1) % 2)
                down(last + 2, FC - 2)
                down(last + 3, FC - 1, True)

            def odd():
                for g in range(4):
                    proj_tm_pair(("odd", "v"), g)

                def z(h):
                    j, lo = h // 2, HD * (h % 2)
                    if h % 2 == 0:
                        pe.wait_ge(evac, nproj[0])
                    if h >= 4:
                        pe.wait_ge(w_masked, h - 3)
                    pe.matmul(ps[:, h % 4, 0:T], o_kT[lo:lo + HD, j, 0:P], o_qT[lo:lo + HD, j, :],
                              start=True, stop=True, skip_group_check=True)
                    pe.matmul(ps[:, h % 4, T:3 * P], o_kT[lo:lo + HD, j, P:T], o_qT[lo:lo + HD, j, P:T],
                              start=False, stop=True, skip_group_check=True).then_inc(z_done, 1)

                def cum(h):
                    pe.wait_ge(sp_masked, h + 1)
                    pe.matmul(ps[:, h % 4, 0:3 * P], k("neg_tri"), o_sp[:, h % 4, :], start=False,
                              stop=False, skip_group_check=True)
                    pe.matmul(ps[:, h % 4, P:T], k("neg_ones"), o_sp[:, h % 4, T:3 * P], start=False,
                              stop=True, skip_group_check=True).then_inc(cum_done, 1)

                def ov(h):
                    pe.wait_ge(w_ready, h + 1)
                    if h % 2 == 0 and h >= 4:
                        pe.wait_ge(ov_out, h // 2 - 1)
                    o = ps[HD * (h % 2):HD * (h % 2) + HD, 6 + (h // 2) % 2, 0:T]
                    pe.matmul(o, o_v[:, 0, h * HD:(h + 1) * HD], o_w[:, h % 4, 0:T], start=True,
                              stop=False, skip_group_check=True)
                    mm = pe.matmul(o[:, P:T], o_v[:, 1, h * HD:(h + 1) * HD], o_w[:, h % 4, T:3 * P],
                                   start=False, stop=True, skip_group_check=True)
                    if h % 2:
                        mm.then_inc(ov_done, 1)

                for j in range(10):
                    if j < 8:
                        proj_fm(("odd", "q", j))
                    if 1 <= j <= 8:
                        cum(2 * j - 2)
                        cum(2 * j - 1)
                    if j < 8:
                        proj_fm(("odd", "k", j))
                    if j >= 2:
                        ov(2 * j - 4)
                        ov(2 * j - 3)
                    if j < 8:
                        z(2 * j)
                        z(2 * j + 1)
                pe.wait_ge(w_masked, 16)
                seed(2)
                out_rows(1, "odd")

            def mix():
                proj_fm(("mix", "if", 0))
                for j in range(4):
                    proj_fm(("mix", "u", j))
                for g in range(2):
                    proj_tm_pair(("mix", "vm"), g)
                pe.wait_ge(rows_ready, 1)
                for n in range(3):
                    mm = pe.transpose(ps[:, 7, n * MH:(n + 1) * MH],
                                      m_row[0:MH, 7 if n == 2 else 3, (n % 2) * P:(n % 2 + 1) * P],
                                      ident[0:MH, 0:MH])
                mm.then_inc(cols_done, 1)
                small_wait(pe, "mix")
                for h in range(MH):
                    pe.wait_ge(conv_silu, h + 1)
                    for part in range(2):
                        mm = pe.matmul(ps[:, h, part * T:(part + 1) * T], m_wqk[:, part, h, :],
                                       m_cT[:, h, :], start=True, stop=True)
                    mm.then_inc(qkm_done, 1)
                for n in ("qa", "ka"):
                    for j in range(4):
                        proj_fm(("mix", n, j))
                for g in range(2):
                    proj_tm_pair(("mix", "va"), g)
                for h in range(MH):
                    pe.wait_ge(qkm_out, h + 1)
                    pe.matmul(ps[:, h, :], k("head_row", h * P, (h + 1) * P)[0:MH],
                              m_row[0:MH, 4:6, :].rearrange("p a b -> p (a b)"), start=True,
                              stop=True).then_inc(bcast_done, 1)
                for j in range(4):
                    proj_fm(("mix", "z", j))
                for h in range(MH):
                    b = 6 + h % 2
                    if h == 1:
                        pe.wait_ge(cols_out, 1)
                    if h >= 2:
                        pe.wait_ge(s_ready, h - 1)
                    pe.matmul(ps[:, b, 0:T], m_km[:, h, 0:P], m_qm[:, h, :], start=True, stop=True)
                    pe.matmul(ps[:, b, T:3 * P], m_km[:, h, P:T], m_qm[:, h, P:T], start=True,
                              stop=True).then_inc(st_done, 1)
                for h in range(MH):
                    pe.wait_ge(s_ready, h + 1)
                    if h == 0:
                        pe.wait_ge(em_out, MH)
                    vh = m_vm[:, :, h * P:(h + 1) * P]
                    for at, l0, l1 in ((0, vh[:, 0, :], vh[:, 1, :]), (T, ones, ones)):
                        pe.matmul(ps[:, h, at:at + T], l0, m_s[:, h, 0:T], start=(at == 0), stop=False,
                                  skip_group_check=True)
                        mm = pe.matmul(ps[:, h, at + P:at + T], l1, m_s[:, h, T:3 * P], start=False,
                                       stop=True, skip_group_check=True)
                    mm.then_inc(num_done, 1)
                pe.wait_ge(sq_ready, 2)
                pe.wait_ge(evac, nproj[0])
                pe.wait_ge(s_ready, MH)
                for b in range(4):
                    mm = pe.matmul(ps[:, 4 + b, :], k("head_ones"),
                                   m_sq.rearrange("p a b -> p (a b)")[:, b * 512:(b + 1) * 512],
                                   start=True, stop=True)
                mm.then_inc(sq_summed, 1)
                pe.wait_ge(hm_sq, 1)
                for b in range(2):
                    mm = pe.matmul(ps[:, b, :], ones,
                                   m_dn.rearrange("p a b -> p (a b)")[:, b * 512:(b + 1) * 512],
                                   start=True, stop=True)
                mm.then_inc(hm_summed, 1)
                pe.wait_ge(hm_rt, 1)
                attention(1, m_qk, MIX_HEADS, m_va, m_S, m_PT)
                attention_out(1, MIX_HEADS, m_va, m_S, m_PT)
                seed(4)
                out_rows(2, "mix")

            def peer():
                first = nproj[0]
                small_wait(pe, "keys")

                def key_scores(s):
                    pe.wait_ge(evac, first + s + 1)
                    if s >= 2:
                        pe.wait_ge(key_out, s - 1)
                    for a in range(NT):
                        mm = pe.matmul(ps[:, 6 + s % 2, a * P:(a + 1) * P],
                                       r_q[:, s % 2, a * P:(a + 1) * P],
                                       keys_s[:, s % 2, (s // 2) * P:(s // 2 + 1) * P],
                                       start=True, stop=True)
                    mm.then_inc(key_done, 1)

                for s in range(2 * PH):
                    proj_fm(("peer", "q", s))
                    if s:
                        key_scores(s - 1)
                key_scores(2 * PH - 1)
                pe.wait_ge(evac, nproj[0])
                base = AT[("peer", "u", 0)]

                def up(e, i=None):
                    w = split(base + e, i)
                    if i is not None:
                        pe.wait_ge(gelu_done, UNROLL * i + (e - 1))
                    elif e >= 2:
                        pe.wait_ge(gelu_done, e - 1)
                    strip_fm(ps[:, 4 + e % 2, 0:T], w)

                def scatter(half, g, i=None):
                    at = HALF * half + g
                    count = lambda v: at + v if i is None else UNROLL * i + (at + v)
                    pe.wait_ge(onehot_ready, count(1))
                    pe.wait_ge(gate_free, count(1))
                    for q in range(4):
                        for part in range(3):
                            mm = pe.matmul(ps[:, 6 + g % 2, q * HALF:(q + 1) * HALF],
                                           oh_second[:, g % 2, q, :], oh_gate[:, g % 2, q, part, :],
                                           start=(part == 0), stop=(part == 2))
                    mm.then_inc(spread, 1)

                for e in range(UNROLL):
                    up(e)
                with pe.Fori(1, HALF // UNROLL) as i:
                    for e in range(UNROLL):
                        up(e, i)
                for e in range(HALF // UNROLL * UNROLL, HALF):
                    up(e)
                pe.wait_ge(route_ready, 1)
                for n in range(3):
                    for a in range(NT):
                        mm = pe.transpose(ps[:, 6 + n // 2, (n % 2) * T + a * P:(n % 2) * T + (a + 1) * P],
                                          xn[:, 0, n * T + a * P:n * T + (a + 1) * P], ident)
                mm.then_inc(eT_done, 1)

                def up_and_gate(e, i):
                    up(e, i)
                    scatter(0, e - HALF, i)

                half_tiles(pe, HALF, up_and_gate)
                for c in range(KC):
                    for a in range(NT):
                        pe.matmul(ps[:, c // 2, (c % 2) * T + a * P:(c % 2) * T + (a + 1) * P],
                                  x_s[:, a, c * P:(c + 1) * P], ident, start=(c % 2 == 0 and a == 0),
                                  stop=False, skip_group_check=True)
                base = AT[("peer", "v", 0)]

                def down(e, i=None):
                    w = split(base + e, i)
                    pe.wait_ge(ff_ready, 2 * FC + e + 1 if i is None else UNROLL * i + (2 * FC + e + 1))
                    for c in range(KC):
                        cols = slice(c * P, (c + 1) * P)
                        mm = mm3(ps[:, c // 2, (c % 2) * T:(c % 2 + 1) * T], w[0][:, cols],
                                 w[1][:, cols], a_hi[:, e % 2, :], a_lo[:, e % 2, :], False,
                                 e == NE1 - 1, skip_group_check=True)
                    mm.then_inc(strip_done, 1)

                def down_and_gate(e, i):
                    down(e, i)
                    scatter(1, e, i)

                half_tiles(pe, 0, down_and_gate)
                half_tiles(pe, HALF, down)
                pe.wait_ge(yT_out, 2)
                for c in range(KC):
                    for a in range(NT):
                        mm = pe.transpose(ps[:, 4 + 2 * a + c // 4, (c % 4) * P:(c % 4 + 1) * P],
                                          xn[:, c // 4, (c % 4) * T + a * P:(c % 4) * T + (a + 1) * P], ident)
                mm.then_inc(out_turned, 1)

            small_wait(pe, "const")
            for n, (name, body) in enumerate([("even", even), ("mlp0", lambda: mlp(0, "mlp0")),
                                              ("odd", odd), ("mlp1", lambda: mlp(1, "mlp1")),
                                              ("mix", mix), ("peer", peer)][:STAGES]):
                norm(n)
                body()

        @block.scalar
        def _(sc):
            small_load(sc, "x", x_s[:, :, :], A["x"].rearrange("b (a p) d -> p (b a) d", p=P))
            small_load(sc, "param", param[:, :], A["param"])
            small_load(sc, "const", const[:, :], A["const"])
            small_load(sc, "ssm", e_B.rearrange("p a b c -> p (a b c)"), A["ssm_b"])
            small_load(sc, "ssm", e_C.rearrange("p a b c -> p (a b c)"), A["ssm_c"])
            ch = Chain(sc, act_chain)
            nproj = [0]
            split = [0]

            def high(n, i=None):
                sc.wait_ge(strip_landed[n % RING], 16 * (n // RING + 1) if i is None
                           else 32 * i + 16 * (n // RING + 1))
                if i is not None:
                    sc.wait_ge(strip_done, UNROLL * i + (n + 1 - RING))
                elif n >= RING:
                    sc.wait_ge(strip_done, n + 1 - RING)
                sc.activation(w_hi[:, n % RING, :], ring[:, n % RING, :], ACT.Copy).then_inc(high_ready, 1)

            def high_to(n):
                for m in range(split[0], min(n + 1, n_strips)):
                    high(m)
                split[0] = max(split[0], n + 1)

            def mix_split(i, mixT, js):
                for j in js:
                    sc.activation(hT_hi[:, j, :], mixT[:, j, :], ACT.Copy).then_inc(mix_high, 1)

            def norm(i):
                if i == 0:
                    small_wait(sc, "x")
                    small_wait(sc, "const")
                    small_wait(sc, "param")
                for a in range(NT):
                    if i:
                        sc.wait_ge(x_ready, NT * (i - 1) + a + 1)
                    ch.add(sc.activation(xn[:, 0, :], x_s[:, a, :], ACT.Square, accum_out=stat[:, a:a + 1]))
                    ch.wait()
                sc.activation(stat[:, 2:4], stat[:, 0:2], ACT.Sqrt, bias=k("eps"),
                              scale=1.0 / D).then_inc(roots, 1)
                if i == 3:
                    small_load(sc, "mix", m_bias.rearrange("p a b -> p (a b)"), A["rel"])
                    small_load(sc, "mix", m_wqk.rearrange("p a b c -> p (a b c)"), A["wqk"])
                if i == 5:
                    small_load(sc, "keys", keys_s.rearrange("p a b -> p (a b)"), A["keys"])
                first = 0 if i == 0 else AT[LASTS[i - 1]] + 1
                high_to(first)
                for c in range(KC // 2):
                    sc.wait_ge(turned, 4 * i + c + 1)
                    for cc in range(2):
                        ins = sc.activation(hT_hi[:, 2 * c + cc, :], ps[:, 4 + c, cc * T:(cc + 1) * T],
                                            ACT.Copy, scale=prm(NORMS[i], 2 * c + cc, 2 * c + cc + 1))
                    ins.then_inc(hT_high, 1)
                high_to(first + RING - 1)

            def out_of(name, dst, src=None, func=ACT.Copy, width=T, **kw):
                high_to(AT[name] + RING - 1)
                sc.wait_ge(strip_done, AT[name] + 1)
                b = 4 + nproj[0] % 2
                nproj[0] += 1
                sc.activation(dst, ps[:, b, 0:width] if src is None else src(b), func, **kw).then_inc(evac, 1)

            def out_of_pair(name, g, dst):
                out_of(name + (2 * g + 1,), dst[:, :, g * T:(g + 1) * T],
                       lambda b: ps[:, b, :].rearrange("p (a c) -> p a c", a=NT))

            def softmax(t, S, sm, sink):
                sc.wait_ge(shifted, t + 1)
                f = S.rearrange("p a b -> p (a b)")
                if sink:
                    ch.add(sc.activation(sm[:, 2, :], sm[:, 2, :], ACT.Exp))
                sc.activation(f, f, ACT.Exp).then_inc(exp_done, 1)

            def attention_out(t, pT, mixT, at):
                for n in range(NH):
                    sc.wait_ge(pT_done, NH * t + n + 1)
                    sc.activation(pT[:, n, :], ps[:, n % 4, 0:3 * P], ACT.Copy).then_inc(pT_out, 1)
                for j in range(4):
                    sc.wait_ge(pv_done, 4 * t + j + 1)
                    sc.activation(mixT[:, at + j, :], ps[:, 6 + j % 2, 0:T], ACT.Copy).then_inc(pv_out, 1)

            def even():
                sc.activation(e_p[:, 0, :], prm("log_dt"), ACT.Exp).then_inc(prm_act, 1)
                sc.wait_ge(prm_dve, 1)
                sc.activation(e_p[:, 3, :], e_p[:, 1, :], ACT.Exp).then_inc(prm_act, 1)
                sc.wait_ge(prm_dve, 2)
                sc.activation(e_p[:, 9, :], e_p[:, 6, :], ACT.Sin).then_inc(prm_act, 1)
                sc.activation(e_p[:, 10, :], e_p[:, 7, :], ACT.Sin).then_inc(prm_act, 1)
                for j in range(4):
                    out_of(("even", "u", j), e_uT[:, j, :])
                out_of(("even", "k", 0), e_qk[:, 4, :])
                for j in range(4):
                    out_of(("even", "q", j), e_qk[:, j, :])
                out_of(("even", "v", 0), e_v.rearrange("p a b -> p (a b)"))
                sc.wait_ge(sq_summed, 1)
                sc.activation(e_rt.rearrange("p a b -> p (a b)"),
                              ps[:, 0:3, :].rearrange("p a b -> p (a b)")[:, 0:5 * T], ACT.Sqrt,
                              bias=k("eps"), scale=1.0 / HD).then_inc(rt_ready, 1)
                softmax(0, e_S, e_sm, True)
                attention_out(0, e_PT, e_mixT, 0)
                sc.wait_ge(pv_out, 4)
                mix_split(0, e_mixT, range(4))
                for j in range(4):
                    sc.wait_ge(y_sum, j + 1)
                    sc.activation(e_y[:, j, :], e_y[:, j, :], ACT.Gelu_apprx_tanh).then_inc(y_gelu, 1)
                sc.wait_ge(y_gelu, 4)
                for j in range(4):
                    sc.activation(hT_hi[:, 4 + j, :], e_y[:, j, :], ACT.Copy).then_inc(y_high, 1)
                for s in range(2):
                    sc.wait_ge(strip_done, AT[("even", "glu", s)] + 1)
                    for j in range(2):
                        sc.activation(e_sq[:, 2 * s + j, :], ps[:, 4 + s, j * T:(j + 1) * T], ACT.Sigmoid,
                                      bias=prm("b_glu", 2 * s + j, 2 * s + j + 1)).then_inc(glu_sig, 1)
                sc.wait_ge(glu_out, 1)
                mix_split(0, e_mixT, range(4, 8))
                high_to(AT[("even", "out", 7)])

            def mlp(n, name):
                base = AT[(name, "gate", 0)]

                def silu(strip, c, i=None):
                    sc.wait_ge(strip_done, strip + 1 if i is None else UNROLL * i + (strip + 1))
                    sc.activation(f_silu[:, c % 2, :], ps[:, 4 + c % 2, 0:T], ACT.Silu).then_inc(silu_ready, 1)

                silu(base, 0)
                high_to(base + 3)
                with sc.Fori(0, (FC - 2) // 2) as i:
                    for u in range(2):
                        at = base + 2 + 3 * u
                        high(at + 2, i)
                        silu(at, 1 + u, i)
                        high(at + 3, i)
                        high(at + 4, i)
                split[0] = base + 2 + 3 * (FC - 2) + 2
                at = base + 2 + 3 * (FC - 2)
                high_to(at + 2)
                silu(at, FC - 1)
                high_to(at + 3)

            def odd():
                for g in range(4):
                    out_of_pair(("odd", "v"), g, o_v)

                def softplus(h):
                    sc.wait_ge(z_done, h + 1)
                    if h >= 2:
                        sc.wait_ge(sp_ready, h - 1)
                    t = o_t[:, h % 2, :]
                    ch.link(sc.activation(t, ps[:, h % 4, 0:3 * P], ACT.Abs))
                    ch.link(sc.activation(t, t, ACT.Exp, scale=-1.0))
                    sc.activation(t, t, ACT.Ln, bias=1.0).then_inc(z_log, 1)

                def weights(h):
                    sc.wait_ge(w_masked, h + 1)
                    if h >= 4:
                        sc.wait_ge(ov_done, (h - 4) // 2 + 1)
                    sc.activation(o_w[:, h % 4, :], o_w0[:, h % 4, :], ACT.Exp).then_inc(w_ready, 1)

                def ov_copy(j):
                    sc.wait_ge(ov_done, j + 1)
                    sc.activation(o_mixT[:, j, :], ps[:, 6 + j % 2, 0:T], ACT.Copy).then_inc(ov_out, 1)

                for j in range(10):
                    if j < 8:
                        out_of(("odd", "q", j), o_qT[:, j, :], scale=HD ** -0.5)
                    if 1 <= j <= 8:
                        weights(2 * j - 2)
                        weights(2 * j - 1)
                    if j < 8:
                        out_of(("odd", "k", j), o_kT[:, j, :])
                    if j >= 2:
                        ov_copy(j - 2)
                    if j < 8:
                        softplus(2 * j)
                        softplus(2 * j + 1)
                sc.wait_ge(ov_out, 8)
                mix_split(1, o_mixT, range(KC))
                high_to(AT[("odd", "out", 7)])

            def mix():
                r = m_row[0:MH]
                high_to(AT[("mix", "if", 0)] + RING - 1)
                sc.wait_ge(strip_done, AT[("mix", "if", 0)] + 1)
                b = 4 + nproj[0] % 2
                nproj[0] += 1
                ch.add(sc.activation(r[:, 0, :], ps[0:MH, b, 0:T], ACT.Identity, bias=prm("ig_b")[0:MH]))
                sc.activation(r[:, 1, :], ps[FG_AT:FG_AT + MH, b, 0:T], ACT.Identity,
                              bias=prm("fg_b")[FG_AT:FG_AT + MH]).then_inc(evac, 1)
                sc.wait_ge(evac, nproj[0])
                ch.link(sc.activation(r[:, 2, :], r[:, 1, :], ACT.Abs))
                ch.link(sc.activation(r[:, 2, :], r[:, 2, :], ACT.Exp, scale=-1.0))
                sc.activation(r[:, 2, :], r[:, 2, :], ACT.Ln, bias=1.0).then_inc(gate_act, 1)
                for j in range(4):
                    out_of(("mix", "u", j), m_up[:, j, 3:T + 3])
                for g in range(2):
                    out_of_pair(("mix", "vm"), g, m_vm)
                sc.wait_ge(cols_done, 1)
                sc.activation(m_rc.rearrange("p a b -> p (a b)"), ps[:, 7, 0:3 * MH],
                              ACT.Copy).then_inc(cols_out, 1)
                for j in range(4):
                    sc.wait_ge(conv_done, j + 1)
                    sc.activation(m_cT[:, j, :], m_cv[:, j, :], ACT.Silu).then_inc(conv_silu, 1)
                for h in range(MH):
                    sc.wait_ge(qkm_done, h + 1)
                    ch.add(sc.activation(m_qm[:, h, :], ps[:, h, 0:T], ACT.Copy))
                    sc.activation(m_km[:, h, :], ps[:, h, T:2 * T], ACT.Copy,
                                  scale=P ** -0.5).then_inc(qkm_out, 1)
                for n, at in (("qa", 0), ("ka", 4)):
                    for j in range(4):
                        out_of(("mix", n, j), m_qk[:, at + j, :])
                for g in range(2):
                    out_of_pair(("mix", "va"), g, m_va)
                sc.wait_ge(cols_out, 1)
                for h in range(MH):
                    sc.wait_ge(expo_in, h + 1)
                    for n, col in ((0, 0), (1, 2), (2, 1)):
                        ins = sc.activation(m_d[:, h, n * P:(n + 1) * P], m_x[:, h, n * P:(n + 1) * P],
                                            ACT.Exp, bias=m_rc[:, col, h:h + 1])
                        if n < 2:
                            ch.add(ins)
                    ins.then_inc(expo_out, 1)
                    sc.activation(m_em[:, h, :], ps[:, h, T:2 * T], ACT.Exp, scale=-1.0).then_inc(em_out, 1)
                for j in range(4):
                    out_of(("mix", "z", j), m_sz[:, j, :], func=ACT.Sigmoid)
                for h in range(MH):
                    sc.wait_ge(num_done, h + 1)
                    sc.activation(m_dn[:, h, :], ps[:, h, T:2 * T], ACT.Abs).then_inc(den_abs, 1)
                sc.wait_ge(sq_summed, 2)
                sc.activation(m_rt.rearrange("p a b -> p (a b)"),
                              ps[:, 4:8, :].rearrange("p a b -> p (a b)"), ACT.Sqrt,
                              bias=k("eps"), scale=1.0 / HD).then_inc(rt_ready, 1)
                sc.wait_ge(hm_summed, 1)
                sc.activation(m_dn.rearrange("p a b -> p (a b)"),
                              ps[:, 0:2, :].rearrange("p a b -> p (a b)"), ACT.Sqrt,
                              bias=k("eps"), scale=1.0 / P).then_inc(hm_rt, 1)
                softmax(1, m_S, m_sm, False)
                attention_out(1, m_PT, m_mixT, 4)
                sc.wait_ge(ym_ready, 1)
                sc.wait_ge(pv_out, 8)
                mix_split(2, m_mixT, range(KC))
                high_to(AT[("mix", "out", 7)])

            def peer():
                def key_copy(s):
                    sc.wait_ge(key_done, s + 1)
                    sc.activation(r_sc[:, s].rearrange("p a b -> p (a b)"), ps[:, 6 + s % 2, 0:T],
                                  ACT.Copy).then_inc(key_out, 1)

                for s in range(2 * PH):
                    if s >= 2:
                        sc.wait_ge(key_done, s - 1)
                    out_of(("peer", "q", s), r_q[:, s % 2, :])
                    if s:
                        key_copy(s - 1)
                key_copy(2 * PH - 1)
                base = AT[("peer", "u", 0)]

                def gelu(e, i=None):
                    n = base + e
                    high(n + RING - 1, i)
                    sc.wait_ge(strip_done, n + 1 if i is None else UNROLL * i + (n + 1))
                    dst = act[:, e, :] if i is None else act[:, bass.ds(UNROLL * i + e, 1), :].rearrange(
                        "p a t -> p (a t)")
                    sc.activation(dst, ps[:, 4 + e % 2, 0:T], ACT.Gelu).then_inc(gelu_done, 1)

                high_to(base + RING - 2)
                with sc.Fori(0, EXP_AT) as i:
                    for e in range(UNROLL):
                        gelu(e, i)
                sc.wait_ge(route_dve, 1)
                f = r_e[:, 2, :]
                sc.activation(f, f, ACT.Exp).then_inc(route_act, 1)
                with sc.Fori(EXP_AT, HALF // UNROLL) as i:
                    for e in range(UNROLL):
                        gelu(e, i)
                for e in range(HALF // UNROLL * UNROLL, HALF):
                    gelu(e)
                sc.wait_ge(route_ready, 1)
                half_tiles(sc, HALF, gelu)
                base = AT[("peer", "v", 0)]

                def value_high(e, i=None):
                    high(base + e + 2, i)
                    act_high(e + 1, i)

                def act_high(e, i=None):
                    src = act[:, e, :] if i is None else act[:, bass.ds(UNROLL * i + e, 1), :].rearrange(
                        "p a t -> p (a t)")
                    sc.activation(a_hi[:, e % 2, :], src, ACT.Copy).then_inc(a_high, 1)

                sc.wait_ge(gate_free, HALF + 2)
                act_high(0)
                half_tiles(sc, 0, value_high, -1)
                high(base + HALF + 1)
                sc.wait_ge(gate_free, NE1 + 2)
                act_high(HALF)
                half_tiles(sc, HALF, value_high, -2)
                sc.wait_ge(strip_done, base + NE1 - 2)
                act_high(NE1 - 1)
                sc.wait_ge(strip_done, AT[LASTS[5]] + 1)
                sc.activation(xn[:, 1, :], ps[:, 2:4, :].rearrange("p a b -> p (a b)"),
                              ACT.Copy).then_inc(yT_out, 1)

            for n, body in enumerate([even, lambda: mlp(0, "mlp0"), odd, lambda: mlp(1, "mlp1"), mix,
                                      peer][:STAGES]):
                norm(n)
                body()

        @block.vector
        def _(ve):
            ch = Chain(ve, dve_chain)

            def tt(o, a, b, op):
                return ve.tensor_tensor(o, a, b, op)

            def low(n, i=None):
                ve.wait_ge(high_ready, n + 1 if i is None else UNROLL * i + (n + 1))
                tt(w_lo[:, n % RING, :], ring[:, n % RING, :], w_hi[:, n % RING, :].bitcast(F32),
                   ALU.subtract).then_inc(low_ready, 1)

            def mix_split(i, mixT):
                for j in range(KC):
                    ve.wait_ge(mix_high, KC * i + j + 1)
                    tt(hT_lo[:, j, :], mixT[:, j, :], hT_hi[:, j, :].bitcast(F32),
                       ALU.subtract).then_inc(mix_low, 1)

            def norm(i):
                if i:
                    ve.wait_ge(strip_done, AT[LASTS[i - 1]] + 1)
                    for a in range(NT):
                        ve.tensor_copy(x_s[:, a, :], ps[:, 2 * a:2 * a + 2, :].rearrange(
                            "p a b -> p (a b)")).then_inc(x_ready, 1)
                    ve.wait_ge(x_ready, NT * i)
                else:
                    small_wait(ve, "x")
                    small_wait(ve, "const")
                    small_wait(ve, "param")
                ve.wait_ge(roots, i + 1)
                ch.link(ve.reciprocal(stat[:, 4:6], stat[:, 2:4]))
                ch.link(ve.tensor_scalar(xn[:, 0, :], x_s[:, 0, :], stat[:, 4:5], None, ALU.mult))
                ve.tensor_scalar(xn[:, 1, :], x_s[:, 1, :], stat[:, 5:6], None, ALU.mult).then_inc(xn_ready, 1)
                for c in range(KC // 2):
                    ve.wait_ge(hT_high, 4 * i + c + 1)
                    for cc in range(2):
                        j = 2 * c + cc
                        ins = ve.scalar_tensor_tensor(out=hT_lo[:, j, :], in0=ps[:, 4 + c, cc * T:(cc + 1) * T],
                                                      scalar=prm(NORMS[i], j, j + 1),
                                                      in1=hT_hi[:, j, :].bitcast(F32), op0=ALU.mult,
                                                      op1=ALU.subtract)
                    ins.then_inc(hT_low, 1)

            def bc(a, axis, shape):
                return a.unsqueeze(axis).broadcast_to(shape)

            def head_norm(t, qk, sq, rt, gains):
                tt(sq, qk, qk, ALU.mult).then_inc(sq_ready, 1)
                ve.wait_ge(rt_ready, t + 1)
                f = rt.rearrange("p a b -> p (a b)")
                ch.link(ve.reciprocal(f, f))
                for lo, hi, g in gains:
                    ins = ve.scalar_tensor_tensor(out=qk[:, lo:hi, :], in0=qk[:, lo:hi, :], scalar=g,
                                                  in1=rt[:, lo:hi, :], op0=ALU.mult, op1=ALU.mult)
                    if hi < qk.shape[1]:
                        ch.add(ins)
                ins.then_inc(qk_ready, 1)

            def softmax_in(t, S, sm, masks, sink):
                for n in range(NH):
                    ve.wait_ge(score_done, NH * t + n + 1)
                    lo, hi = masks(n)
                    ch.add(ve.scalar_tensor_tensor(out=S[:, n, 0:P], in0=ps[:, n % 4, 0:P],
                                                   scalar=HD ** -0.5, in1=lo, op0=ALU.mult, op1=ALU.add))
                    ve.scalar_tensor_tensor(out=S[:, n, P:3 * P], in0=ps[:, n % 4, P:3 * P],
                                            scalar=HD ** -0.5, in1=hi, op0=ALU.mult,
                                            op1=ALU.add).then_inc(score_out, 1)
                ve.wait_ge(score_out, NH * (t + 1))
                parts = ((S[:, :, 0:P], 0, P), (S[:, :, P:3 * P], NH, 2 * P))
                for s, at, w in parts:
                    ch.add(ve.tensor_reduce(sm[:, 0, at:at + NH], s, AX, ALU.max))
                ch.wait()
                if sink is not None:
                    m = sm[:, 0, :].rearrange("p (a h) -> p a h", a=2)
                    ch.link(tt(m, m, bc(sink, 1, [P, 2, NH]), ALU.max))
                    ch.add(tt(sm[:, 2, :].rearrange("p (a h) -> p a h", a=2),
                              bc(sink, 1, [P, 2, NH]), m, ALU.subtract))
                s, at, w = parts[0]
                ch.add(tt(s, s, bc(sm[:, 0, at:at + NH], 2, [P, NH, w]), ALU.subtract))
                s, at, w = parts[1]
                tt(s, s, bc(sm[:, 0, at:at + NH], 2, [P, NH, w]), ALU.subtract).then_inc(shifted, 1)

            def softmax_out(t, S, sm, count, sink):
                ve.wait_ge(exp_done, t + 1)
                if count is not None:
                    ch.link(tt(S, S, bc(count, 1, [P, NH, 3 * P]), ALU.mult))
                parts = ((S[:, :, 0:P], 0, P), (S[:, :, P:3 * P], NH, 2 * P))
                for s, at, w in parts:
                    ch.add(ve.tensor_reduce(sm[:, 1, at:at + NH], s, AX, ALU.add))
                ch.wait()
                if sink:
                    ch.link(tt(sm[:, 1, :], sm[:, 1, :], sm[:, 2, :], ALU.add))
                ch.link(ve.reciprocal(sm[:, 3, :], sm[:, 1, :]))
                for s, at, w in parts:
                    ins = tt(s, s, bc(sm[:, 3, at:at + NH], 2, [P, NH, w]), ALU.mult)
                    if at == 0:
                        ch.add(ins)
                ins.then_inc(probs, 1)

            def even():
                small_wait(ve, "ssm")
                p = lambda n: e_p[:, n, :]
                ve.wait_ge(prm_act, 1)
                ch.add(tt(p(2), prm("a_im"), p(0), ALU.mult))
                tt(p(1), prm("a_re"), p(0), ALU.mult).then_inc(prm_dve, 1)
                ve.wait_ge(prm_dve, 1)
                ch.link(ve.tensor_scalar(p(4), p(2), INV_2PI, None, ALU.mult))
                ch.link(ve.tensor_scalar(p(4), p(4), ROUND, None, ALU.add))
                ch.link(ve.tensor_scalar(p(4), p(4), -ROUND, None, ALU.add))
                ch.link(ve.scalar_tensor_tensor(out=p(5), in0=p(4), scalar=-C1, in1=p(2), op0=ALU.mult, op1=ALU.add))
                ch.link(ve.scalar_tensor_tensor(out=p(5), in0=p(4), scalar=-C2, in1=p(5), op0=ALU.mult, op1=ALU.add))
                ch.add(ve.tensor_scalar(p(6), p(5), PI_LO, -PI_LO, ALU.min, ALU.max))
                ch.link(ve.tensor_scalar(p(7), p(5), TWO_PI / 4, None, ALU.add))
                ch.link(ve.tensor_scalar(p(8), p(7), TWO_PI / 2, -TWO_PI, ALU.is_gt, ALU.mult))
                ch.link(tt(p(7), p(7), p(8), ALU.add))
                ve.tensor_scalar(p(7), p(7), PI_LO, -PI_LO, ALU.min, ALU.max).then_inc(prm_dve, 1)
                ve.wait_ge(prm_act, 4)
                ch.add(tt(p(11), p(3), p(10), ALU.mult))
                ch.add(tt(p(12), p(3), p(9), ALU.mult))
                ch.add(tt(p(15), prm("a_re"), prm("a_re"), ALU.mult))
                ch.link(tt(p(16), prm("a_im"), prm("a_im"), ALU.mult))
                ch.link(tt(p(15), p(15), p(16), ALU.add))
                ch.link(ve.reciprocal(p(15), p(15)))
                ch.link(ve.tensor_scalar(p(17), p(11), -1.0, None, ALU.add))
                ch.add(tt(p(13), p(17), prm("a_re"), ALU.mult))
                ch.add(tt(p(16), p(12), prm("a_im"), ALU.mult))
                ch.add(tt(p(14), p(12), prm("a_re"), ALU.mult))
                ch.link(tt(p(18), p(17), prm("a_im"), ALU.mult))
                ch.add(tt(p(13), p(13), p(16), ALU.add))
                ch.link(tt(p(14), p(14), p(18), ALU.subtract))
                ch.add(tt(p(13), p(13), p(15), ALU.mult))
                ch.link(tt(p(14), p(14), p(15), ALU.mult))
                wr, wi = (bc(p(n), 2, [P, SG, 32]) for n in (13, 14))
                cr, ci = e_C[:, 0], e_C[:, 1]
                ch.add(tt(e_CW[:, 0], cr, wr, ALU.mult))
                ch.link(tt(e_ctmp, ci, wi, ALU.mult))
                ch.link(tt(e_CW[:, 0], e_CW[:, 0], e_ctmp, ALU.subtract))
                ch.add(tt(e_CW[:, 1], cr, wi, ALU.mult))
                ch.link(tt(e_ctmp, ci, wr, ALU.mult))
                ve.scalar_tensor_tensor(out=e_CW[:, 1], in0=e_CW[:, 1], scalar=-1.0, in1=e_ctmp,
                                        op0=ALU.mult, op1=ALU.subtract).then_inc(cw_ready, 1)
                ch.add(ve.memset(e_cos[:, :, 0:1], 1.0))
                ch.add(ve.memset(e_sin[:, :, 0:1], 0.0))
                ch.add(ve.tensor_copy(p(19), p(10)))
                ch.link(ve.tensor_copy(p(20), p(9)))
                n = 1
                while n < T:
                    bcos, bsin = bc(p(19), 2, [P, SG, n]), bc(p(20), 2, [P, SG, n])
                    t0 = e_tmp[:, 0, 0:SG * n].rearrange("p (a b) -> p a b", a=SG)
                    t1 = e_tmp[:, 1, 0:SG * n].rearrange("p (a b) -> p a b", a=SG)
                    old_c, old_s = e_cos[:, :, 0:n], e_sin[:, :, 0:n]
                    new_c, new_s = e_cos[:, :, n:2 * n], e_sin[:, :, n:2 * n]
                    ch.add(tt(t0, old_s, bsin, ALU.mult))
                    ch.add(tt(t1, old_s, bcos, ALU.mult))
                    ch.add(tt(new_c, old_c, bcos, ALU.mult))
                    ch.add(tt(new_s, old_c, bsin, ALU.mult))
                    ch.add(tt(p(21), p(19), p(19), ALU.mult))
                    ch.add(tt(p(22), p(20), p(20), ALU.mult))
                    ch.link(tt(p(23), p(19), p(20), ALU.mult))
                    ch.add(tt(new_c, new_c, t0, ALU.subtract))
                    ch.add(tt(new_s, new_s, t1, ALU.add))
                    ch.add(tt(p(19), p(21), p(22), ALU.subtract))
                    ch.link(ve.tensor_scalar(p(20), p(23), 2.0, None, ALU.mult))
                    n *= 2
                ve.wait_ge(evac, 9)
                head_norm(0, e_qk, e_sq, e_rt, [(0, 4, prm("q_norm")), (4, 5, prm("k_norm"))])

                def ssm(c):
                    ve.wait_ge(bu_done, c + 1)
                    if c >= 4:
                        ve.wait_ge(back, c - 3)
                    src = ps[:, 6 + c % 2, :].rearrange("p (a b) -> p a b", a=2)
                    zt0 = e_zt[:, 0, :].rearrange("p (a b) -> p a b", a=2)
                    zt1 = e_zt[:, 1, :].rearrange("p (a b) -> p a b", a=2)
                    ch.add(tt(zt0, src, bc(e_cos[:, c, :], 1, [P, 2, T]), ALU.mult))
                    tt(zt1, src, bc(e_sin[:, c, :], 1, [P, 2, T]), ALU.mult).then_inc(bu_used, 1)
                    ve.wait_ge(bu_used, c + 1)
                    z = e_z[:, c % 4]
                    ch.add(tt(z[:, 0, :], zt0[:, 0, :], zt1[:, 1, :], ALU.add))
                    ch.link(tt(z[:, 1, :], zt0[:, 1, :], zt1[:, 0, :], ALU.subtract))
                    m = e_p[:, 3, c:c + 1].broadcast_to([P, T])
                    ch.add(ve.tensor_tensor_scan(z[:, 0, :], m, z[:, 0, :], 0.0, ALU.mult, ALU.add))
                    ve.tensor_tensor_scan(z[:, 1, :], m, z[:, 1, :], 0.0, ALU.mult, ALU.add).then_inc(scanned, 1)

                def y(j):
                    ve.wait_ge(y_done, 4 * j + 4)
                    ve.scalar_tensor_tensor(out=e_y[:, j, :], in0=e_uT[:, j, :], scalar=prm("ssm_d", j, j + 1),
                                            in1=ps[:, 4 + j % 2, 0:T], op0=ALU.mult,
                                            op1=ALU.add).then_inc(y_sum, 1)

                ssm(0)
                ssm(1)
                mask = k("window_mask")
                softmax_in(0, e_S, e_sm, lambda n: (mask[:, 0:P], mask[:, P:3 * P]), prm("sinks"))
                for c in range(2, 6):
                    ssm(c)
                softmax_out(0, e_S, e_sm, None, True)
                for c in range(6, SG):
                    ssm(c)
                    if c % 4 == 0 and c >= 8:
                        y(c // 4 - 2)
                y(2)
                y(3)
                for j in range(4):
                    ve.wait_ge(y_high, j + 1)
                    tt(hT_lo[:, 4 + j, :], e_y[:, j, :], hT_hi[:, 4 + j, :].bitcast(F32),
                       ALU.subtract).then_inc(y_low, 1)
                ve.wait_ge(glu_sig, 4)
                tt(e_mixT[:, 4:8, :], e_y, e_sq[:, 0:4, :], ALU.mult).then_inc(glu_out, 1)
                mix_split(0, e_mixT)

            def mlp(n, name):
                base = AT[(name, "gate", 0)]

                def combine(strip, c, i=None):
                    at = lambda v: v if i is None else 2 * i + v
                    ve.wait_ge(strip_done, strip + 1 if i is None else UNROLL * i + (strip + 1))
                    ve.wait_ge(silu_ready, at(FC * n + c + 1))
                    tt(f_act[:, c % 2, :], f_silu[:, c % 2, :], ps[:, 6 + c % 2, 0:T],
                       ALU.mult).then_inc(a_ready, 1)
                    ve.wait_ge(a_ready, at(FC * n + c + 1))
                    ve.tensor_copy(a_hi[:, c % 2, :], f_act[:, c % 2, :]).then_inc(a_high, 1)
                    ve.wait_ge(a_high, at(FC * n + c + 1))
                    tt(a_lo[:, c % 2, :], f_act[:, c % 2, :], a_hi[:, c % 2, :].bitcast(F32),
                       ALU.subtract).then_inc(ff_ready, 1)

                for m in range(3):
                    low(base + m)
                combine(base + 1, 0)
                low(base + 3)
                with ve.Fori(0, (FC - 2) // 2) as i:
                    for u in range(2):
                        at = base + 2 + 3 * u
                        low(at + 2, i)
                        low(at + 3, i)
                        combine(at + 1, 1 + u, i)
                        low(at + 4, i)
                at = base + 2 + 3 * (FC - 2)
                low(at + 2)
                low(at + 3)
                combine(at + 1, FC - 1)

            def odd():
                def softplus(h):
                    ve.wait_ge(z_log, h + 1)
                    if h >= 4:
                        ve.wait_ge(cum_done, h - 3)
                    ve.scalar_tensor_tensor(out=o_sp[:, h % 4, :], in0=ps[:, h % 4, 0:3 * P], scalar=0.0,
                                            in1=o_t[:, h % 2, :], op0=ALU.max,
                                            op1=ALU.add).then_inc(sp_ready, 1)

                def weights(h):
                    ve.wait_ge(cum_done, h + 1)
                    if h >= 4:
                        ve.wait_ge(w_ready, h - 3)
                    tt(o_w0[:, h % 4, :], ps[:, h % 4, 0:3 * P], k("strict_mask"),
                       ALU.add).then_inc(w_masked, 1)

                for j in range(9):
                    if j >= 1:
                        weights(2 * j - 2)
                        weights(2 * j - 1)
                    if j < 8:
                        softplus(2 * j)
                        softplus(2 * j + 1)
                mix_split(1, o_mixT)

            def mix():
                r = m_row[0:MH]
                ch.add(ve.memset(r[:, 9, :], 1.0))
                ch.link(ve.memset(m_up[:, :, 0:3], 0.0))
                ve.wait_ge(gate_act, 1)
                ch.link(ve.scalar_tensor_tensor(out=r[:, 1, :], in0=r[:, 1, :], scalar=0.0, in1=r[:, 2, :],
                                                op0=ALU.min, op1=ALU.subtract))
                for a in range(NT):
                    ch.add(ve.tensor_tensor_scan(r[:, 6, a * P:(a + 1) * P], r[:, 9, a * P:(a + 1) * P],
                                                 r[:, 1, a * P:(a + 1) * P], 0.0, ALU.mult, ALU.add))
                ch.wait()
                ch.link(tt(r[:, 3, :], r[:, 0, :], r[:, 6, :], ALU.subtract))
                ch.link(ve.tensor_tensor_scan(r[:, 8, 0:P], r[:, 3, 0:P], r[:, 3, 0:P], 0.0, ALU.max, ALU.max))
                ch.link(tt(r[:, 2, 0:1], r[:, 6, P - 1:P], r[:, 8, P - 1:P], ALU.add))
                ch.link(ve.tensor_tensor_scan(r[:, 8, P:T], r[:, 3, P:T], r[:, 3, P:T], r[:, 2, 0:1],
                                              ALU.max, ALU.max))
                ch.add(ve.tensor_scalar(r[:, 4, :], r[:, 8, :], -1.0, None, ALU.mult))
                ch.add(tt(r[:, 5, :], r[:, 6, :], r[:, 8, :], ALU.add))
                ve.tensor_scalar(r[:, 7, 0:P], r[:, 3, 0:P], r[:, 6, P - 1:P], None,
                                 ALU.add).then_inc(rows_ready, 1)
                for j in range(4):
                    ve.wait_ge(evac, GATE_EVAC + 1 + j + 1)
                    cw = lambda i: prm("conv_w", 4 * j + i, 4 * j + i + 1)
                    o = m_cv[:, j, :]
                    ch.link(ve.tensor_scalar(o, m_up[:, j, 0:T], cw(0), prm("conv_b", j, j + 1),
                                             ALU.mult, ALU.add))
                    for i in range(1, 4):
                        ins = ve.scalar_tensor_tensor(out=o, in0=m_up[:, j, i:T + i], scalar=cw(i), in1=o,
                                                      op0=ALU.mult, op1=ALU.add)
                        if i < 3:
                            ch.link(ins)
                    ins.then_inc(conv_done, 1)
                for h in range(MH):
                    ve.wait_ge(bcast_done, h + 1)
                    x = m_x[:, h, :]
                    ch.add(tt(x[:, 0:T], ps[:, h, 0:T], k("causal_mask", 0, T), ALU.add))
                    tt(x[:, T:3 * P], ps[:, h, P:T], k("causal_mask", T, 3 * P), ALU.add).then_inc(expo_in, 1)
                for h in range(MH):
                    decay(h)
                small_wait(ve, "mix")
                ch.add(tt(m_bias, m_bias, bc(k("dilated_mask", P, 3 * P), 1, [P, NH, T]), ALU.add))
                head_norm(1, m_qk, m_sq, m_rt,
                          [(j, j + 1, prm("qn" if j < 4 else "kn", j % 4, j % 4 + 1)) for j in range(8)])
                f = lambda a: a.rearrange("p a b -> p (a b)")
                ve.wait_ge(den_abs, MH)
                ve.wait_ge(em_out, MH)
                ch.link(tt(f(m_dn), f(m_dn), f(m_em), ALU.max))
                ch.link(ve.reciprocal(f(m_dn), f(m_dn)))
                ch.link(tt(m_hm, ps[:, 0:MH, 0:T], m_dn, ALU.mult))
                tt(f(m_dn), f(m_hm), f(m_hm), ALU.mult).then_inc(hm_sq, 1)
                for h in range(MH):
                    ch.add(ve.tensor_scalar(m_cs[:, h, :], m_cT[:, h, :], prm("skip", h, h + 1), None, ALU.mult))
                ve.wait_ge(hm_rt, 1)
                ch.link(ve.reciprocal(f(m_dn), f(m_dn)))
                ch.link(tt(f(m_hm), f(m_hm), f(m_dn), ALU.mult))
                for h in range(MH):
                    ch.add(ve.scalar_tensor_tensor(out=m_hm[:, h, :], in0=m_hm[:, h, :],
                                                   scalar=prm("mh_norm", h, h + 1), in1=m_cs[:, h, :],
                                                   op0=ALU.mult, op1=ALU.add))
                ch.wait()
                ve.wait_ge(evac, GATE_EVAC + 1 + 20)
                tt(m_mixT[:, 0:4, :], m_hm, m_sz, ALU.mult).then_inc(ym_ready, 1)
                softmax_in(1, m_S, m_sm, lambda n: (m_bias[:, n, P:T], m_bias[:, n, :]), None)
                softmax_out(1, m_S, m_sm, k("dilated_count"), False)
                mix_split(2, m_mixT)

            def decay(h):
                ve.wait_ge(st_done, h + 1)
                ve.wait_ge(expo_out, h + 1)
                tt(m_s[:, h, :], ps[:, 6 + h % 2, 0:3 * P], m_d[:, h, :], ALU.mult).then_inc(s_ready, 1)

            def peer():
                def top16(v, i, row):
                    ch.link(ve.max(v[:, 0:8], row))
                    ch.link(ve.max_index(i[:, 0:8], v[:, 0:8], row))
                    ch.link(ve.match_replace(out=row, in_to_replace=v[:, 0:8], in_values=row, imm_value=-3e38))
                    ch.link(ve.max(v[:, 8:16], row))
                    ch.link(ve.max_index(i[:, 8:16], v[:, 8:16], row))

                iu, icu = r_i.bitcast(U32), r_ic.bitcast(U32)
                for s in range(2 * PH):
                    ve.wait_ge(key_out, s + 1)
                    for a in range(NT):
                        top16(r_v[:, a, s, :], iu[:, a, s, :], r_sc[:, s, a, :])
                    if s % 2:
                        h = s // 2
                        for a in range(NT):
                            ch.link(tt(r_c[:, a, :].rearrange("p (a b) -> p a b", a=TOPK),
                                       bc(r_v[:, a, s - 1, :], 2, [P, TOPK, TOPK]),
                                       bc(r_v[:, a, s, :], 1, [P, TOPK, TOPK]), ALU.add))
                            top16(r_vc[:, a, h, :], icu[:, a, h, :], r_c[:, a, :])
                n = NT * PH
                g = r_e[:, 2, :].rearrange("p (a b) -> p a b", b=TOPK)
                vc = r_vc.rearrange("p a h b -> p (a h) b")
                tt(g, vc, vc[:, :, 0:1].broadcast_to([P, n, TOPK]), ALU.subtract).then_inc(route_dve, 1)
                ic = icu.rearrange("p a h b -> p (a h b)")
                hl = r_hl.bitcast(U32)
                ch.add(ve.tensor_scalar(hl[:, 0, :], ic, 4, None, ALU.logical_shift_right))
                ch.add(ve.tensor_scalar(hl[:, 1, :], ic, 15, None, ALU.bitwise_and))
                ch.link(ve.tensor_copy(r_if.rearrange("p a s b -> p (a s b)"),
                                       iu.rearrange("p a s b -> p (a s b)")))
                ch.link(ve.tensor_copy(r_hlf.rearrange("p a b -> p (a b)"), hl.rearrange("p a b -> p (a b)")))
                big = [P, PH, TOPK, TOPK]
                tmp = keys_s.rearrange("p a b -> p (a b)").rearrange(
                    "p (h k i) -> p h k i", h=PH, k=TOPK)
                iota16 = k("iota", 0, TOPK).unsqueeze(1).unsqueeze(1).broadcast_to(big)
                for a in range(NT):
                    for part in range(2):
                        at = r_hlf[:, part, a * P:(a + 1) * P].rearrange("p (h k) -> p h k", h=PH)
                        keys = r_if[:, a, part:2 * PH:2, :]
                        ch.link(tt(tmp, at.unsqueeze(3).broadcast_to(big), iota16, ALU.is_equal))
                        ch.link(tt(tmp, tmp, keys.unsqueeze(2).broadcast_to(big), ALU.mult))
                        ch.link(ve.tensor_reduce(
                            r_e[:, part, a * P:(a + 1) * P].rearrange("p (h k) -> p h k", h=PH), tmp, AX,
                            ALU.add))
                ve.wait_ge(route_act, 1)
                s = r_sum[:, 0, :]
                ch.link(ve.tensor_reduce(s, g, AX, ALU.add))
                ch.link(ve.reciprocal(s, s))
                ch.link(tt(g, g, bc(s, 2, [P, n, TOPK]), ALU.mult))
                ve.tensor_copy(xn[:, 0, 0:3 * T], r_e.rearrange("p a b -> p (a b)")).then_inc(route_ready, 1)
                ve.wait_ge(eT_done, 1)
                ch.add(ve.tensor_copy(iota_b[:, :], k("iota")))
                ve.tensor_copy(key_at[:, :, :], ps[:, 6, :].rearrange("p (a b) -> p a b", a=2)).then_inc(gate_free, 1)
                ch.link(ve.tensor_copy(gate3[:, :, 0], ps[:, 7, 0:T]))
                tt(gate_rest[:, 0, :], ps[:, 7, 0:T], gate3[:, :, 0], ALU.subtract).then_inc(gate_free, 1)
                ve.wait_ge(gate_free, 2)
                ch.link(ve.tensor_copy(gate3[:, :, 1], gate_rest[:, 0, :]))
                ch.link(tt(gate_rest[:, 1, :], gate_rest[:, 0, :], gate3[:, :, 1], ALU.subtract))
                ch.link(ve.tensor_copy(gate3[:, :, 2], gate_rest[:, 1, :]))

                def one_hot(half, g, i=None):
                    tok = slice(4 * g, 4 * g + 4) if i is None else bass.ds(4 * UNROLL * i + 4 * g, 4)
                    wide, narrow = [P, 4, P], [P, 4, HALF]
                    tt(oh_first[:, g % 2], bc(iota_b[:, HALF * half:HALF * (half + 1)], 1, narrow),
                       bc(key_at[:, 0, tok], 2, narrow), ALU.is_equal).then_inc(first_ready, 1)
                    tt(oh_second[:, g % 2], bc(iota_b[:, :], 1, wide), bc(key_at[:, 1, tok], 2, wide),
                       ALU.is_equal)
                    at = HALF * half + g + 1
                    ve.wait_ge(first_ready, at if i is None else UNROLL * i + at)
                    shape = [P, 4, 3, HALF]
                    tt(oh_gate[:, g % 2], bc(oh_first[:, g % 2], 2, shape), bc(gate3[:, tok, :], 3, shape),
                       ALU.mult).then_inc(onehot_ready, 1)

                def apply_gates(half, g, i=None):
                    at = HALF * half + g + 1
                    ve.wait_ge(spread, at if i is None else UNROLL * i + at)
                    tok = slice(4 * g, 4 * g + 4) if i is None else bass.ds(4 * UNROLL * i + 4 * g, 4)
                    part = act[:, HALF * half:HALF * (half + 1), tok]
                    tt(part, part, ps[:, 6 + g % 2, 0:4 * HALF].rearrange("p (q e) -> p e q", q=4),
                       ALU.mult).then_inc(gate_free, 1)

                def act_low(e, i=None):
                    ve.wait_ge(a_high, 2 * FC + e + 1 if i is None else UNROLL * i + (2 * FC + e + 1))
                    src = act[:, e, :] if i is None else act[:, bass.ds(UNROLL * i + e, 1), :].rearrange(
                        "p a t -> p (a t)")
                    tt(a_lo[:, e % 2, :], src, a_hi[:, e % 2, :].bitcast(F32),
                       ALU.subtract).then_inc(ff_ready, 1)

                def gate_first(g, i):
                    one_hot(0, g + 1, i)
                    apply_gates(0, g, i)

                def gate_second(e, i):
                    act_low(e + 1, i)
                    one_hot(1, e + 1, i)
                    apply_gates(1, e, i)

                one_hot(0, 0)
                ve.wait_ge(gelu_done, HALF)
                half_tiles(ve, 0, gate_first, -1)
                apply_gates(0, HALF - 1)
                one_hot(1, 0)
                ve.wait_ge(gate_free, HALF + 2)
                act_low(0)
                ve.wait_ge(gelu_done, NE1)
                half_tiles(ve, 0, gate_second, -1)
                apply_gates(1, HALF - 1)
                ve.wait_ge(gate_free, NE1 + 2)
                act_low(HALF)
                half_tiles(ve, HALF, lambda e, i: act_low(e + 1, i), -1)
                ve.wait_ge(strip_done, AT[LASTS[5]] + 1)
                ve.tensor_copy(xn[:, 0, :], ps[:, 0:2, :].rearrange("p a b -> p (a b)")).then_inc(yT_out, 1)
                ve.wait_ge(out_turned, 1)
                for a in range(NT):
                    ve.tensor_copy(x_s[:, a, :], ps[:, 4 + 2 * a:6 + 2 * a, :].rearrange(
                        "p a b -> p (a b)")).then_inc(x_ready, 1)

            for n, body in enumerate([even, lambda: mlp(0, "mlp0"), odd, lambda: mlp(1, "mlp1"), mix,
                                      peer][:STAGES]):
                norm(n)
                body()
            if STAGES < 6:
                ve.wait_ge(strip_done, n_strips)
                for a in range(2):
                    ve.tensor_copy(x_s[:, a, :],
                               ps[:, 2*a:2*a+2, :].rearrange("p a b -> p (a b)")).then_inc(x_ready, 1)

        @block.gpsimd
        def _(po):
            ch = Chain(po, pool_chain)

            def low(n, i=None):
                po.wait_ge(high_ready, n + 1 if i is None else UNROLL * i + (n + 1))
                po.tensor_tensor(w_lo[:, n % RING, :], ring[:, n % RING, :],
                                 w_hi[:, n % RING, :].bitcast(F32), ALU.subtract).then_inc(low_ready, 1)

            def lows(first, last):
                for n in range(AT[first], AT[last] + 1):
                    low(n)

            lows(STRIPS[0], ("even", "v", 0))
            for c in range(SG):
                po.wait_ge(scanned, c + 1)
                z = e_z[:, c % 4]
                h0 = e_ht[:, 0, :].rearrange("p (a b) -> p a b", a=2)
                h1 = e_ht[:, 1, :].rearrange("p (a b) -> p a b", a=2)
                ch.add(po.tensor_tensor(h0, z, e_cos[:, c, :].unsqueeze(1).broadcast_to([P, 2, T]), ALU.mult))
                ch.link(po.tensor_tensor(h1, z, e_sin[:, c, :].unsqueeze(1).broadcast_to([P, 2, T]), ALU.mult))
                if c >= 4:
                    po.wait_ge(y_done, c - 3)
                h = e_h[:, c % 4]
                ch.add(po.tensor_tensor(h[:, 0, :], h0[:, 0, :], h1[:, 1, :], ALU.subtract))
                po.tensor_tensor(h[:, 1, :], h0[:, 1, :], h1[:, 0, :], ALU.add).then_inc(back, 1)
                po.wait_ge(back, c + 1)
            lows(("even", "glu", 0), ("even", "out", 7))
            if STAGES >= 3:
                po.wait_ge(low_ready, AT[("odd", "v", 0)])
                lows(("odd", "v", 0), ("odd", "v", 7))
                for j in range(9):
                    if j < 8:
                        lows(("odd", "q", j), ("odd", "k", j))
                    if j:
                        for h in (2 * j - 2, 2 * j - 1):
                            po.wait_ge(sp_ready, h + 1)
                            v = o_sp[:, h % 4, :].rearrange("p (b c) -> p b c", c=P)[:, 0:3:2, :]
                            po.affine_select(out=v, in_=v, compare_op=ALU.is_gt, fill=0.0, base=0,
                                             pattern=[[0, 2], [1, P]],
                                             channel_multiplier=-1).then_inc(sp_masked, 1)
                lows(("odd", "out", 0), ("odd", "out", 7))
            if STAGES >= 5:
                po.wait_ge(low_ready, AT[("mix", "if", 0)])
                lows(("mix", "if", 0), ("mix", "out", 7))
            if STAGES >= 6:
                base = AT[("peer", "q", 0)]
                for n in range(2 * PH):
                    low(base + n)
                base = AT[("peer", "u", 0)]
                with po.Fori(0, 2 * NE1 // UNROLL) as i:
                    for e in range(UNROLL):
                        low(base + e, i)
                for e in range(2 * NE1 // UNROLL * UNROLL, 2 * NE1):
                    low(base + e)


def _constants():
    c = np.zeros((P, N_CONST), np.float32)

    def put(name, v):
        c[:v.shape[0], CONST[name][0]:CONST[name][1]] = v

    i, j = np.arange(P)[:, None], np.arange(P)[None, :]
    put("ident", np.eye(P))
    put("ones", np.ones((P, P)))
    put("head_ones", (i // HD == j // HD) * 1.0)
    put("neg_tri", (i >= j) * -1.0)
    put("neg_ones", -np.ones((P, P)))
    put("iota", np.broadcast_to(j, (P, P)))
    free = np.zeros((P, P))
    strict, causal = np.where(i < j, 0.0, -BIG), np.where(i <= j, 0.0, -BIG)
    put("strict_mask", np.concatenate([strict, free, strict], 1))
    put("causal_mask", np.concatenate([causal, free, causal], 1))
    dist = np.concatenate([i - j, i - j + P, i - j], 1)
    put("window_mask", np.where((dist >= 0) & (dist < 128), 0.0, -BIG))
    count = sum(((dist >= 0) & (dist % dil == 0) & (dist // dil <= win // dil)).astype(np.float32)
                for win, dil in ((128, 1), (512, 4), (2048, 16)))
    put("dilated_count", count)
    put("dilated_mask", np.where(count > 0, 0.0, -BIG))
    put("head_row", np.repeat(np.eye(MH), P, axis=1))
    put("eps", np.full((P, 1), EPS))
    return c


def _buckets():
    d = np.arange(T)
    large = 16 + (np.log(np.maximum(d, 1).astype(np.float32) / np.float32(16))
                  / np.float32(np.log(2048 / 16)) * 16).astype(np.int32)
    return np.where(d < 16, d, np.minimum(large, 31))


def _layout(v):
    f = {n: np.asarray(a) for n, a in v.items()}
    strips = np.empty((NS, P, D), np.float32)

    def cols(w, at, rows=D):
        w = w[:, at]
        return w.reshape(rows // P, P, w.shape[1]).transpose(1, 0, 2).reshape(P, -1)

    def put(name, w):
        strips[AT[name]] = w

    ar = np.arange
    w = f["even_w_in"][0]
    for j in range(4):
        put(("even", "u", j), cols(w, 768 + P * j + ar(P)))
        put(("even", "q", j), cols(w, np.concatenate([HD * j + ar(HD), HD * (j + 4) + ar(HD)])))
    put(("even", "k", 0), cols(w, 512 + ar(P)))
    put(("even", "v", 0), cols(w, 640 + ar(P)))
    for j in range(2):
        put(("even", "glu", j), cols(f["ssm_w_glu"][0], 256 * j + ar(256), 512))
    w = f["even_w_out"][0]
    for j in range(8):
        rows = np.concatenate([HD * j + ar(HD), HD * (j + 4) + ar(HD)]) if j < 4 else P * j + ar(P)
        put(("even", "out", j), w[rows])
        put(("odd", "out", j), f["odd_w_out"][0][P * j:P * j + P])
        put(("mix", "out", j), f["w_out_2"][0][P * j:P * j + P])
    for n in range(2):
        for c in range(FC):
            put((f"mlp{n}", "gate", c), cols(f["ffn_w_gate"][n], P * c + ar(P)))
            put((f"mlp{n}", "up", c), cols(f["ffn_w_up"][n], P * c + ar(P)))
            put((f"mlp{n}", "down", c), f["ffn_w_down"][n][P * c:P * c + P])
    for j in range(8):
        for n, part in enumerate("qk"):
            put(("odd", part, j), cols(f["odd_w_in"][0], D * n + P * j + ar(P)))

    def put_pairs(name, w, first, n):
        for j in range(n):
            rows = D // 2 * (j % 2)
            put(name + (j,), cols(w[rows:rows + D // 2], first + T * (j // 2) + ar(T), D // 2))

    put_pairs(("odd", "v"), f["odd_w_in"][0], 2 * D, 8)
    w = f["w_in_2"][0]
    put_pairs(("mix", "vm"), w, 512, 4)
    put_pairs(("mix", "va"), w, 2568, 4)
    at = {"u": 0, "z": 1024, "qa": 1544, "ka": 2056}
    for part, first in at.items():
        for j in range(4):
            put(("mix", part, j), cols(w, first + P * j + ar(P)))
    gates = np.zeros((P, KC, P), np.float32)
    gates[:, :, 0:MH] = cols(w, 1536 + ar(MH)).reshape(P, KC, MH)
    gates[:, :, FG_AT:FG_AT + MH] = cols(w, 1536 + MH + ar(MH)).reshape(P, KC, MH)
    put(("mix", "if", 0), gates.reshape(P, D))
    for s in range(2 * PH):
        put(("peer", "q", s), cols(f["w_query_2"][0], P * s + ar(P)))
    u = f["expert_u_2"][0].reshape(NE1, P, KC, P)
    first = AT[("peer", "u", 0)]
    strips[first:first + NE1] = u.transpose(0, 3, 2, 1).reshape(NE1, P, D)
    first = AT[("peer", "v", 0)]
    strips[first:first + NE1] = f["expert_v_2"][0].reshape(NE1, P, D)

    param = np.zeros((P, N_PARAM), np.float32)

    def prm(name, w):
        param[:w.shape[0], PARAM[name][0]:PARAM[name][1]] = w

    chunks = lambda a: a.reshape(-1, P).T
    for name, a in (("even_norm", f["even_norm"][0]), ("mlp0_norm", f["ffn_norm"][0]),
                    ("odd_norm", f["odd_norm"][0]), ("mlp1_norm", f["ffn_norm"][1]),
                    ("mix_norm", f["norm1_g_2"][0]), ("peer_norm", f["norm2_g_2"][0]),
                    ("ssm_d", f["ssm_d"][0]), ("b_glu", f["ssm_b_glu"][0]),
                    ("conv_b", f["conv_b_2"][0]), ("mh_norm", f["mh_norm_g_2"][0].reshape(-1)),
                    ("skip", f["skip_m_2"][0].reshape(-1)), ("qn", f["qn_g_2"][0].reshape(-1)),
                    ("kn", f["kn_g_2"][0].reshape(-1)), ("a_re", f["ssm_a_re"][0].reshape(-1)),
                    ("a_im", f["ssm_a_im"][0].reshape(-1)),
                    ("log_dt", np.repeat(f["ssm_log_dt"][0], HD))):
        prm(name, chunks(a))
    prm("q_norm", np.tile(f["q_norm"][0], 2)[:, None])
    prm("k_norm", np.tile(f["k_norm"][0], 2)[:, None])
    order = [n // 2 + 4 * (n % 2) for n in range(NH)]
    prm("sinks", np.broadcast_to(f["sinks"][0][order], (P, NH)))
    prm("conv_w", f["conv_w_2"][0].reshape(4, 4, P).transpose(2, 1, 0).reshape(P, 16))
    prm("ig_b", f["ig_b_2"][0][:, None])
    param[FG_AT:FG_AT + MH, PARAM["fg_b"][0]] = f["fg_b_2"][0]

    ssm_b = np.zeros((4, 2, 16, 2, 4, 2, HD), np.float32)
    ssm_c = np.zeros((2, HD, 2, SG, 2, 16), np.float32)
    for part, (b, c) in enumerate((("ssm_b_re", "ssm_c_re"), ("ssm_b_im", "ssm_c_im"))):
        bb = f[b][0].reshape(4, 4, 2, HD, 16)
        cc = f[c][0].reshape(SG, 2, 16, HD)
        for g in range(2):
            ssm_b[:, g, :, part, :, g, :] = bb[:, :, g].transpose(1, 3, 0, 2)
            ssm_c[g, :, part, :, g, :] = cc[:, g].transpose(2, 0, 1)
    keys = np.stack([f[f"sub_keys{n}_2"][0].transpose(2, 0, 1).reshape(P, D) for n in (1, 2)], 1)
    wqk = np.stack([f[n][0].transpose(1, 0, 2) for n in ("wq_m_2", "wk_m_2")], 1)
    dist = np.arange(P)[:, None] + P - np.arange(T)[None, :]
    rel = f["rel_bias_2"][_buckets()[np.abs(dist) % T]].transpose(0, 2, 1)
    return {"strips": strips, "const": _constants(), "param": param, "ssm_b": ssm_b.reshape(P, D),
            "ssm_c": ssm_c.reshape(P, D), "keys": keys.reshape(P, 2 * D), "wqk": wqk.reshape(P, D),
            "rel": np.ascontiguousarray(rel).reshape(P, NH * T), "x": f["x"]}


def kernel(**inputs):
    import concourse.bacc as bacc
    from concourse.bass_utils import run_bass_kernel_spmd

    arrays = {f"in_{n}": np.ascontiguousarray(a) for n, a in _layout(inputs).items()}
    nc = bacc.Bacc("TRN2", target_bir_lowering=False, num_devices=1,
                   dynamic_dma_scratch_size=1024)
    A = {n[3:]: nc.dram_tensor(n, a.shape, F32, kind="ExternalInput").ap() for n, a in arrays.items()}
    out = nc.dram_tensor("out", (1, T, D), F32, kind="ExternalOutput").ap()
    build(nc, A, out)
    return run_bass_kernel_spmd(nc, [arrays], core_ids=[0]).results[0]["out"]
```

```python
from contextlib import ExitStack

import numpy as np

import concourse.bass as bass
from concourse import mybir

P = 128
D = 1024
T = 256
NT = T // P
KC = D // P
RING = 3
UNROLL = 2 * RING
FC = 2816 // P
HD = 64
SG = 16
NH = 8
MH = 4
PH = 8
TOPK = 16
FREE_TILES = 78
NE1 = 128
HALF = NE1 // 2
EPS = 1e-6
BIG = 1e30

F32 = mybir.dt.float32
F32R = mybir.dt.float32r
BF16 = mybir.dt.bfloat16
U32 = mybir.dt.uint32
ALU = mybir.AluOpType
ACT = mybir.ActivationFunctionType
AX = mybir.AxisListType.X

TWO_PI = 6.283185307179586
INV_2PI = 0.15915494309189535
C1 = 6.28125
C2 = TWO_PI - C1
ROUND = 12582912.0
PI_LO = 3.1415925

NORMS = ["even_norm", "mlp0_norm", "odd_norm", "mlp1_norm", "mix_norm", "peer_norm"]
LASTS = [("even", "out", 7), ("mlp0", "down", FC - 1), ("odd", "out", 7), ("mlp1", "down", FC - 1),
         ("mix", "out", 3), ("peer", "v", NE1 - 1)]
STAGE_OF = {"mlp0": 1, "mlp1": 3}
EVEN_HEADS = [(n // 2, n % 2, 4, HD * (n % 2)) for n in range(NH)]
MIX_HEADS = [(n // 2, n % 2, 4 + n // 2, HD * n) for n in range(NH)]
EXP_AT = 6
FG_AT = 32
EVEN_SLOTS = (4, 5, 6, 7, 4, 5, 6, 7)
MIX_ORDER = (4, 5, 6, 7, 0, 1, 2, 3)
GATE_EVAC = 10 + 20
SMALL = ["x", "first", "const", "param", "ssm", "keys", "mix"]
SMALL_N = {"x": 1, "first": 1, "const": 1, "param": 1, "ssm": 3, "keys": 1, "mix": 3}


def strip_names():
    names = []

    def mlp(n):
        names.extend([(n, "gate", 0), (n, "up", 0)])
        for c in range(1, FC):
            names.extend([(n, "gate", c), (n, "up", c), (n, "down", c - 1)])
        names.append((n, "down", FC - 1))

    names += [("even", "u", j) for j in range(4)] + [("even", "k", 0)]
    names += [("even", "q", j) for j in range(4)] + [("even", "v", 0)]
    names += [("even", "out", j) for j in range(4)] + [("even", "glu", j) for j in range(2)]
    names += [("even", "out", j) for j in range(4, 8)]
    mlp("mlp0")
    names += [("odd", "v", j) for j in range(8)]
    for j in range(8):
        names += [("odd", "q", j), ("odd", "k", j)]
    names += [("odd", "out", j) for j in range(8)]
    mlp("mlp1")
    names += [("mix", "if", 0)] + [("mix", "u", j) for j in range(4)]
    names += [("mix", "vm", j) for j in range(4)]
    names += [("mix", n, j) for n in ("qa", "ka", "va", "z") for j in range(4)]
    names += [("mix", "out", j) for j in MIX_ORDER]
    names += [("peer", "q", j) for j in range(2 * PH)]
    names += [("peer", "u", e) for e in range(NE1)] + [("peer", "v", e) for e in range(NE1)]
    return names


STRIPS = strip_names()
AT = {name: n for n, name in enumerate(STRIPS)}
NS = len(STRIPS)

CONST = {}
PARAM = {}


def _columns(table, widths):
    at = 0
    for name, width in widths:
        table[name] = (at, at + width)
        at += width
    return at


N_CONST = _columns(CONST, [
    ("ident", P), ("eps", 1), ("ones", P), ("head_sel", P), ("all_sel", MH * MH),
    ("neg_tri", P), ("neg_ones", P), ("iota", P),
    ("window_mask", 3 * P), ("strict_mask", 3 * P), ("causal_mask", 3 * P), ("dilated_mask", 3 * P),
    ("dilated_count", 3 * P), ("head_row", MH * P)])
N_FIRST = P + 1
N_PARAM = _columns(PARAM, [
    ("even_norm", KC), ("mlp0_norm", KC), ("odd_norm", KC), ("mlp1_norm", KC), ("mix_norm", KC),
    ("peer_norm", KC), ("q_norm", 1), ("k_norm", 1), ("sinks", NH), ("a_re", SG), ("a_im", SG),
    ("log_dt", SG), ("ssm_d", 4), ("b_glu", 4), ("conv_w", 16), ("conv_b", 4), ("ig_b", 1),
    ("fg_b", 1), ("mh_norm", MH), ("skip", MH), ("qn", 4), ("kn", 4)])


def build(nc, A, out):
    with ExitStack() as ctx:
        def sb(name, shape, dt=F32):
            return ctx.enter_context(nc.sbuf_tensor(name, shape, dt))

        def sem(name):
            return ctx.enter_context(nc.semaphore(name))

        ring = sb("ring", [P, RING, D])
        w_hi = sb("w_hi", [P, RING, D], F32R)
        w_lo = sb("w_lo", [P, RING, D], F32R)
        x_s = sb("x_s", [P, NT, D])
        xn = sb("xn", [P, NT, D])
        scale_diag = sb("scale_diag", [P, NT, P])
        hT_hi = sb("hT_hi", [P, KC, T], F32R)
        hT_lo = sb("hT_lo", [P, KC, T], F32R)
        a_hi = sb("a_hi", [P, 2, T], F32R)
        a_lo = sb("a_lo", [P, 2, T], F32R)
        const = sb("const", [P, N_CONST])
        param = sb("param", [P, N_PARAM])
        stat = sb("stat", [P, 8])
        key_at = sb("key_at", [P, 2, T], BF16)
        gate3 = sb("gate3", [P, T, 3], BF16)
        gate_rest = sb("gate_rest", [P, 2, T])
        iota_b = sb("iota_b", [P, P], BF16)
        ARENA = NE1 * T
        arena = sb("arena", [P, ARENA])
        ps = ctx.enter_context(nc.psum_tensor("ps", [P, 8, 512], F32))

        def k(name, a=0, b=None):
            lo, hi = CONST[name]
            return const[:, lo + a:(hi if b is None else lo + b)]

        def prm(name, a=0, b=None):
            lo, hi = PARAM[name]
            return param[:, lo + a:(hi if b is None else lo + b)]

        class Lay:

            def __init__(self, at=0):
                self.at = at

            def __call__(self, *shape):
                n = int(np.prod(shape))
                assert self.at + n <= ARENA, (self.at, n)
                v = arena[:, self.at:self.at + n]
                self.at += n
                if len(shape) == 2:
                    v = v.rearrange("p (a b) -> p a b", a=shape[0])
                if len(shape) == 3:
                    v = v.rearrange("p (a b c) -> p a b c", a=shape[0], b=shape[1])
                return v

        ident = k("ident")
        ones = k("ones")

        L = Lay()
        e_uT = L(4, T)
        e_qk = L(5, T)
        e_v = L(NT, P)
        e_B = L(2, 4, P)
        e_C = L(2, SG, 32)
        e_CW = L(2, SG, 32)
        e_ctmp = L(SG, 32)
        e_cos = L(SG, T)
        e_sin = L(SG, T)
        e_sq = L(5, T)
        e_rt = L(5, T)
        e_p = L(24, SG)
        e_z = L(4, 2, T)
        e_zt = L(2, 2 * T)
        e_ht = L(2, 2 * T)
        e_mark = L.at
        e_tmp = L(2, SG * P)
        L.at = e_mark
        e_h = L(4, 2, T)
        e_S = L(NH, 3 * P)
        e_PT = L(NH, 3 * P)
        e_sm = L(6, 2 * NH)
        e_y = L(4, T)
        e_mixT = L(KC, T)

        L = Lay()
        f_silu = L(2, T)
        f_act = L(2, T)

        L = Lay(2048)
        o_v = L(NT, D)
        o_qT = L(8, T)
        o_kT = L(8, T)
        o_t = L(2, 3 * P)
        o_sp = L(4, 3 * P)
        o_w0 = L(4, 3 * P)
        o_w = L(4, 3 * P)
        o_mixT = L(KC, T)

        L = Lay(1024)
        m_up = L(4, T + 3)
        m_x_at = L.at
        m_cv = L(4, T)
        m_cs = L(4, T)
        m_x = Lay(m_x_at)(MH, 3 * P)
        m_cT = L(4, T)
        m_sz = L(4, T)
        m_vm = L(NT, 512)
        m_va = L(NT, 512)
        m_qk = L(8, T)
        m_pT_at = L.at
        m_sq = L(8, T)
        m_rt = L(8, T)
        m_PT = Lay(m_pT_at)(NH, 3 * P)
        m_S = L(NH, 3 * P)
        m_bias = L(NH, T)
        m_wqk = L(2, MH, P)
        m_qm = L(MH, T)
        m_km = L(MH, T)
        m_row = L(10, T)
        m_rc = L(3, MH)
        m_d_at = L.at
        m_d = L(MH, 3 * P)
        m_hm = Lay(m_d_at)(MH, T)
        m_s = L(MH, 3 * P)
        m_em = L(MH, T)
        m_dn = L(MH, T)
        m_sm = L(6, 2 * NH)
        m_mixT = L(KC, T)

        act = arena[:, 0:NE1 * T].rearrange("p (e t) -> p e t", t=T)
        L = Lay(FREE_TILES * T)
        keys_s = L(2, D)
        r_q = L(2, T)
        r_sc = L(2 * PH, NT, P)
        r_v = L(NT, 2 * PH, TOPK)
        r_i = L(NT, 2 * PH, TOPK)
        r_if = L(NT, 2 * PH, TOPK)
        r_c = L(2, 256)
        r_vc = L(NT, PH, TOPK)
        r_ic = L(NT, PH, TOPK)
        r_hl = L(2, NT * PH * TOPK)
        r_hlf = L(2, NT * PH * TOPK)
        r_e = L(3, NT * PH * TOPK)
        r_sum = L(1, NT * PH)
        spare = xn[:, :, :].bitcast(BF16)
        oh_second = spare[:, :, 0:4 * P].rearrange("p g (t c) -> p g t c", c=P)
        oh_first = spare[:, :, 4 * P:4 * P + 4 * HALF].rearrange("p g (t c) -> p g t c", c=HALF)
        oh_gate = spare[:, :, 4 * P + 4 * HALF:4 * P + 16 * HALF].rearrange(
            "p g (t s c) -> p g t s c", s=3, c=HALF)

        strip_landed = [sem(f"strip_landed{i}") for i in range(RING)]
        first_half = sem("first_half")
        strip_done = sem("strip_done")
        high_ready = sem("high_ready")
        low_ready = sem("low_ready")
        small_in = [sem(f"small_in{i}") for i in range(8)]
        half_table = sem("half_table")
        sine_parts = sem("sine_parts")
        roots = sem("roots")
        diag_ready = sem("diag_ready")
        x_ready = sem("x_ready")
        turned = sem("turned")
        hT_high = sem("hT_high")
        hT_low = sem("hT_low")
        mix_high = sem("mix_high")
        mix_low = sem("mix_low")
        a_ready = sem("a_ready")
        a_high = sem("a_high")
        evac = sem("evac")
        silu_ready = sem("silu_ready")
        ff_ready = sem("ff_ready")
        prm_act = sem("prm_act")
        prm_dve = sem("prm_dve")
        cw_ready = sem("cw_ready")
        sq_ready = sem("sq_ready")
        sq_summed = sem("sq_summed")
        rs_ready = sem("rs_ready")
        rt_wide = sem("rt_wide")
        rt_used = sem("rt_used")
        rt_ready = sem("rt_ready")
        score_done = sem("score_done")
        score_out = sem("score_out")
        shifted = sem("shifted")
        exp_done = sem("exp_done")
        probs = sem("probs")
        pT_done = sem("pT_done")
        pT_out = sem("pT_out")
        pv_done = sem("pv_done")
        pv_out = sem("pv_out")
        bu_done = sem("bu_done")
        bu_used = sem("bu_used")
        scanned = sem("scanned")
        back = sem("back")
        y_done = sem("y_done")
        y_sum = sem("y_sum")
        y_gelu = sem("y_gelu")
        y_high = sem("y_high")
        y_low = sem("y_low")
        glu_sig = sem("glu_sig")
        glu_out = sem("glu_out")
        z_done = sem("z_done")
        z_log = sem("z_log")
        sp_ready = sem("sp_ready")
        sp_masked = sem("sp_masked")
        cum_done = sem("cum_done")
        w_masked = sem("w_masked")
        w_ready = sem("w_ready")
        ov_done = sem("ov_done")
        ov_out = sem("ov_out")
        gate_act = sem("gate_act")
        rows_ready = sem("rows_ready")
        cols_done = sem("cols_done")
        cols_out = sem("cols_out")
        conv_done = sem("conv_done")
        conv_silu = sem("conv_silu")
        qkm_done = sem("qkm_done")
        qkm_out = sem("qkm_out")
        bcast_done = sem("bcast_done")
        expo_in = sem("expo_in")
        expo_out = sem("expo_out")
        em_out = sem("em_out")
        st_done = sem("st_done")
        s_ready = sem("s_ready")
        num_done = sem("num_done")
        den_abs = sem("den_abs")
        hm_sq = sem("hm_sq")
        hm_summed = sem("hm_summed")
        hm_wide = sem("hm_wide")
        hm_used = sem("hm_used")
        ym_ready = sem("ym_ready")
        key_done = sem("key_done")
        key_out = sem("key_out")
        route_dve = sem("route_dve")
        route_act = sem("route_act")
        route_ready = sem("route_ready")
        eT_done = sem("eT_done")
        gelu_done = sem("gelu_done")
        first_ready = sem("first_ready")
        onehot_ready = sem("onehot_ready")
        spread = sem("spread")
        gate_free = sem("gate_free")
        yT_out = sem("yT_out")
        out_turned = sem("out_turned")
        act_chain = sem("act_chain")
        dve_chain = sem("dve_chain")
        pool_chain = sem("pool_chain")
        out_done = sem("out_done")

        block = ctx.enter_context(nc.Block())

        class Chain:

            def __init__(self, eng, s):
                self.eng, self.s, self.n = eng, s, 0

            def add(self, ins):
                self.n += 1
                ins.then_inc(self.s, 1)

            def wait(self):
                self.eng.wait_ge(self.s, self.n)

            def link(self, ins):
                self.add(ins)
                self.wait()

        def norm_bank(i, c):
            return (5, 4, 6, 7)[c] if i == 5 else 4 + c

        def half_tiles(eng, first, step, left_out=0):
            with eng.Fori(0, HALF // UNROLL) as i:
                for u in range(UNROLL):
                    step(first + u, i)
            for e in range(HALF // UNROLL * UNROLL, HALF - left_out):
                step(first + e, None)

        def small_load(eng, name, dst, src):
            eng.dma_start(dst, src).then_inc(small_in[SMALL.index(name)], 16)

        def small_wait(eng, name):
            eng.wait_ge(small_in[SMALL.index(name)], 16 * SMALL_N[name])

        @block.sync
        def _(sp):
            for n in range(RING):
                sp.dma_start(ring[:, n, :], A["strips"][n]).then_inc(strip_landed[n], 16)
            rounds = NS // RING
            with sp.Fori(1, rounds) as i:
                for j in range(RING):
                    sp.wait_ge(low_ready, RING * i + (j + 1 - RING))
                    sp.dma_start(ring[:, j, :], A["strips"][RING * i + j]).then_inc(strip_landed[j], 16)
            for n in range(rounds * RING, NS):
                sp.wait_ge(low_ready, n + 1 - RING)
                sp.dma_start(ring[:, n % RING, :], A["strips"][n]).then_inc(strip_landed[n % RING], 16)
            sp.wait_ge(x_ready, 4 * (len(NORMS) - 1) + NT)
            sp.dma_start(out.rearrange("b (a p) d -> p (b a) d", p=P), x_s[:, :, :]).then_inc(out_done, 16)
            sp.wait_ge(out_done, 16)

        @block.tensor
        def _(pe):
            def split(n, i=None):
                pe.wait_ge(low_ready, n + 1 if i is None else UNROLL * i + (n + 1))
                return w_hi[:, n % RING, :], w_lo[:, n % RING, :]

            def mm3(out, l_hi, l_lo, r_hi, r_lo, start, stop, **kw):
                pe.matmul(out, l_hi, r_hi, start=start, stop=False, **kw)
                pe.matmul(out, l_lo, r_hi, start=False, stop=False, **kw)
                return pe.matmul(out, l_hi, r_lo, start=False, stop=stop, **kw)

            def input_ready(fresh, c):
                if fresh is not None and c % 2 == 0:
                    pe.wait_ge(hT_low, 4 * fresh + c // 2 + 1)

            def strip_fm(out, w, fresh=None):
                for c in range(KC):
                    input_ready(fresh, c)
                    cols = slice(c * P, (c + 1) * P)
                    mm = mm3(out, w[0][:, cols], w[1][:, cols], hT_hi[:, c, :], hT_lo[:, c, :],
                             c == 0, c == KC - 1)
                mm.then_inc(strip_done, 1)

            nproj = [0]

            def proj_bank():
                m = nproj[0]
                nproj[0] += 1
                if m >= 2:
                    pe.wait_ge(evac, m - 1)
                return 4 + m % 2

            def proj_fm(name, fresh=None):
                w = split(AT[name])
                strip_fm(ps[:, proj_bank(), 0:T], w, fresh)

            def proj_tm(name):
                w = split(AT[name])
                b = proj_bank()
                for a in range(NT):
                    for c in range(KC):
                        cols, tok = slice(c * P, (c + 1) * P), slice(a * P, (a + 1) * P)
                        mm = mm3(ps[:, b, tok], hT_hi[:, c, tok], hT_lo[:, c, tok], w[0][:, cols],
                                 w[1][:, cols], c == 0, c == KC - 1)
                mm.then_inc(strip_done, 1)

            def proj_tm_pair(name, g, fresh=None):
                b = proj_bank()
                for half in range(2):
                    w = split(AT[name + (2 * g + half,)])
                    for a in range(NT):
                        for c in range(4):
                            input_ready(fresh, 4 * half + c)
                            cols, tok = slice(c * T, (c + 1) * T), slice(a * P, (a + 1) * P)
                            mm = mm3(ps[:, b, a * T:(a + 1) * T], hT_hi[:, 4 * half + c, tok],
                                     hT_lo[:, 4 * half + c, tok], w[0][:, cols], w[1][:, cols],
                                     half == 0 and a == 0 and c == 0, half == 1 and c == 3,
                                     skip_group_check=True)
                    mm.then_inc(strip_done, 1)

            def norm(i):
                for a in range(NT):
                    pe.wait_ge(diag_ready, NT * i + a + 1)
                    for c in range(KC):
                        at = (c % 2) * T + a * P
                        mm = pe.matmul(ps[:, norm_bank(i, c // 2), at:at + P], x_s[:, a, c * P:(c + 1) * P],
                                       scale_diag[:, a, :], start=True, stop=True)
                        if a == NT - 1 and c % 2:
                            mm.then_inc(turned, 1)

            def rows(w, hi, lo, first, last):
                for a in range(NT):
                    for b in range(2):
                        tok, cols = slice(a * P, (a + 1) * P), slice(b * 512, (b + 1) * 512)
                        mm = mm3(ps[:, 2 * a + b, :], hi[:, tok], lo[:, tok], w[0][:, cols],
                                 w[1][:, cols], first, last, skip_group_check=True)
                    if last and a == 0:
                        mm.then_inc(first_half, 1)
                mm.then_inc(strip_done, 1)

            def out_rows(i, name, ns, order=range(KC), slots=range(KC)):
                for n in ns:
                    j = order[n]
                    pe.wait_ge(mix_low, KC * i + n + 1)
                    rows(split(AT[(name, "out", j)]), hT_hi[:, slots[j], :], hT_lo[:, slots[j], :],
                         n == 0, n == KC - 1)

            def head_sums(sq, chunks, bank):
                for c in range(chunks):
                    mm = pe.matmul(ps[0:16, bank, 0:T], k("head_sel", 16 * c, 16 * c + 16), sq[:, c, :],
                                   start=(c == 0), stop=(c == chunks - 1))
                mm.then_inc(sq_summed, 1)

            def head_spread(rows, table, chunks, bank):
                table = table.rearrange("p a b -> p (a b)")
                for n, c in enumerate(chunks):
                    mm = pe.matmul(ps[:, bank + n // 2, (n % 2) * T:(n % 2 + 1) * T],
                                   table[0:16, c * P:(c + 1) * P], rows[0:16, 0, :], start=True, stop=True)
                mm.then_inc(rt_wide, 1)

            def attention(t, qk, heads):
                pe.wait_ge(rt_used, 3 if t else 1)
                for n in range(NH):
                    jq, half, jk, vc = heads[n]
                    if n >= 4:
                        pe.wait_ge(score_out, NH * t + n - 3)
                    lo, hi = HD * half, HD * half + HD
                    pe.matmul(ps[:, n % 4, 0:P], qk[lo:hi, jq, 0:P], qk[lo:hi, jk, 0:P],
                              start=True, stop=True)
                    pe.matmul(ps[:, n % 4, P:3 * P], qk[lo:hi, jq, P:T], qk[lo:hi, jk, :],
                              start=True, stop=True).then_inc(score_done, 1)

            def attention_out(t, heads, v, probs_s, pT):
                pe.wait_ge(probs, t + 1)
                for n in range(NH):
                    if n >= 4:
                        pe.wait_ge(pT_out, NH * t + n - 3)
                    for b in range(3):
                        mm = pe.transpose(ps[:, n % 4, b * P:(b + 1) * P],
                                          probs_s[:, n, b * P:(b + 1) * P], ident)
                    mm.then_inc(pT_done, 1)
                pe.wait_ge(pT_out, NH * (t + 1))
                for n, (jq, half, jk, vc) in enumerate(heads):
                    pe.wait_ge(pT_out, NH * t + n + 1)
                    if n % 2 == 0 and n >= 4:
                        pe.wait_ge(pv_out, 4 * t + n // 2 - 1)
                    b = (n // 2) % 2
                    o = ps[HD * half:HD * half + HD, b, 0:T]
                    pe.matmul(o, v[:, 0, vc:vc + HD], pT[:, n, 0:T], start=True, stop=False,
                              skip_group_check=True)
                    mm = pe.matmul(o[:, P:T], v[:, 1, vc:vc + HD], pT[:, n, T:3 * P], start=False,
                                   stop=True, skip_group_check=True)
                    if n % 2:
                        mm.then_inc(pv_done, 1)

            def even():
                for j in range(4):
                    proj_fm(("even", "u", j), None if j else 0)
                proj_fm(("even", "k", 0))
                for j in range(4):
                    proj_fm(("even", "q", j))
                proj_tm(("even", "v", 0))
                small_wait(pe, "const")
                pe.wait_ge(sq_ready, 1)
                head_sums(e_sq, 5, 0)
                small_wait(pe, "ssm")
                pe.wait_ge(rs_ready, 1)
                head_spread(e_rt, e_rt[:, 1:5, :], range(5), 1)

                def bu(c):
                    if c >= 2:
                        pe.wait_ge(bu_used, c - 1)
                    lo = 32 * (c % 4)
                    for part in range(2):
                        mm = pe.matmul(ps[:, 6 + c % 2, part * T:(part + 1) * T],
                                       e_B[lo:lo + 32, part, c // 4, :], e_uT[lo:lo + 32, c // 4, :],
                                       start=True, stop=True)
                    mm.then_inc(bu_done, 1)

                def y(c):
                    pe.wait_ge(back, c + 1)
                    if c == 0:
                        pe.wait_ge(cw_ready, 1)
                    lo = 32 * (c % 4)
                    for part in range(2):
                        mm = pe.matmul(ps[lo:lo + 32, 4 + (c // 4) % 2, 0:T], e_CW[:, part, c, :],
                                       e_h[:, c % 4, part, :], start=(part == 0),
                                       stop=(part == 1), skip_group_check=True)
                    mm.then_inc(y_done, 1)

                small_wait(pe, "ssm")
                bu(0)
                bu(1)
                attention(0, e_qk, EVEN_HEADS)
                for c in range(SG):
                    if c >= 4 and c % 4 == 0 and c >= 8:
                        pe.wait_ge(y_sum, c // 4 - 1)
                    if c == 0:
                        pe.wait_ge(evac, nproj[0])
                    if c + 2 < SG:
                        bu(c + 2)
                    y(c)
                    if c == 6:
                        attention_out(0, EVEN_HEADS, e_v, e_S, e_PT)
                    if 10 <= c < 14:
                        if c == 10:
                            pe.wait_ge(pv_out, 4)
                        out_rows(0, "even", [c - 10], slots=EVEN_SLOTS)
                pe.wait_ge(y_low, 4)
                for s in range(2):
                    w = split(AT[("even", "glu", s)])
                    for j in range(2):
                        for c in range(4):
                            cols = slice(c * T + j * P, c * T + (j + 1) * P)
                            mm = mm3(ps[:, 4 + s, j * T:(j + 1) * T], w[0][:, cols], w[1][:, cols],
                                     hT_hi[:, c, :], hT_lo[:, c, :], c == 0, c == 3)
                    mm.then_inc(strip_done, 1)
                out_rows(0, "even", range(4, 8), slots=EVEN_SLOTS)

            def mlp(n, name):
                base = AT[(name, "gate", 0)]

                def gate_up(strip, bank, i=None, fresh=None):
                    for part in range(2):
                        strip_fm(ps[:, bank + 2 * part, 0:T], split(strip + part, i),
                                 None if part else fresh)

                def down(strip, c, i=None):
                    w = split(strip, i)
                    pe.wait_ge(ff_ready, FC * n + c + 1 if i is None else 2 * i + (FC * n + c + 1))
                    first = i is None and c == 0
                    rows(w, a_hi[:, c % 2, :], a_lo[:, c % 2, :], first, i is None and c == FC - 1)

                def chunk_pair(i=None):
                    for u in range(2):
                        gate_up(base + 2 + 3 * u, 4 + (1 + u) % 2, i)
                        down(base + 4 + 3 * u, u, i)

                gate_up(base, 4, fresh=STAGE_OF[name])
                chunk_pair()
                with pe.Fori(1, (FC - 2) // 2) as i:
                    chunk_pair(i)
                last = base + 2 + 3 * (FC - 2)
                gate_up(last, 4 + (FC - 1) % 2)
                down(last + 2, FC - 2)
                down(last + 3, FC - 1)

            def odd():
                for g in range(4):
                    proj_tm_pair(("odd", "v"), g, None if g else 2)

                def z(j):
                    pe.wait_ge(evac, nproj[0])
                    if j >= 2:
                        pe.wait_ge(w_masked, j - 1)
                    for h in (2 * j, 2 * j + 1):
                        lo = HD * (h % 2)
                        pe.matmul(ps[:, h % 4, 0:T], o_kT[lo:lo + HD, j, 0:P], o_qT[lo:lo + HD, j, :],
                                  start=True, stop=True, skip_group_check=True)
                        mm = pe.matmul(ps[:, h % 4, T:3 * P], o_kT[lo:lo + HD, j, P:T],
                                       o_qT[lo:lo + HD, j, P:T], start=False, stop=True,
                                       skip_group_check=True)
                    mm.then_inc(z_done, 1)

                def cum(j):
                    pe.wait_ge(sp_masked, j + 1)
                    for h in (2 * j, 2 * j + 1):
                        pe.matmul(ps[:, h % 4, 0:3 * P], k("neg_tri"), o_sp[:, h % 4, :], start=False,
                                  stop=False, skip_group_check=True)
                        mm = pe.matmul(ps[:, h % 4, P:T], k("neg_ones"), o_sp[:, h % 4, T:3 * P],
                                       start=False, stop=True, skip_group_check=True)
                    mm.then_inc(cum_done, 1)

                def ov(j):
                    pe.wait_ge(w_ready, j + 1)
                    if j >= 2:
                        pe.wait_ge(ov_out, j - 1)
                    for h in (2 * j, 2 * j + 1):
                        o = ps[HD * (h % 2):HD * (h % 2) + HD, 6 + j % 2, 0:T]
                        pe.matmul(o, o_v[:, 0, h * HD:(h + 1) * HD], o_w[:, h % 4, 0:T], start=True,
                                  stop=False, skip_group_check=True)
                        mm = pe.matmul(o[:, P:T], o_v[:, 1, h * HD:(h + 1) * HD], o_w[:, h % 4, T:3 * P],
                                       start=False, stop=True, skip_group_check=True)
                    mm.then_inc(ov_done, 1)

                for j in range(9):
                    if j < 8:
                        proj_fm(("odd", "q", j))
                        proj_fm(("odd", "k", j))
                    if j >= 2:
                        ov(j - 2)
                    if j >= 1:
                        cum(j - 1)
                    if j < 8:
                        z(j)
                pe.wait_ge(w_masked, 8)
                out_rows(1, "odd", range(2))
                ov(7)
                out_rows(1, "odd", range(2, KC))

            def mix():
                proj_fm(("mix", "if", 0), 4)
                for j in range(4):
                    proj_fm(("mix", "u", j))
                for g in range(2):
                    proj_tm_pair(("mix", "vm"), g)
                pe.wait_ge(rows_ready, 1)
                for n in range(3):
                    mm = pe.transpose(ps[:, 7, n * MH:(n + 1) * MH],
                                      m_row[0:MH, 7 if n == 2 else 3, (n % 2) * P:(n % 2 + 1) * P],
                                      ident[0:MH, 0:MH])
                mm.then_inc(cols_done, 1)
                small_wait(pe, "mix")
                for h in range(MH):
                    pe.wait_ge(conv_silu, h + 1)
                    for part in range(2):
                        mm = pe.matmul(ps[:, h, part * T:(part + 1) * T], m_wqk[:, part, h, :],
                                       m_cT[:, h, :], start=True, stop=True)
                    mm.then_inc(qkm_done, 1)
                for n in ("qa", "ka"):
                    for j in range(4):
                        proj_fm(("mix", n, j))
                for g in range(2):
                    proj_tm_pair(("mix", "va"), g)
                    if g == 0:
                        pe.wait_ge(sq_ready, 2)
                        head_sums(m_sq, 8, 6)
                pe.wait_ge(rs_ready, 2)
                pe.wait_ge(cols_out, 1)
                head_spread(m_rt, m_rt[:, 4:8, :], range(4), 6)
                for j in range(4):
                    proj_fm(("mix", "z", j))
                    if j == 0:
                        pe.wait_ge(rt_used, 2)
                        head_spread(m_rt, m_rt[:, 4:8, :], range(4, 8), 6)
                    if j == 1:
                        pe.wait_ge(qkm_out, MH)
                        attention(1, m_qk, MIX_HEADS)
                pe.wait_ge(score_out, 2 * NH)
                for h in range(MH):
                    pe.matmul(ps[:, h, :], k("head_row", h * P, (h + 1) * P)[0:MH],
                              m_row[0:MH, 4:6, :].rearrange("p a b -> p (a b)"), start=True,
                              stop=True).then_inc(bcast_done, 1)
                for h in range(MH):
                    b = 6 + h % 2
                    if h == 0:
                        pe.wait_ge(rt_used, 3)
                    if h >= 2:
                        pe.wait_ge(s_ready, h - 1)
                    pe.matmul(ps[:, b, 0:T], m_km[:, h, 0:P], m_qm[:, h, :], start=True, stop=True)
                    pe.matmul(ps[:, b, T:3 * P], m_km[:, h, P:T], m_qm[:, h, P:T], start=True,
                              stop=True).then_inc(st_done, 1)
                for h in range(MH):
                    pe.wait_ge(s_ready, h + 1)
                    if h == 0:
                        pe.wait_ge(evac, nproj[0])
                        pe.wait_ge(em_out, MH)
                    vh = m_vm[:, :, h * P:(h + 1) * P]
                    for at, l0, l1 in ((0, vh[:, 0, :], vh[:, 1, :]), (T, ones, ones)):
                        pe.matmul(ps[:, 4 + h, at:at + T], l0, m_s[:, h, 0:T], start=(at == 0), stop=False,
                                  skip_group_check=True)
                        mm = pe.matmul(ps[:, 4 + h, at + P:at + T], l1, m_s[:, h, T:3 * P], start=False,
                                       stop=True, skip_group_check=True)
                    mm.then_inc(num_done, 1)
                attention_out(1, MIX_HEADS, m_va, m_S, m_PT)
                pe.wait_ge(pv_out, 8)
                out_rows(2, "mix", range(3), MIX_ORDER)
                pe.wait_ge(hm_sq, 1)
                for h in range(MH):
                    mm = pe.matmul(ps[0:MH, 4, 0:T], k("all_sel", MH * h, MH * h + MH), m_dn[:, h, :],
                                   start=(h == 0), stop=(h == MH - 1))
                mm.then_inc(hm_summed, 1)
                out_rows(2, "mix", [3], MIX_ORDER)
                pe.wait_ge(rs_ready, 3)
                for h in range(MH):
                    mm = pe.matmul(ps[:, 4 + h // 2, (h % 2) * T:(h % 2 + 1) * T],
                                   k("head_row", h * P, (h + 1) * P)[0:MH], m_row[0:MH, 9, :], start=True,
                                   stop=True)
                mm.then_inc(hm_wide, 1)
                out_rows(2, "mix", range(4, KC), MIX_ORDER)

            def peer():
                first = nproj[0]
                small_wait(pe, "keys")

                def key_scores(s):
                    pe.wait_ge(evac, first + s + 1)
                    if s >= 2:
                        pe.wait_ge(key_out, s - 1)
                    for a in range(NT):
                        mm = pe.matmul(ps[:, 6 + s % 2, a * P:(a + 1) * P],
                                       r_q[:, s % 2, a * P:(a + 1) * P],
                                       keys_s[:, s % 2, (s // 2) * P:(s // 2 + 1) * P],
                                       start=True, stop=True)
                    mm.then_inc(key_done, 1)

                for s in range(2 * PH):
                    proj_fm(("peer", "q", s), None if s else 5)
                    if s:
                        key_scores(s - 1)
                key_scores(2 * PH - 1)
                pe.wait_ge(evac, nproj[0])
                base = AT[("peer", "u", 0)]

                def up(e, i=None):
                    w = split(base + e, i)
                    if i is not None:
                        pe.wait_ge(gelu_done, UNROLL * i + (e - 1))
                    elif e >= 2:
                        pe.wait_ge(gelu_done, e - 1)
                    strip_fm(ps[:, 4 + e % 2, 0:T], w)

                def scatter(half, g, i=None):
                    at = HALF * half + g
                    count = lambda v: at + v if i is None else UNROLL * i + (at + v)
                    pe.wait_ge(onehot_ready, count(1))
                    pe.wait_ge(gate_free, count(1))
                    for q in range(4):
                        for part in range(3):
                            mm = pe.matmul(ps[:, 6 + g % 2, q * HALF:(q + 1) * HALF],
                                           oh_second[:, g % 2, q, :], oh_gate[:, g % 2, q, part, :],
                                           start=(part == 0), stop=(part == 2))
                    mm.then_inc(spread, 1)

                for e in range(UNROLL):
                    up(e)
                with pe.Fori(1, HALF // UNROLL) as i:
                    for e in range(UNROLL):
                        up(e, i)
                for e in range(HALF // UNROLL * UNROLL, HALF):
                    up(e)
                pe.wait_ge(route_ready, 1)
                for n in range(3):
                    for a in range(NT):
                        mm = pe.transpose(ps[:, 6 + n // 2, (n % 2) * T + a * P:(n % 2) * T + (a + 1) * P],
                                          xn[:, 0, n * T + a * P:n * T + (a + 1) * P], ident)
                mm.then_inc(eT_done, 1)

                def up_and_gate(e, i):
                    up(e, i)
                    scatter(0, e - HALF, i)

                half_tiles(pe, HALF, up_and_gate)
                for c in range(KC):
                    for a in range(NT):
                        pe.matmul(ps[:, c // 2, (c % 2) * T + a * P:(c % 2) * T + (a + 1) * P],
                                  x_s[:, a, c * P:(c + 1) * P], ident, start=(c % 2 == 0 and a == 0),
                                  stop=False, skip_group_check=True)
                base = AT[("peer", "v", 0)]

                def down(e, i=None):
                    w = split(base + e, i)
                    pe.wait_ge(ff_ready, 2 * FC + e + 1 if i is None else UNROLL * i + (2 * FC + e + 1))
                    for c in range(KC):
                        cols = slice(c * P, (c + 1) * P)
                        mm = mm3(ps[:, c // 2, (c % 2) * T:(c % 2 + 1) * T], w[0][:, cols],
                                 w[1][:, cols], a_hi[:, e % 2, :], a_lo[:, e % 2, :], False,
                                 e == NE1 - 1, skip_group_check=True)
                    mm.then_inc(strip_done, 1)

                def down_and_gate(e, i):
                    down(e, i)
                    scatter(1, e, i)

                half_tiles(pe, 0, down_and_gate)
                half_tiles(pe, HALF, down)
                pe.wait_ge(yT_out, 2)
                for c in range(KC):
                    for a in range(NT):
                        mm = pe.transpose(ps[:, 4 + 2 * a + c // 4, (c % 4) * P:(c % 4 + 1) * P],
                                          xn[:, c // 4, (c % 4) * T + a * P:(c % 4) * T + (a + 1) * P], ident)
                mm.then_inc(out_turned, 1)

            small_wait(pe, "x")
            for n, (name, body) in enumerate([("even", even), ("mlp0", lambda: mlp(0, "mlp0")),
                                              ("odd", odd), ("mlp1", lambda: mlp(1, "mlp1")),
                                              ("mix", mix), ("peer", peer)]):
                norm(n)
                body()

        @block.scalar
        def _(sc):
            small_load(sc, "x", x_s[:, :, :], A["x"].rearrange("b (a p) d -> p (b a) d", p=P))
            small_load(sc, "first", const[:, 0:N_FIRST], A["const"][:, 0:N_FIRST])
            small_load(sc, "param", param[:, :], A["param"])
            small_load(sc, "const", const[:, N_FIRST:], A["const"][:, N_FIRST:])
            small_load(sc, "ssm", e_B.rearrange("p a b c -> p (a b c)"), A["ssm_b"])
            small_load(sc, "ssm", e_C.rearrange("p a b c -> p (a b c)"), A["ssm_c"])
            small_load(sc, "ssm", e_rt[0:16, 1:5, :].rearrange("p a b -> p (a b)"), A["head_rows"])
            ch = Chain(sc, act_chain)
            nproj = [0]
            split = [0]

            def high(n, i=None):
                sc.wait_ge(strip_landed[n % RING], 16 * (n // RING + 1) if i is None
                           else 32 * i + 16 * (n // RING + 1))
                if i is not None:
                    sc.wait_ge(strip_done, UNROLL * i + (n + 1 - RING))
                elif n >= RING:
                    sc.wait_ge(strip_done, n + 1 - RING)
                sc.activation(w_hi[:, n % RING, :], ring[:, n % RING, :], ACT.Copy).then_inc(high_ready, 1)

            def high_to(n):
                for m in range(split[0], min(n + 1, NS)):
                    high(m)
                split[0] = max(split[0], n + 1)

            def mix_split(i, mixT, js, slots=range(KC)):
                for j in js:
                    sc.activation(hT_hi[:, slots[j], :], mixT[:, j, :], ACT.Copy).then_inc(mix_high, 1)

            def norm(i):
                if i == 0:
                    small_wait(sc, "x")
                    small_wait(sc, "first")
                    small_wait(sc, "param")
                first = 0 if i == 0 else AT[LASTS[i - 1]] + 1
                ch.add(sc.activation(stat[:, 6:7], k("eps"), ACT.Sqrt))
                high_to(first + (1 if i else RING - 1))
                for a in range(NT):
                    if i:
                        sc.wait_ge(x_ready, 4 * (i - 1) + 2 * (a + 1))
                    ch.link(sc.activation(xn[:, a, :], x_s[:, a, :], ACT.Square, accum_out=stat[:, a:a + 1]))
                    sc.activation(stat[:, 2 + a:3 + a], stat[:, a:a + 1], ACT.Sqrt, bias=k("eps"),
                                  scale=1.0 / D).then_inc(roots, 1)
                if i == 3:
                    small_load(sc, "mix", m_bias.rearrange("p a b -> p (a b)"), A["rel"])
                    small_load(sc, "mix", m_wqk.rearrange("p a b c -> p (a b c)"), A["wqk"])
                    small_load(sc, "mix", m_rt[0:16, 4:8, :].rearrange("p a b -> p (a b)"), A["head_rows"])
                if i == 5:
                    small_load(sc, "keys", keys_s.rearrange("p a b -> p (a b)"), A["keys"])
                for c in range(KC // 2):
                    sc.wait_ge(turned, 4 * i + c + 1)
                    for cc in range(2):
                        ins = sc.activation(hT_hi[:, 2 * c + cc, :], ps[:, norm_bank(i, c), cc * T:(cc + 1) * T],
                                            ACT.Copy, scale=prm(NORMS[i], 2 * c + cc, 2 * c + cc + 1))
                    ins.then_inc(hT_high, 1)
                high_to(first + RING - 1)

            def out_of(name, dst, src=None, func=ACT.Copy, width=T, **kw):
                high_to(AT[name] + RING - 1)
                sc.wait_ge(strip_done, AT[name] + 1)
                b = 4 + nproj[0] % 2
                nproj[0] += 1
                sc.activation(dst, ps[:, b, 0:width] if src is None else src(b), func, **kw).then_inc(evac, 1)

            def out_of_pair(name, g, dst):
                out_of(name + (2 * g + 1,), dst[:, :, g * T:(g + 1) * T],
                       lambda b: ps[:, b, :].rearrange("p (a c) -> p a c", a=NT))

            def softmax(t, S, sm, sink):
                sc.wait_ge(shifted, t + 1)
                f = S.rearrange("p a b -> p (a b)")
                if sink:
                    ch.add(sc.activation(sm[:, 2, :], sm[:, 2, :], ACT.Exp))
                sc.activation(f, f, ACT.Exp).then_inc(exp_done, 1)

            def attention_out(t, pT, mixT, at):
                for n in range(NH):
                    sc.wait_ge(pT_done, NH * t + n + 1)
                    sc.activation(pT[:, n, :], ps[:, n % 4, 0:3 * P], ACT.Copy).then_inc(pT_out, 1)
                for j in range(4):
                    sc.wait_ge(pv_done, 4 * t + j + 1)
                    sc.activation(mixT[:, at + j, :], ps[:, j % 2, 0:T], ACT.Copy).then_inc(pv_out, 1)

            def even():
                sc.activation(e_p[:, 0, :], prm("log_dt"), ACT.Exp).then_inc(prm_act, 1)
                sc.wait_ge(prm_dve, 1)
                sc.activation(e_p[:, 3, :], e_p[:, 1, :], ACT.Exp).then_inc(prm_act, 1)
                sc.wait_ge(prm_dve, 2)
                sc.activation(e_p[:, 9, :], e_p[:, 6, :], ACT.Sin).then_inc(prm_act, 1)
                sc.activation(e_p[:, 10, :], e_p[:, 7, :], ACT.Sin).then_inc(prm_act, 1)
                for j in range(4):
                    out_of(("even", "u", j), e_uT[:, j, :])
                out_of(("even", "k", 0), e_qk[:, 4, :])
                for j in range(4):
                    out_of(("even", "q", j), e_qk[:, j, :])
                out_of(("even", "v", 0), e_v.rearrange("p a b -> p (a b)"))
                sc.wait_ge(sq_summed, 1)
                sc.activation(e_rt[0:16, 0, :], ps[0:16, 0, 0:T], ACT.Sqrt, bias=k("eps")[0:16],
                              scale=1.0 / HD).then_inc(rt_ready, 1)
                softmax(0, e_S, e_sm, True)
                attention_out(0, e_PT, e_mixT, 0)
                sc.wait_ge(pv_out, 4)
                mix_split(0, e_mixT, range(4), EVEN_SLOTS)
                high_to(AT[("even", "out", 2)])
                for j in range(4):
                    sc.wait_ge(y_sum, j + 1)
                    sc.activation(e_y[:, j, :], e_y[:, j, :], ACT.Gelu_apprx_tanh).then_inc(y_gelu, 1)
                    if j == 0:
                        high_to(AT[("even", "glu", 1)])
                sc.wait_ge(y_gelu, 4)
                for j in range(4):
                    sc.activation(hT_hi[:, j, :], e_y[:, j, :], ACT.Copy).then_inc(y_high, 1)
                high_to(AT[("even", "out", 4)])
                for s in range(2):
                    sc.wait_ge(strip_done, AT[("even", "glu", s)] + 1)
                    for j in range(2):
                        sc.activation(e_sq[:, 2 * s + j, :], ps[:, 4 + s, j * T:(j + 1) * T], ACT.Sigmoid,
                                      bias=prm("b_glu", 2 * s + j, 2 * s + j + 1)).then_inc(glu_sig, 1)
                    high_to(AT[("even", "out", 5 + s)])
                    sc.wait_ge(glu_out, s + 1)
                    mix_split(0, e_mixT, range(4 + 2 * s, 6 + 2 * s), EVEN_SLOTS)
                high_to(AT[("even", "out", 7)])

            def mlp(n, name):
                base = AT[(name, "gate", 0)]

                def silu(strip, c, i=None):
                    sc.wait_ge(strip_done, strip + 1 if i is None else UNROLL * i + (strip + 1))
                    sc.activation(f_silu[:, c % 2, :], ps[:, 4 + c % 2, 0:T], ACT.Silu).then_inc(silu_ready, 1)

                silu(base, 0)
                high_to(base + 3)
                with sc.Fori(0, (FC - 2) // 2) as i:
                    for u in range(2):
                        at = base + 2 + 3 * u
                        high(at + 2, i)
                        silu(at, 1 + u, i)
                        high(at + 3, i)
                        high(at + 4, i)
                split[0] = base + 2 + 3 * (FC - 2) + 2
                at = base + 2 + 3 * (FC - 2)
                high_to(at + 2)
                silu(at, FC - 1)
                high_to(at + 3)

            def odd():
                for g in range(4):
                    out_of_pair(("odd", "v"), g, o_v)

                def softplus(j):
                    sc.wait_ge(z_done, j + 1)
                    if j:
                        sc.wait_ge(sp_ready, j)
                    ch.link(sc.activation(o_t, ps[:, 2 * (j % 2):2 * (j % 2) + 2, 0:3 * P], ACT.Abs))
                    ch.link(sc.activation(o_t, o_t, ACT.Exp, scale=-1.0))
                    sc.activation(o_t, o_t, ACT.Ln, bias=1.0).then_inc(z_log, 1)

                def weights(j):
                    sc.wait_ge(w_masked, j + 1)
                    if j >= 2:
                        sc.wait_ge(ov_done, j - 1)
                    at = 2 * (j % 2)
                    sc.activation(o_w[:, at:at + 2, :], o_w0[:, at:at + 2, :], ACT.Exp).then_inc(w_ready, 1)

                def ov_copy(j):
                    sc.wait_ge(ov_done, j + 1)
                    sc.activation(o_mixT[:, j, :], ps[:, 6 + j % 2, 0:T], ACT.Copy).then_inc(ov_out, 1)

                for j in range(8):
                    out_of(("odd", "q", j), o_qT[:, j, :], scale=HD ** -0.5)
                    out_of(("odd", "k", j), o_kT[:, j, :])
                    if j:
                        weights(j - 1)
                    softplus(j)
                    if j >= 2:
                        ov_copy(j - 2)
                sc.wait_ge(ov_out, 6)
                mix_split(1, o_mixT, range(6))
                weights(7)
                high_to(AT[("odd", "out", 1)])
                ov_copy(6)
                ov_copy(7)
                sc.wait_ge(ov_out, 8)
                mix_split(1, o_mixT, range(6, KC))
                high_to(AT[("odd", "out", 7)])

            def mix():
                r = m_row[0:MH]
                high_to(AT[("mix", "if", 0)] + RING - 1)
                sc.wait_ge(strip_done, AT[("mix", "if", 0)] + 1)
                b = 4 + nproj[0] % 2
                nproj[0] += 1
                ch.add(sc.activation(r[:, 0, :], ps[0:MH, b, 0:T], ACT.Identity, bias=prm("ig_b")[0:MH]))
                sc.activation(r[:, 1, :], ps[FG_AT:FG_AT + MH, b, 0:T], ACT.Identity,
                              bias=prm("fg_b")[FG_AT:FG_AT + MH]).then_inc(evac, 1)
                sc.wait_ge(evac, nproj[0])
                ch.link(sc.activation(r[:, 2, :], r[:, 1, :], ACT.Abs))
                ch.link(sc.activation(r[:, 2, :], r[:, 2, :], ACT.Exp, scale=-1.0))
                sc.activation(r[:, 2, :], r[:, 2, :], ACT.Ln, bias=1.0).then_inc(gate_act, 1)
                for j in range(4):
                    out_of(("mix", "u", j), m_up[:, j, 3:T + 3])
                for g in range(2):
                    out_of_pair(("mix", "vm"), g, m_vm)
                sc.wait_ge(cols_done, 1)
                sc.activation(m_rc.rearrange("p a b -> p (a b)"), ps[:, 7, 0:3 * MH],
                              ACT.Copy).then_inc(cols_out, 1)
                for j in range(4):
                    sc.wait_ge(conv_done, j + 1)
                    sc.activation(m_cT[:, j, :], m_cv[:, j, :], ACT.Silu).then_inc(conv_silu, 1)
                for h in range(MH):
                    sc.wait_ge(qkm_done, h + 1)
                    ch.add(sc.activation(m_qm[:, h, :], ps[:, h, 0:T], ACT.Copy))
                    sc.activation(m_km[:, h, :], ps[:, h, T:2 * T], ACT.Copy,
                                  scale=P ** -0.5).then_inc(qkm_out, 1)
                for n, at in (("qa", 0), ("ka", 4)):
                    for j in range(4):
                        out_of(("mix", n, j), m_qk[:, at + j, :])
                out_of_pair(("mix", "va"), 0, m_va)
                sc.wait_ge(sq_summed, 2)
                sc.activation(m_rt[0:16, 0, :], ps[0:16, 6, 0:T], ACT.Sqrt, bias=k("eps")[0:16],
                              scale=1.0 / HD).then_inc(rt_ready, 1)
                out_of_pair(("mix", "va"), 1, m_va)
                for j in range(4):
                    out_of(("mix", "z", j), m_sz[:, j, :], func=ACT.Sigmoid)
                softmax(1, m_S, m_sm, False)
                sc.wait_ge(cols_out, 1)
                for h in range(MH):
                    sc.wait_ge(expo_in, h + 1)
                    for n, col in ((0, 0), (1, 2), (2, 1)):
                        ins = sc.activation(m_d[:, h, n * P:(n + 1) * P], m_x[:, h, n * P:(n + 1) * P],
                                            ACT.Exp, bias=m_rc[:, col, h:h + 1])
                        if n < 2:
                            ch.add(ins)
                    ins.then_inc(expo_out, 1)
                    sc.activation(m_em[:, h, :], ps[:, h, T:2 * T], ACT.Exp, scale=-1.0).then_inc(em_out, 1)
                for h in range(MH):
                    sc.wait_ge(num_done, h + 1)
                    sc.activation(m_dn[:, h, :], ps[:, 4 + h, T:2 * T], ACT.Abs).then_inc(den_abs, 1)
                attention_out(1, m_PT, m_mixT, 4)
                sc.wait_ge(pv_out, 8)
                mix_split(2, m_mixT, MIX_ORDER[:4])
                high_to(AT[("mix", "out", MIX_ORDER[4])])
                sc.wait_ge(hm_summed, 1)
                sc.activation(r[:, 9, :], ps[0:MH, 4, 0:T], ACT.Sqrt, bias=k("eps")[0:MH],
                              scale=1.0 / P).then_inc(rt_ready, 1)
                high_to(AT[("mix", "out", MIX_ORDER[5])])
                sc.wait_ge(ym_ready, 1)
                mix_split(2, m_mixT, MIX_ORDER[4:])
                high_to(AT[("mix", "out", MIX_ORDER[7])])

            def peer():
                def key_copy(s):
                    sc.wait_ge(key_done, s + 1)
                    sc.activation(r_sc[:, s].rearrange("p a b -> p (a b)"), ps[:, 6 + s % 2, 0:T],
                                  ACT.Copy).then_inc(key_out, 1)

                for s in range(2 * PH):
                    if s >= 2:
                        sc.wait_ge(key_done, s - 1)
                    out_of(("peer", "q", s), r_q[:, s % 2, :])
                    if s:
                        key_copy(s - 1)
                key_copy(2 * PH - 1)
                base = AT[("peer", "u", 0)]

                def gelu(e, i=None):
                    n = base + e
                    high(n + RING - 1, i)
                    sc.wait_ge(strip_done, n + 1 if i is None else UNROLL * i + (n + 1))
                    dst = act[:, e, :] if i is None else act[:, bass.ds(UNROLL * i + e, 1), :].rearrange(
                        "p a t -> p (a t)")
                    sc.activation(dst, ps[:, 4 + e % 2, 0:T], ACT.Gelu).then_inc(gelu_done, 1)

                high_to(base + RING - 2)
                with sc.Fori(0, EXP_AT) as i:
                    for e in range(UNROLL):
                        gelu(e, i)
                sc.wait_ge(route_dve, 1)
                f = r_e[:, 2, :]
                sc.activation(f, f, ACT.Exp).then_inc(route_act, 1)
                with sc.Fori(EXP_AT, HALF // UNROLL) as i:
                    for e in range(UNROLL):
                        gelu(e, i)
                for e in range(HALF // UNROLL * UNROLL, HALF):
                    gelu(e)
                sc.wait_ge(route_ready, 1)
                half_tiles(sc, HALF, gelu)
                base = AT[("peer", "v", 0)]

                def value_high(e, i=None):
                    high(base + e + 2, i)
                    act_high(e + 1, i)

                def act_high(e, i=None):
                    src = act[:, e, :] if i is None else act[:, bass.ds(UNROLL * i + e, 1), :].rearrange(
                        "p a t -> p (a t)")
                    sc.activation(a_hi[:, e % 2, :], src, ACT.Copy).then_inc(a_high, 1)

                sc.wait_ge(gate_free, HALF + 2)
                act_high(0)
                half_tiles(sc, 0, value_high, 1)
                high(base + HALF + 1)
                sc.wait_ge(gate_free, NE1 + 2)
                act_high(HALF)
                half_tiles(sc, HALF, value_high, 2)
                sc.wait_ge(strip_done, base + NE1 - 2)
                act_high(NE1 - 1)
                sc.wait_ge(strip_done, AT[LASTS[5]] + 1)
                sc.activation(xn[:, 1, :], ps[:, 2:4, :].rearrange("p a b -> p (a b)"),
                              ACT.Copy).then_inc(yT_out, 1)

            for n, body in enumerate([even, lambda: mlp(0, "mlp0"), odd, lambda: mlp(1, "mlp1"), mix,
                                      peer]):
                norm(n)
                body()

        @block.vector
        def _(ve):
            ch = Chain(ve, dve_chain)

            def tt(o, a, b, op):
                return ve.tensor_tensor(o, a, b, op)

            def low(n, i=None):
                ve.wait_ge(high_ready, n + 1 if i is None else UNROLL * i + (n + 1))
                tt(w_lo[:, n % RING, :], ring[:, n % RING, :], w_hi[:, n % RING, :].bitcast(F32),
                   ALU.subtract).then_inc(low_ready, 1)

            def mix_split(i, mixT, ns=range(KC), order=range(KC), slots=range(KC)):
                for n in ns:
                    j = order[n]
                    ve.wait_ge(mix_high, KC * i + n + 1)
                    tt(hT_lo[:, slots[j], :], mixT[:, j, :], hT_hi[:, slots[j], :].bitcast(F32),
                       ALU.subtract).then_inc(mix_low, 1)

            def norm(i):
                if i:
                    for a in range(NT):
                        if a == 0:
                            ve.wait_ge(first_half, i)
                        else:
                            ve.wait_ge(strip_done, AT[LASTS[i - 1]] + 1)
                        for b in range(2):
                            v = x_s[:, a, b * 512:(b + 1) * 512]
                            tt(v, v, ps[:, 2 * a + b, :], ALU.add).then_inc(x_ready, 1)
                else:
                    small_wait(ve, "x")
                    small_wait(ve, "first")
                    small_wait(ve, "param")
                for a in range(NT):
                    ve.wait_ge(roots, NT * i + a + 1)
                    ch.link(ve.reciprocal(stat[:, 4 + a:5 + a], stat[:, 2 + a:3 + a]))
                    ve.tensor_scalar(scale_diag[:, a, :], ident, stat[:, 4 + a:5 + a], None,
                                     ALU.mult).then_inc(diag_ready, 1)
                for c in range(KC // 2):
                    ve.wait_ge(hT_high, 4 * i + c + 1)
                    for cc in range(2):
                        j = 2 * c + cc
                        ins = ve.scalar_tensor_tensor(out=hT_lo[:, j, :], in0=ps[:, norm_bank(i, c), cc * T:(cc + 1) * T],
                                                      scalar=prm(NORMS[i], j, j + 1),
                                                      in1=hT_hi[:, j, :].bitcast(F32), op0=ALU.mult,
                                                      op1=ALU.subtract)
                    ins.then_inc(hT_low, 1)

            def bc(a, axis, shape):
                return a.unsqueeze(axis).broadcast_to(shape)

            def invert(n, rows):
                ve.wait_ge(rt_ready, n)
                ve.reciprocal(rows, rows).then_inc(rs_ready, 1)

            def head_norm(t, qk, gains, bank):
                ve.wait_ge(rt_wide, t)
                for n, (c, g) in enumerate(gains):
                    ins = ve.scalar_tensor_tensor(out=qk[:, c, :], in0=qk[:, c, :], scalar=g,
                                                  in1=ps[:, bank + n // 2, (n % 2) * T:(n % 2 + 1) * T],
                                                  op0=ALU.mult, op1=ALU.mult)
                ins.then_inc(rt_used, 1)

            def softmax_in(t, S, sm, masks, sink):
                for n in range(NH):
                    ve.wait_ge(score_done, NH * t + n + 1)
                    lo, hi = masks(n)
                    ch.add(ve.scalar_tensor_tensor(out=S[:, n, 0:P], in0=ps[:, n % 4, 0:P],
                                                   scalar=HD ** -0.5, in1=lo, op0=ALU.mult, op1=ALU.add))
                    ve.scalar_tensor_tensor(out=S[:, n, P:3 * P], in0=ps[:, n % 4, P:3 * P],
                                            scalar=HD ** -0.5, in1=hi, op0=ALU.mult,
                                            op1=ALU.add).then_inc(score_out, 1)
                ve.wait_ge(score_out, NH * (t + 1))
                parts = ((S[:, :, 0:P], 0, P), (S[:, :, P:3 * P], NH, 2 * P))
                for s, at, w in parts:
                    ch.add(ve.tensor_reduce(sm[:, 0, at:at + NH], s, AX, ALU.max))
                ch.wait()
                if sink is not None:
                    m = sm[:, 0, :].rearrange("p (a h) -> p a h", a=2)
                    ch.link(tt(m, m, bc(sink, 1, [P, 2, NH]), ALU.max))
                    ch.add(tt(sm[:, 2, :].rearrange("p (a h) -> p a h", a=2),
                              bc(sink, 1, [P, 2, NH]), m, ALU.subtract))
                s, at, w = parts[0]
                ch.add(tt(s, s, bc(sm[:, 0, at:at + NH], 2, [P, NH, w]), ALU.subtract))
                s, at, w = parts[1]
                tt(s, s, bc(sm[:, 0, at:at + NH], 2, [P, NH, w]), ALU.subtract).then_inc(shifted, 1)

            def softmax_out(t, S, sm, count, sink):
                ve.wait_ge(exp_done, t + 1)
                if count is not None:
                    ch.link(tt(S, S, bc(count, 1, [P, NH, 3 * P]), ALU.mult))
                parts = ((S[:, :, 0:P], 0, P), (S[:, :, P:3 * P], NH, 2 * P))
                for s, at, w in parts:
                    ch.add(ve.tensor_reduce(sm[:, 1, at:at + NH], s, AX, ALU.add))
                ch.wait()
                if sink:
                    ch.link(tt(sm[:, 1, :], sm[:, 1, :], sm[:, 2, :], ALU.add))
                ch.link(ve.reciprocal(sm[:, 3, :], sm[:, 1, :]))
                for s, at, w in parts:
                    ins = tt(s, s, bc(sm[:, 3, at:at + NH], 2, [P, NH, w]), ALU.mult)
                    if at == 0:
                        ch.add(ins)
                ins.then_inc(probs, 1)

            def even():
                small_wait(ve, "const")
                small_wait(ve, "ssm")
                p = lambda n: e_p[:, n, :]
                ve.wait_ge(prm_act, 1)
                ch.add(tt(p(2), prm("a_im"), p(0), ALU.mult))
                tt(p(1), prm("a_re"), p(0), ALU.mult).then_inc(prm_dve, 1)
                ve.wait_ge(prm_dve, 1)
                ch.link(ve.tensor_scalar(p(4), p(2), INV_2PI, None, ALU.mult))
                ch.link(ve.tensor_scalar(p(4), p(4), ROUND, None, ALU.add))
                ch.link(ve.tensor_scalar(p(4), p(4), -ROUND, None, ALU.add))
                ch.link(ve.scalar_tensor_tensor(out=p(5), in0=p(4), scalar=-C1, in1=p(2), op0=ALU.mult, op1=ALU.add))
                ch.link(ve.scalar_tensor_tensor(out=p(5), in0=p(4), scalar=-C2, in1=p(5), op0=ALU.mult, op1=ALU.add))
                ch.add(ve.tensor_scalar(p(6), p(5), PI_LO, -PI_LO, ALU.min, ALU.max))
                ch.link(ve.tensor_scalar(p(7), p(5), TWO_PI / 4, None, ALU.add))
                ch.link(ve.tensor_scalar(p(8), p(7), TWO_PI / 2, -TWO_PI, ALU.is_gt, ALU.mult))
                ch.link(tt(p(7), p(7), p(8), ALU.add))
                ve.tensor_scalar(p(7), p(7), PI_LO, -PI_LO, ALU.min, ALU.max).then_inc(prm_dve, 1)
                ve.wait_ge(prm_act, 4)
                ch.add(tt(p(11), p(3), p(10), ALU.mult))
                ch.add(tt(p(12), p(3), p(9), ALU.mult))
                ch.add(tt(p(15), prm("a_re"), prm("a_re"), ALU.mult))
                ch.link(tt(p(16), prm("a_im"), prm("a_im"), ALU.mult))
                ch.link(tt(p(15), p(15), p(16), ALU.add))
                ch.link(ve.reciprocal(p(15), p(15)))
                ch.link(ve.tensor_scalar(p(17), p(11), -1.0, None, ALU.add))
                ch.add(tt(p(13), p(17), prm("a_re"), ALU.mult))
                ch.add(tt(p(16), p(12), prm("a_im"), ALU.mult))
                ch.add(tt(p(14), p(12), prm("a_re"), ALU.mult))
                ch.link(tt(p(18), p(17), prm("a_im"), ALU.mult))
                ch.add(tt(p(13), p(13), p(16), ALU.add))
                ch.link(tt(p(14), p(14), p(18), ALU.subtract))
                ch.add(tt(p(13), p(13), p(15), ALU.mult))
                ch.link(tt(p(14), p(14), p(15), ALU.mult))
                wr, wi = (bc(p(n), 2, [P, SG, 32]) for n in (13, 14))
                cr, ci = e_C[:, 0], e_C[:, 1]
                ch.add(tt(e_CW[:, 0], cr, wr, ALU.mult))
                ch.link(tt(e_ctmp, ci, wi, ALU.mult))
                ch.link(tt(e_CW[:, 0], e_CW[:, 0], e_ctmp, ALU.subtract))
                ch.add(tt(e_CW[:, 1], cr, wi, ALU.mult))
                ch.link(tt(e_ctmp, ci, wr, ALU.mult))
                ve.scalar_tensor_tensor(out=e_CW[:, 1], in0=e_CW[:, 1], scalar=-1.0, in1=e_ctmp,
                                        op0=ALU.mult, op1=ALU.subtract).then_inc(cw_ready, 1)
                ch.add(ve.memset(e_cos[:, :, 0:1], 1.0))
                ch.add(ve.memset(e_sin[:, :, 0:1], 0.0))
                ch.add(ve.tensor_copy(p(19), p(10)))
                ch.link(ve.tensor_copy(p(20), p(9)))
                n = 1
                while n < T:
                    if n == P:
                        ve.wait_ge(evac, 9)
                        tt(e_sq, e_qk, e_qk, ALU.mult).then_inc(sq_ready, 1)
                    bcos, bsin = bc(p(19), 2, [P, SG, n]), bc(p(20), 2, [P, SG, n])
                    t0 = e_tmp[:, 0, 0:SG * n].rearrange("p (a b) -> p a b", a=SG)
                    t1 = e_tmp[:, 1, 0:SG * n].rearrange("p (a b) -> p a b", a=SG)
                    old_c, old_s = e_cos[:, :, 0:n], e_sin[:, :, 0:n]
                    new_c, new_s = e_cos[:, :, n:2 * n], e_sin[:, :, n:2 * n]
                    if n == P:
                        ch.add(tt(t0, old_s, bsin, ALU.mult))
                        ch.link(tt(new_c, old_c, bcos, ALU.mult))
                        ch.add(tt(new_c, new_c, t0, ALU.subtract))
                        invert(1, e_rt[0:16, 0, :])
                        ve.wait_ge(sine_parts, 2)
                        ch.link(tt(new_s, new_s, t1, ALU.add))
                        break
                    ch.add(tt(t0, old_s, bsin, ALU.mult))
                    ch.add(tt(t1, old_s, bcos, ALU.mult))
                    ch.add(tt(new_c, old_c, bcos, ALU.mult))
                    ch.add(tt(new_s, old_c, bsin, ALU.mult))
                    ch.add(tt(p(21), p(19), p(19), ALU.mult))
                    ch.add(tt(p(22), p(20), p(20), ALU.mult))
                    ch.link(tt(p(23), p(19), p(20), ALU.mult))
                    ch.add(tt(new_c, new_c, t0, ALU.subtract))
                    ch.add(tt(new_s, new_s, t1, ALU.add))
                    ch.add(tt(p(19), p(21), p(22), ALU.subtract))
                    n *= 2
                    ins = ve.tensor_scalar(p(20), p(23), 2.0, None, ALU.mult)
                    if n < P:
                        ch.link(ins)
                    else:
                        ins.then_inc(half_table, 1)
                        ve.wait_ge(half_table, 1)
                head_norm(1, e_qk, [(c, prm("q_norm")) for c in range(4)] + [(4, prm("k_norm"))], 1)

                def ssm(c):
                    ve.wait_ge(bu_done, c + 1)
                    if c >= 4:
                        ve.wait_ge(back, c - 3)
                    src = ps[:, 6 + c % 2, :].rearrange("p (a b) -> p a b", a=2)
                    zt0 = e_zt[:, 0, :].rearrange("p (a b) -> p a b", a=2)
                    zt1 = e_zt[:, 1, :].rearrange("p (a b) -> p a b", a=2)
                    ch.add(tt(zt0, src, bc(e_cos[:, c, :], 1, [P, 2, T]), ALU.mult))
                    tt(zt1, src, bc(e_sin[:, c, :], 1, [P, 2, T]), ALU.mult).then_inc(bu_used, 1)
                    ve.wait_ge(bu_used, c + 1)
                    z = e_z[:, c % 4]
                    ch.add(tt(z[:, 0, :], zt0[:, 0, :], zt1[:, 1, :], ALU.add))
                    ch.link(tt(z[:, 1, :], zt0[:, 1, :], zt1[:, 0, :], ALU.subtract))
                    m = e_p[:, 3, c:c + 1].broadcast_to([P, T])
                    ch.add(ve.tensor_tensor_scan(z[:, 0, :], m, z[:, 0, :], 0.0, ALU.mult, ALU.add))
                    ve.tensor_tensor_scan(z[:, 1, :], m, z[:, 1, :], 0.0, ALU.mult, ALU.add).then_inc(scanned, 1)

                def y(j):
                    ve.wait_ge(y_done, 4 * j + 4)
                    ve.scalar_tensor_tensor(out=e_y[:, j, :], in0=e_uT[:, j, :], scalar=prm("ssm_d", j, j + 1),
                                            in1=ps[:, 4 + j % 2, 0:T], op0=ALU.mult,
                                            op1=ALU.add).then_inc(y_sum, 1)

                ssm(0)
                ssm(1)
                mask = k("window_mask")
                softmax_in(0, e_S, e_sm, lambda n: (mask[:, 0:P], mask[:, P:3 * P]), prm("sinks"))
                for c in range(2, 6):
                    ssm(c)
                softmax_out(0, e_S, e_sm, None, True)
                for c in range(6, SG):
                    ssm(c)
                    if c % 4 == 0 and c >= 8:
                        y(c // 4 - 2)
                    if c == 9:
                        mix_split(0, e_mixT, range(4), slots=EVEN_SLOTS)
                        ve.wait_ge(low_ready, AT[("even", "out", 0)])
                    if 9 <= c < 15:
                        low(AT[("even", "out", 0)] + c - 9)
                y(2)
                y(3)
                for j in range(4):
                    ve.wait_ge(y_high, j + 1)
                    tt(hT_lo[:, j, :], e_y[:, j, :], hT_hi[:, j, :].bitcast(F32),
                       ALU.subtract).then_inc(y_low, 1)
                for s in range(2):
                    ve.wait_ge(glu_sig, 2 * s + 2)
                    tt(e_mixT[:, 4 + 2 * s:6 + 2 * s, :], e_y[:, 2 * s:2 * s + 2, :],
                       e_sq[:, 2 * s:2 * s + 2, :], ALU.mult).then_inc(glu_out, 1)
                    mix_split(0, e_mixT, range(4 + 2 * s, 6 + 2 * s), slots=EVEN_SLOTS)

            def mlp(n, name):
                base = AT[(name, "gate", 0)]

                def combine(strip, c, i=None):
                    at = lambda v: v if i is None else 2 * i + v
                    ve.wait_ge(strip_done, strip + 1 if i is None else UNROLL * i + (strip + 1))
                    ve.wait_ge(silu_ready, at(FC * n + c + 1))
                    tt(f_act[:, c % 2, :], f_silu[:, c % 2, :], ps[:, 6 + c % 2, 0:T],
                       ALU.mult).then_inc(a_ready, 1)
                    ve.wait_ge(a_ready, at(FC * n + c + 1))
                    ve.tensor_copy(a_hi[:, c % 2, :], f_act[:, c % 2, :]).then_inc(a_high, 1)
                    ve.wait_ge(a_high, at(FC * n + c + 1))
                    tt(a_lo[:, c % 2, :], f_act[:, c % 2, :], a_hi[:, c % 2, :].bitcast(F32),
                       ALU.subtract).then_inc(ff_ready, 1)

                ve.wait_ge(low_ready, base + 2)
                low(base + 2)
                combine(base + 1, 0)
                low(base + 3)
                with ve.Fori(0, (FC - 2) // 2) as i:
                    for u in range(2):
                        at = base + 2 + 3 * u
                        low(at + 2, i)
                        low(at + 3, i)
                        combine(at + 1, 1 + u, i)
                        low(at + 4, i)
                at = base + 2 + 3 * (FC - 2)
                low(at + 2)
                low(at + 3)
                combine(at + 1, FC - 1)

            def odd():
                def bank_pair(j):
                    return ps[:, 2 * (j % 2):2 * (j % 2) + 2, 0:3 * P]

                def softplus(j):
                    ve.wait_ge(z_log, j + 1)
                    at = 2 * (j % 2)
                    ve.scalar_tensor_tensor(out=o_sp[:, at:at + 2, :], in0=bank_pair(j), scalar=0.0,
                                            in1=o_t, op0=ALU.max, op1=ALU.add).then_inc(sp_ready, 1)

                def weights(j):
                    ve.wait_ge(cum_done, j + 1)
                    if j >= 2:
                        ve.wait_ge(w_ready, j - 1)
                    at = 2 * (j % 2)
                    tt(o_w0[:, at:at + 2, :], bank_pair(j), bc(k("strict_mask"), 1, [P, 2, 3 * P]),
                       ALU.add).then_inc(w_masked, 1)

                for j in range(8):
                    if j:
                        weights(j - 1)
                    softplus(j)
                weights(7)
                mix_split(1, o_mixT)

            def mix():
                r = m_row[0:MH]
                ch.add(ve.memset(r[:, 9, :], 1.0))
                ch.link(ve.memset(m_up[:, :, 0:3], 0.0))
                ve.wait_ge(gate_act, 1)
                ch.link(ve.scalar_tensor_tensor(out=r[:, 1, :], in0=r[:, 1, :], scalar=0.0, in1=r[:, 2, :],
                                                op0=ALU.min, op1=ALU.subtract))
                for a in range(NT):
                    ch.add(ve.tensor_tensor_scan(r[:, 6, a * P:(a + 1) * P], r[:, 9, a * P:(a + 1) * P],
                                                 r[:, 1, a * P:(a + 1) * P], 0.0, ALU.mult, ALU.add))
                ch.wait()
                ch.link(tt(r[:, 3, :], r[:, 0, :], r[:, 6, :], ALU.subtract))
                ch.link(ve.tensor_tensor_scan(r[:, 8, 0:P], r[:, 3, 0:P], r[:, 3, 0:P], 0.0, ALU.max, ALU.max))
                ch.link(tt(r[:, 2, 0:1], r[:, 6, P - 1:P], r[:, 8, P - 1:P], ALU.add))
                ch.link(ve.tensor_tensor_scan(r[:, 8, P:T], r[:, 3, P:T], r[:, 3, P:T], r[:, 2, 0:1],
                                              ALU.max, ALU.max))
                ch.add(ve.tensor_scalar(r[:, 4, :], r[:, 8, :], -1.0, None, ALU.mult))
                ch.add(tt(r[:, 5, :], r[:, 6, :], r[:, 8, :], ALU.add))
                ve.tensor_scalar(r[:, 7, 0:P], r[:, 3, 0:P], r[:, 6, P - 1:P], None,
                                 ALU.add).then_inc(rows_ready, 1)
                for j in range(4):
                    ve.wait_ge(evac, GATE_EVAC + 1 + j + 1)
                    cw = lambda i: prm("conv_w", 4 * j + i, 4 * j + i + 1)
                    o = m_cv[:, j, :]
                    ch.link(ve.tensor_scalar(o, m_up[:, j, 0:T], cw(0), prm("conv_b", j, j + 1),
                                             ALU.mult, ALU.add))
                    for i in range(1, 4):
                        ins = ve.scalar_tensor_tensor(out=o, in0=m_up[:, j, i:T + i], scalar=cw(i), in1=o,
                                                      op0=ALU.mult, op1=ALU.add)
                        if i < 3:
                            ch.link(ins)
                    ins.then_inc(conv_done, 1)
                small_wait(ve, "mix")
                ch.add(tt(m_bias, m_bias, bc(k("dilated_mask", P, 3 * P), 1, [P, NH, T]), ALU.add))
                ve.wait_ge(evac, GATE_EVAC + 15)
                tt(m_sq, m_qk, m_qk, ALU.mult).then_inc(sq_ready, 1)
                invert(2, m_rt[0:16, 0, :])
                for n, name in enumerate(("qn", "kn")):
                    head_norm(2 + n, m_qk, [(4 * n + j, prm(name, j, j + 1)) for j in range(4)], 6)
                ch.wait()
                softmax_in(1, m_S, m_sm, lambda n: (m_bias[:, n, P:T], m_bias[:, n, :]), None)
                for h in range(MH):
                    ve.wait_ge(bcast_done, h + 1)
                    x = m_x[:, h, :]
                    ch.add(tt(x[:, 0:T], ps[:, h, 0:T], k("causal_mask", 0, T), ALU.add))
                    tt(x[:, T:3 * P], ps[:, h, P:T], k("causal_mask", T, 3 * P), ALU.add).then_inc(expo_in, 1)
                softmax_out(1, m_S, m_sm, k("dilated_count"), False)
                for h in range(MH):
                    decay(h)
                f = lambda a: a.rearrange("p a b -> p (a b)")
                ve.wait_ge(den_abs, MH)
                ve.wait_ge(em_out, MH)
                ch.link(tt(f(m_dn), f(m_dn), f(m_em), ALU.max))
                ch.link(ve.reciprocal(f(m_dn), f(m_dn)))
                mix_split(2, m_mixT, range(4), MIX_ORDER)
                ch.link(tt(m_hm, ps[:, 4:4 + MH, 0:T], m_dn, ALU.mult))
                tt(f(m_dn), f(m_hm), f(m_hm), ALU.mult).then_inc(hm_sq, 1)
                for h in range(MH):
                    ch.add(ve.tensor_scalar(m_cs[:, h, :], m_cT[:, h, :], prm("skip", h, h + 1), None, ALU.mult))
                invert(3, r[:, 9, :])
                ve.wait_ge(hm_wide, 1)
                tt(f(m_hm), f(m_hm), f(ps[:, 4:6, :]), ALU.mult).then_inc(hm_used, 1)
                ve.wait_ge(hm_used, 1)
                for h in range(MH):
                    ch.add(ve.scalar_tensor_tensor(out=m_hm[:, h, :], in0=m_hm[:, h, :],
                                                   scalar=prm("mh_norm", h, h + 1), in1=m_cs[:, h, :],
                                                   op0=ALU.mult, op1=ALU.add))
                ch.wait()
                tt(m_mixT[:, 0:4, :], m_hm, m_sz, ALU.mult).then_inc(ym_ready, 1)
                mix_split(2, m_mixT, range(4, KC), MIX_ORDER)

            def decay(h):
                ve.wait_ge(st_done, h + 1)
                ve.wait_ge(expo_out, h + 1)
                tt(m_s[:, h, :], ps[:, 6 + h % 2, 0:3 * P], m_d[:, h, :], ALU.mult).then_inc(s_ready, 1)

            def peer():
                def top16(v, i, row):
                    ch.link(ve.max(v[:, 0:8], row))
                    ch.link(ve.max_index(i[:, 0:8], v[:, 0:8], row))
                    ch.link(ve.match_replace(out=row, in_to_replace=v[:, 0:8], in_values=row, imm_value=-3e38))
                    ch.link(ve.max(v[:, 8:16], row))
                    ch.link(ve.max_index(i[:, 8:16], v[:, 8:16], row))

                iu, icu = r_i.bitcast(U32), r_ic.bitcast(U32)
                for s in range(2 * PH):
                    ve.wait_ge(key_out, s + 1)
                    for a in range(NT):
                        top16(r_v[:, a, s, :], iu[:, a, s, :], r_sc[:, s, a, :])
                    if s % 2:
                        h = s // 2
                        for a in range(NT):
                            ch.link(tt(r_c[:, a, :].rearrange("p (a b) -> p a b", a=TOPK),
                                       bc(r_v[:, a, s - 1, :], 2, [P, TOPK, TOPK]),
                                       bc(r_v[:, a, s, :], 1, [P, TOPK, TOPK]), ALU.add))
                            top16(r_vc[:, a, h, :], icu[:, a, h, :], r_c[:, a, :])
                n = NT * PH
                g = r_e[:, 2, :].rearrange("p (a b) -> p a b", b=TOPK)
                vc = r_vc.rearrange("p a h b -> p (a h) b")
                tt(g, vc, vc[:, :, 0:1].broadcast_to([P, n, TOPK]), ALU.subtract).then_inc(route_dve, 1)
                ic = icu.rearrange("p a h b -> p (a h b)")
                hl = r_hl.bitcast(U32)
                ch.add(ve.tensor_scalar(hl[:, 0, :], ic, 4, None, ALU.logical_shift_right))
                ch.add(ve.tensor_scalar(hl[:, 1, :], ic, 15, None, ALU.bitwise_and))
                ch.link(ve.tensor_copy(r_if.rearrange("p a s b -> p (a s b)"),
                                       iu.rearrange("p a s b -> p (a s b)")))
                ch.link(ve.tensor_copy(r_hlf.rearrange("p a b -> p (a b)"), hl.rearrange("p a b -> p (a b)")))
                big = [P, PH, TOPK, TOPK]
                tmp = keys_s.rearrange("p a b -> p (a b)").rearrange(
                    "p (h k i) -> p h k i", h=PH, k=TOPK)
                iota16 = k("iota", 0, TOPK).unsqueeze(1).unsqueeze(1).broadcast_to(big)
                for a in range(NT):
                    for part in range(2):
                        at = r_hlf[:, part, a * P:(a + 1) * P].rearrange("p (h k) -> p h k", h=PH)
                        keys = r_if[:, a, part:2 * PH:2, :]
                        ch.link(tt(tmp, at.unsqueeze(3).broadcast_to(big), iota16, ALU.is_equal))
                        ch.link(tt(tmp, tmp, keys.unsqueeze(2).broadcast_to(big), ALU.mult))
                        ch.link(ve.tensor_reduce(
                            r_e[:, part, a * P:(a + 1) * P].rearrange("p (h k) -> p h k", h=PH), tmp, AX,
                            ALU.add))
                ve.wait_ge(route_act, 1)
                s = r_sum[:, 0, :]
                ch.link(ve.tensor_reduce(s, g, AX, ALU.add))
                ch.link(ve.reciprocal(s, s))
                ch.link(tt(g, g, bc(s, 2, [P, n, TOPK]), ALU.mult))
                ve.tensor_copy(xn[:, 0, 0:3 * T], r_e.rearrange("p a b -> p (a b)")).then_inc(route_ready, 1)
                ve.wait_ge(eT_done, 1)
                ch.add(ve.tensor_copy(iota_b[:, :], k("iota")))
                ve.tensor_copy(key_at[:, :, :], ps[:, 6, :].rearrange("p (a b) -> p a b", a=2)).then_inc(gate_free, 1)
                ch.link(ve.tensor_copy(gate3[:, :, 0], ps[:, 7, 0:T]))
                tt(gate_rest[:, 0, :], ps[:, 7, 0:T], gate3[:, :, 0], ALU.subtract).then_inc(gate_free, 1)
                ve.wait_ge(gate_free, 2)
                ch.link(ve.tensor_copy(gate3[:, :, 1], gate_rest[:, 0, :]))
                ch.link(tt(gate_rest[:, 1, :], gate_rest[:, 0, :], gate3[:, :, 1], ALU.subtract))
                ch.link(ve.tensor_copy(gate3[:, :, 2], gate_rest[:, 1, :]))

                def one_hot(half, g, i=None):
                    tok = slice(4 * g, 4 * g + 4) if i is None else bass.ds(4 * UNROLL * i + 4 * g, 4)
                    wide, narrow = [P, 4, P], [P, 4, HALF]
                    tt(oh_first[:, g % 2], bc(iota_b[:, HALF * half:HALF * (half + 1)], 1, narrow),
                       bc(key_at[:, 0, tok], 2, narrow), ALU.is_equal).then_inc(first_ready, 1)
                    tt(oh_second[:, g % 2], bc(iota_b[:, :], 1, wide), bc(key_at[:, 1, tok], 2, wide),
                       ALU.is_equal)
                    at = HALF * half + g + 1
                    ve.wait_ge(first_ready, at if i is None else UNROLL * i + at)
                    shape = [P, 4, 3, HALF]
                    tt(oh_gate[:, g % 2], bc(oh_first[:, g % 2], 2, shape), bc(gate3[:, tok, :], 3, shape),
                       ALU.mult).then_inc(onehot_ready, 1)

                def apply_gates(half, g, i=None):
                    at = HALF * half + g + 1
                    ve.wait_ge(spread, at if i is None else UNROLL * i + at)
                    tok = slice(4 * g, 4 * g + 4) if i is None else bass.ds(4 * UNROLL * i + 4 * g, 4)
                    part = act[:, HALF * half:HALF * (half + 1), tok]
                    tt(part, part, ps[:, 6 + g % 2, 0:4 * HALF].rearrange("p (q e) -> p e q", q=4),
                       ALU.mult).then_inc(gate_free, 1)

                def act_low(e, i=None):
                    ve.wait_ge(a_high, 2 * FC + e + 1 if i is None else UNROLL * i + (2 * FC + e + 1))
                    src = act[:, e, :] if i is None else act[:, bass.ds(UNROLL * i + e, 1), :].rearrange(
                        "p a t -> p (a t)")
                    tt(a_lo[:, e % 2, :], src, a_hi[:, e % 2, :].bitcast(F32),
                       ALU.subtract).then_inc(ff_ready, 1)

                def gate_first(g, i):
                    one_hot(0, g + 1, i)
                    apply_gates(0, g, i)

                def gate_second(e, i):
                    act_low(e + 1, i)
                    one_hot(1, e + 1, i)
                    apply_gates(1, e, i)

                one_hot(0, 0)
                ve.wait_ge(gelu_done, HALF)
                half_tiles(ve, 0, gate_first, 1)
                apply_gates(0, HALF - 1)
                one_hot(1, 0)
                ve.wait_ge(gate_free, HALF + 2)
                act_low(0)
                ve.wait_ge(gelu_done, NE1)
                half_tiles(ve, 0, gate_second, 1)
                apply_gates(1, HALF - 1)
                ve.wait_ge(gate_free, NE1 + 2)
                act_low(HALF)
                half_tiles(ve, HALF, lambda e, i: act_low(e + 1, i), 1)
                ve.wait_ge(strip_done, AT[LASTS[5]] + 1)
                ve.tensor_copy(xn[:, 0, :], ps[:, 0:2, :].rearrange("p a b -> p (a b)")).then_inc(yT_out, 1)
                ve.wait_ge(out_turned, 1)
                for a in range(NT):
                    ve.tensor_copy(x_s[:, a, :], ps[:, 4 + 2 * a:6 + 2 * a, :].rearrange(
                        "p a b -> p (a b)")).then_inc(x_ready, 1)

            for n, body in enumerate([even, lambda: mlp(0, "mlp0"), odd, lambda: mlp(1, "mlp1"), mix,
                                      peer]):
                norm(n)
                body()

        @block.gpsimd
        def _(po):
            ch = Chain(po, pool_chain)

            def low(n, i=None):
                po.wait_ge(high_ready, n + 1 if i is None else UNROLL * i + (n + 1))
                po.tensor_tensor(w_lo[:, n % RING, :], ring[:, n % RING, :],
                                 w_hi[:, n % RING, :].bitcast(F32), ALU.subtract).then_inc(low_ready, 1)

            def lows(first, last):
                for n in range(AT[first], AT[last] + 1):
                    low(n)

            lows(STRIPS[0], ("even", "v", 0))
            po.wait_ge(half_table, 1)
            for n, (old, base, new) in enumerate((
                    (e_sin, 19, e_tmp[:, 1].rearrange("p (a b) -> p a b", a=SG)),
                    (e_cos, 20, e_sin[:, :, P:T]))):
                po.tensor_tensor(new, old[:, :, 0:P],
                                 e_p[:, base, :].unsqueeze(2).broadcast_to([P, SG, P]),
                                 ALU.mult).then_inc(sine_parts, 1)
            for c in range(SG):
                po.wait_ge(scanned, c + 1)
                z = e_z[:, c % 4]
                h0 = e_ht[:, 0, :].rearrange("p (a b) -> p a b", a=2)
                h1 = e_ht[:, 1, :].rearrange("p (a b) -> p a b", a=2)
                ch.add(po.tensor_tensor(h0, z, e_cos[:, c, :].unsqueeze(1).broadcast_to([P, 2, T]), ALU.mult))
                ch.link(po.tensor_tensor(h1, z, e_sin[:, c, :].unsqueeze(1).broadcast_to([P, 2, T]), ALU.mult))
                if c >= 4:
                    po.wait_ge(y_done, c - 3)
                h = e_h[:, c % 4]
                ch.add(po.tensor_tensor(h[:, 0, :], h0[:, 0, :], h1[:, 1, :], ALU.subtract))
                po.tensor_tensor(h[:, 1, :], h0[:, 1, :], h1[:, 0, :], ALU.add).then_inc(back, 1)
                po.wait_ge(back, c + 1)
            po.wait_ge(low_ready, AT[("even", "out", 4)])
            lows(("even", "out", 4), ("even", "out", 7))
            lows(("mlp0", "gate", 0), ("mlp0", "up", 0))
            po.wait_ge(low_ready, AT[("odd", "v", 0)])
            lows(("odd", "v", 0), ("odd", "v", 7))
            for j in range(9):
                if j < 8:
                    lows(("odd", "q", j), ("odd", "k", j))
                if j:
                    po.wait_ge(sp_ready, j)
                    for h in (2 * j - 2, 2 * j - 1):
                        v = o_sp[:, h % 4, :].rearrange("p (b c) -> p b c", c=P)[:, 0:3:2, :]
                        ins = po.affine_select(out=v, in_=v, compare_op=ALU.is_gt, fill=0.0, base=0,
                                               pattern=[[0, 2], [1, P]], channel_multiplier=-1)
                    ins.then_inc(sp_masked, 1)
            lows(("odd", "out", 0), ("odd", "out", 7))
            lows(("mlp1", "gate", 0), ("mlp1", "up", 0))
            po.wait_ge(low_ready, AT[("mix", "if", 0)])
            lows(("mix", "if", 0), LASTS[4])
            base = AT[("peer", "q", 0)]
            for n in range(2 * PH):
                low(base + n)
            base = AT[("peer", "u", 0)]
            with po.Fori(0, 2 * NE1 // UNROLL) as i:
                for e in range(UNROLL):
                    low(base + e, i)
            for e in range(2 * NE1 // UNROLL * UNROLL, 2 * NE1):
                low(base + e)


def _constants():
    c = np.zeros((P, N_CONST), np.float32)

    def put(name, v):
        c[:v.shape[0], CONST[name][0]:CONST[name][1]] = v

    i, j = np.arange(P)[:, None], np.arange(P)[None, :]
    put("ident", np.eye(P))
    put("ones", np.ones((P, P)))
    put("head_sel", (j % 16 == 2 * (j // 16) + i // HD) * 1.0)
    put("all_sel", np.tile(np.eye(MH).reshape(1, -1), (P, 1)))
    put("neg_tri", (i >= j) * -1.0)
    put("neg_ones", -np.ones((P, P)))
    put("iota", np.broadcast_to(j, (P, P)))
    free = np.zeros((P, P))
    strict, causal = np.where(i < j, 0.0, -BIG), np.where(i <= j, 0.0, -BIG)
    put("strict_mask", np.concatenate([strict, free, strict], 1))
    put("causal_mask", np.concatenate([causal, free, causal], 1))
    dist = np.concatenate([i - j, i - j + P, i - j], 1)
    put("window_mask", np.where((dist >= 0) & (dist < 128), 0.0, -BIG))
    count = sum(((dist >= 0) & (dist % dil == 0) & (dist // dil <= win // dil)).astype(np.float32)
                for win, dil in ((128, 1), (512, 4), (2048, 16)))
    put("dilated_count", count)
    put("dilated_mask", np.where(count > 0, 0.0, -BIG))
    put("head_row", np.repeat(np.eye(MH), P, axis=1))
    put("eps", np.full((P, 1), EPS))
    return c


def _buckets():
    d = np.arange(T)
    large = 16 + (np.log(np.maximum(d, 1).astype(np.float32) / np.float32(16))
                  / np.float32(np.log(2048 / 16)) * 16).astype(np.int32)
    return np.where(d < 16, d, np.minimum(large, 31))


def _layout(v):
    f = {n: np.asarray(a) for n, a in v.items()}
    strips = np.empty((NS, P, D), np.float32)

    def cols(w, at, rows=D):
        w = w[:, at]
        return w.reshape(rows // P, P, w.shape[1]).transpose(1, 0, 2).reshape(P, -1)

    def put(name, w):
        strips[AT[name]] = w

    ar = np.arange
    w = f["even_w_in"][0]
    for j in range(4):
        put(("even", "u", j), cols(w, 768 + P * j + ar(P)))
        put(("even", "q", j), cols(w, np.concatenate([HD * j + ar(HD), HD * (j + 4) + ar(HD)])))
    put(("even", "k", 0), cols(w, 512 + ar(P)))
    put(("even", "v", 0), cols(w, 640 + ar(P)))
    for j in range(2):
        put(("even", "glu", j), cols(f["ssm_w_glu"][0], 256 * j + ar(256), 512))
    w = f["even_w_out"][0]
    for j in range(8):
        rows = np.concatenate([HD * j + ar(HD), HD * (j + 4) + ar(HD)]) if j < 4 else P * j + ar(P)
        put(("even", "out", j), w[rows])
        put(("odd", "out", j), f["odd_w_out"][0][P * j:P * j + P])
        put(("mix", "out", j), f["w_out_2"][0][P * j:P * j + P])
    for n in range(2):
        for c in range(FC):
            put((f"mlp{n}", "gate", c), cols(f["ffn_w_gate"][n], P * c + ar(P)))
            put((f"mlp{n}", "up", c), cols(f["ffn_w_up"][n], P * c + ar(P)))
            put((f"mlp{n}", "down", c), f["ffn_w_down"][n][P * c:P * c + P])
    for j in range(8):
        for n, part in enumerate("qk"):
            put(("odd", part, j), cols(f["odd_w_in"][0], D * n + P * j + ar(P)))

    def put_pairs(name, w, first, n):
        for j in range(n):
            rows = D // 2 * (j % 2)
            put(name + (j,), cols(w[rows:rows + D // 2], first + T * (j // 2) + ar(T), D // 2))

    put_pairs(("odd", "v"), f["odd_w_in"][0], 2 * D, 8)
    w = f["w_in_2"][0]
    put_pairs(("mix", "vm"), w, 512, 4)
    put_pairs(("mix", "va"), w, 2568, 4)
    at = {"u": 0, "z": 1024, "qa": 1544, "ka": 2056}
    for part, first in at.items():
        for j in range(4):
            put(("mix", part, j), cols(w, first + P * j + ar(P)))
    gates = np.zeros((P, KC, P), np.float32)
    gates[:, :, 0:MH] = cols(w, 1536 + ar(MH)).reshape(P, KC, MH)
    gates[:, :, FG_AT:FG_AT + MH] = cols(w, 1536 + MH + ar(MH)).reshape(P, KC, MH)
    put(("mix", "if", 0), gates.reshape(P, D))
    for s in range(2 * PH):
        put(("peer", "q", s), cols(f["w_query_2"][0], P * s + ar(P)))
    u = f["expert_u_2"][0].reshape(NE1, P, KC, P)
    first = AT[("peer", "u", 0)]
    strips[first:first + NE1] = u.transpose(0, 3, 2, 1).reshape(NE1, P, D)
    first = AT[("peer", "v", 0)]
    strips[first:first + NE1] = f["expert_v_2"][0].reshape(NE1, P, D)

    param = np.zeros((P, N_PARAM), np.float32)

    def prm(name, w):
        param[:w.shape[0], PARAM[name][0]:PARAM[name][1]] = w

    chunks = lambda a: a.reshape(-1, P).T
    for name, a in (("even_norm", f["even_norm"][0]), ("mlp0_norm", f["ffn_norm"][0]),
                    ("odd_norm", f["odd_norm"][0]), ("mlp1_norm", f["ffn_norm"][1]),
                    ("mix_norm", f["norm1_g_2"][0]), ("peer_norm", f["norm2_g_2"][0]),
                    ("ssm_d", f["ssm_d"][0]), ("b_glu", f["ssm_b_glu"][0]),
                    ("conv_b", f["conv_b_2"][0]), ("mh_norm", f["mh_norm_g_2"][0].reshape(-1)),
                    ("skip", f["skip_m_2"][0].reshape(-1)), ("qn", f["qn_g_2"][0].reshape(-1)),
                    ("kn", f["kn_g_2"][0].reshape(-1)), ("a_re", f["ssm_a_re"][0].reshape(-1)),
                    ("a_im", f["ssm_a_im"][0].reshape(-1)),
                    ("log_dt", np.repeat(f["ssm_log_dt"][0], HD))):
        prm(name, chunks(a))
    prm("q_norm", np.tile(f["q_norm"][0], 2)[:, None])
    prm("k_norm", np.tile(f["k_norm"][0], 2)[:, None])
    order = [n // 2 + 4 * (n % 2) for n in range(NH)]
    prm("sinks", np.broadcast_to(f["sinks"][0][order], (P, NH)))
    prm("conv_w", f["conv_w_2"][0].reshape(4, 4, P).transpose(2, 1, 0).reshape(P, 16))
    prm("ig_b", f["ig_b_2"][0][:, None])
    param[FG_AT:FG_AT + MH, PARAM["fg_b"][0]] = f["fg_b_2"][0]

    ssm_b = np.zeros((4, 2, 16, 2, 4, 2, HD), np.float32)
    ssm_c = np.zeros((2, HD, 2, SG, 2, 16), np.float32)
    for part, (b, c) in enumerate((("ssm_b_re", "ssm_c_re"), ("ssm_b_im", "ssm_c_im"))):
        bb = f[b][0].reshape(4, 4, 2, HD, 16)
        cc = f[c][0].reshape(SG, 2, 16, HD)
        for g in range(2):
            ssm_b[:, g, :, part, :, g, :] = bb[:, :, g].transpose(1, 3, 0, 2)
            ssm_c[g, :, part, :, g, :] = cc[:, g].transpose(2, 0, 1)
    keys = np.stack([f[f"sub_keys{n}_2"][0].transpose(2, 0, 1).reshape(P, D) for n in (1, 2)], 1)
    wqk = np.stack([f[n][0].transpose(1, 0, 2) for n in ("wq_m_2", "wk_m_2")], 1)
    head_rows = (np.arange(16)[:, None] == np.arange(D)[None, :] // HD).astype(np.float32)
    dist = np.arange(P)[:, None] + P - np.arange(T)[None, :]
    rel = f["rel_bias_2"][_buckets()[np.abs(dist) % T]].transpose(0, 2, 1)
    return {"strips": strips, "const": _constants(), "param": param, "ssm_b": ssm_b.reshape(P, D),
            "ssm_c": ssm_c.reshape(P, D), "head_rows": head_rows, "keys": keys.reshape(P, 2 * D), "wqk": wqk.reshape(P, D),
            "rel": np.ascontiguousarray(rel).reshape(P, NH * T), "x": f["x"]}


def kernel(**inputs):
    import concourse.bacc as bacc
    from concourse.bass_utils import run_bass_kernel_spmd

    arrays = {f"in_{n}": np.ascontiguousarray(a) for n, a in _layout(inputs).items()}
    nc = bacc.Bacc("TRN2", target_bir_lowering=False, num_devices=1,
                   dynamic_dma_scratch_size=1024)
    A = {n[3:]: nc.dram_tensor(n, a.shape, F32, kind="ExternalInput").ap() for n, a in arrays.items()}
    out = nc.dram_tensor("out", (1, T, D), F32, kind="ExternalOutput").ap()
    build(nc, A, out)
    return run_bass_kernel_spmd(nc, [arrays], core_ids=[0]).results[0]["out"]
```
